# Optimizing a Trainium2 kernel written in Bass

```python
import math
import jax, jax.numpy as jnp
from jax import lax
import numpy as np

D_MODEL = 1024
BATCH = 1
SEQ = 512
DEPTH = 2

CHUNK = 64
Q_BLOCK = 128
PLE_DIM = 256
MIX_WIDTH = D_MODEL // 2
POOL_WINDOWS = (2, 4, 8, 16)
POOL_GROUPS = len(POOL_WINDOWS)
POOL_GROUP_DIM = MIX_WIDTH // POOL_GROUPS
CONV_WIDTH = 3
ATTN_HEADS = 4
ATTN_HEAD_DIM = MIX_WIDTH // (2 * ATTN_HEADS)
ATTN_V_DIM = 2 * ATTN_HEAD_DIM
ATTN_QK_WIDTH = ATTN_HEADS * 2 * ATTN_HEAD_DIM
ATTN_V_WIDTH = ATTN_HEADS * ATTN_V_DIM
N_BRANCHES = 3
D_IN = 4 * MIX_WIDTH + 2 * ATTN_QK_WIDTH + ATTN_V_WIDTH + N_BRANCHES * D_MODEL
D_FF = 4 * D_MODEL
EPS = 1e-6
NEG_INF = -1e30


def rms_norm(x, g):
    xf = x.astype(jnp.float32)
    y = xf * lax.rsqrt(jnp.mean(xf * xf, axis=-1, keepdims=True) + EPS)
    return (y * g.astype(jnp.float32)).astype(x.dtype)

def multiscale_pool(a, w, scale):
    b_, s_, _ = a.shape
    af = a.astype(jnp.float32).reshape(b_, s_, POOL_GROUPS, POOL_GROUP_DIM)
    cs = jnp.cumsum(af, axis=1)
    t = jnp.arange(s_)
    outs = []
    for g, win in enumerate(POOL_WINDOWS):
        csg = cs[:, :, g]
        prev = jnp.pad(csg, ((0, 0), (win, 0), (0, 0)))[:, :s_]
        cnt = jnp.minimum(t + 1, win).astype(jnp.float32)[None, :, None]
        outs.append((csg - prev) / cnt - af[:, :, g])
    pooled = jnp.stack(outs, axis=2)
    mixed = jnp.einsum('bsgc,gcd->bsgd', pooled, w.astype(jnp.float32))
    return (mixed.reshape(b_, s_, MIX_WIDTH) * scale.astype(jnp.float32)).astype(a.dtype)

def causal_depthwise_conv(z, w):
    c = z.shape[-1]
    return lax.conv_general_dilated(
        z, w[:, None, :].astype(z.dtype), window_strides=(1,),
        padding=[(CONV_WIDTH - 1, 0)], dimension_numbers=('NWC', 'WIO', 'NWC'),
        feature_group_count=c)

def diff_attention(q1, q2, k1, k2, v, lam):
    b_, s_, h_, d_ = q1.shape
    dv = v.shape[-1]
    nb = s_ // Q_BLOCK
    scale = d_ ** -0.5
    k1, k2, v = (t.transpose(0, 2, 1, 3) for t in (k1, k2, v))

    def to_blocks(q):
        return q.reshape(b_, nb, Q_BLOCK, h_, d_).transpose(1, 0, 3, 2, 4)

    key_chunk = jnp.arange(s_) // CHUNK

    def one_block(args):
        qb1, qb2, bi = args
        q_chunk = (bi * Q_BLOCK + jnp.arange(Q_BLOCK)) // CHUNK
        mask = key_chunk[None, :] <= q_chunk[:, None]

        def probs(q, k):
            s = jnp.einsum('bhqd,bhkd->bhqk', q, k).astype(jnp.float32) * scale
            return jax.nn.softmax(jnp.where(mask, s, NEG_INF), axis=-1)

        att = probs(qb1, k1) - lam * probs(qb2, k2)
        return jnp.einsum('bhqk,bhkd->bhqd', att.astype(v.dtype), v)

    out = lax.map(one_block, (to_blocks(q1), to_blocks(q2), jnp.arange(nb)))
    return out.transpose(1, 0, 3, 2, 4).reshape(b_, s_, h_, dv)

def first_inputs(seed: int = 0) -> dict:
    key = jax.random.key(seed)
    ks = jax.random.split(key, 24)
    nrm = lambda k, shape, s: jax.random.normal(k, shape, jnp.float32) * s
    gain = lambda k, shape: 1.0 + 0.1 * jax.random.normal(k, shape, jnp.float32)
    L = DEPTH
    return {
        'x': nrm(ks[0], (BATCH, SEQ, D_MODEL), 1.0),
        'p': nrm(ks[1], (DEPTH, BATCH, SEQ, PLE_DIM), 1.0),
        'norm_mix_g': gain(ks[2], (L, D_MODEL)),
        'w_in': nrm(ks[3], (L, D_MODEL, D_IN), D_MODEL ** -0.5),
        'pool_w': nrm(ks[4], (L, POOL_GROUPS, POOL_GROUP_DIM, POOL_GROUP_DIM), POOL_GROUP_DIM ** -0.5),
        'pool_scale': gain(ks[5], (L, MIX_WIDTH)),
        'conv_w': nrm(ks[6], (L, CONV_WIDTH, MIX_WIDTH), CONV_WIDTH ** -0.5),
        'q_norm_g': gain(ks[7], (L, ATTN_HEAD_DIM)),
        'k_norm_g': gain(ks[8], (L, ATTN_HEAD_DIM)),
        'lam_q1': nrm(ks[9], (L, ATTN_HEAD_DIM), 0.1),
        'lam_k1': nrm(ks[10], (L, ATTN_HEAD_DIM), 0.1),
        'lam_q2': nrm(ks[11], (L, ATTN_HEAD_DIM), 0.1),
        'lam_k2': nrm(ks[12], (L, ATTN_HEAD_DIM), 0.1),
        'sub_norm_g': gain(ks[13], (L, ATTN_V_DIM)),
        'w_pool_out': nrm(ks[14], (L, MIX_WIDTH, D_MODEL), MIX_WIDTH ** -0.5),
        'w_conv_out': nrm(ks[15], (L, MIX_WIDTH, D_MODEL), MIX_WIDTH ** -0.5),
        'w_attn_out': nrm(ks[16], (L, ATTN_V_WIDTH, D_MODEL), ATTN_V_WIDTH ** -0.5),
        'w_o': nrm(ks[17], (L, D_MODEL, D_MODEL), D_MODEL ** -0.5),
        'norm_mlp_g': gain(ks[18], (L, D_MODEL)),
        'w_up': nrm(ks[19], (L, D_MODEL, D_FF), D_MODEL ** -0.5),
        'w_down': nrm(ks[20], (L, D_FF, D_MODEL), D_FF ** -0.5),
        'norm_ple_g': gain(ks[21], (L, D_MODEL)),
        'w_ple_gate': nrm(ks[22], (L, D_MODEL, D_MODEL), D_MODEL ** -0.5),
        'w_ple_proj': nrm(ks[23], (L, PLE_DIM, D_MODEL), PLE_DIM ** -0.5),
    }

def first_block(x, p, norm_mix_g, w_in, pool_w, pool_scale, conv_w, q_norm_g, k_norm_g,
              lam_q1, lam_k1, lam_q2, lam_k2, sub_norm_g, w_pool_out, w_conv_out,
              w_attn_out, w_o, norm_mlp_g, w_up, w_down, norm_ple_g, w_ple_gate, w_ple_proj):
    b_, s_, _ = x.shape
    sizes = [MIX_WIDTH, MIX_WIDTH, MIX_WIDTH, MIX_WIDTH,
             ATTN_QK_WIDTH, ATTN_QK_WIDTH, ATTN_V_WIDTH]
    split_at = [int(c) for c in np.cumsum(sizes)]
    h = x
    for i in range(DEPTH):
        u = rms_norm(h, norm_mix_g[i])
        proj = u @ w_in[i]
        a_in, c_x, c_b, c_c, q, k, v, gates = jnp.split(proj, split_at, axis=-1)

        y_a = multiscale_pool(a_in, pool_w[i], pool_scale[i])

        y_b = c_b * causal_depthwise_conv(c_c * c_x, conv_w[i])

        q = q.reshape(b_, s_, ATTN_HEADS, 2, ATTN_HEAD_DIM)
        k = k.reshape(b_, s_, ATTN_HEADS, 2, ATTN_HEAD_DIM)
        v = v.reshape(b_, s_, ATTN_HEADS, ATTN_V_DIM)
        q1 = rms_norm(q[..., 0, :], q_norm_g[i])
        q2 = rms_norm(q[..., 1, :], q_norm_g[i])
        k1 = rms_norm(k[..., 0, :], k_norm_g[i])
        k2 = rms_norm(k[..., 1, :], k_norm_g[i])
        lam_init = 0.8 - 0.6 * math.exp(-0.3 * i)
        lam = (jnp.exp(jnp.sum(lam_q1[i].astype(jnp.float32) * lam_k1[i].astype(jnp.float32)))
               - jnp.exp(jnp.sum(lam_q2[i].astype(jnp.float32) * lam_k2[i].astype(jnp.float32)))
               + lam_init)
        o = diff_attention(q1, q2, k1, k2, v, lam)
        o = rms_norm(o, sub_norm_g[i]) * (1.0 - lam_init)
        y_c = o.reshape(b_, s_, ATTN_V_WIDTH)

        g_a, g_b, g_c = jnp.split(jax.nn.sigmoid(gates), N_BRANCHES, axis=-1)
        merged = (g_a * (y_a @ w_pool_out[i])
                  + g_b * (y_b @ w_conv_out[i])
                  + g_c * (y_c @ w_attn_out[i]))
        h = h + merged @ w_o[i]

        m = rms_norm(h, norm_mlp_g[i])
        h = h + jnp.square(jax.nn.relu(m @ w_up[i])) @ w_down[i]

        e = rms_norm(h, norm_ple_g[i])
        h = h + jax.nn.sigmoid(e @ w_ple_gate[i]) * (p[i] @ w_ple_proj[i])
    return h


DEPTH_2 = 1

ROPE_THETA = 500000.0
NEG = -1e30

MLA_HEADS = 8
MLA_NOPE = 64
MLA_ROPE = 32
MLA_QK = MLA_NOPE + MLA_ROPE
MLA_V = 64
MLA_Q_LORA = 768
MLA_KV_LORA = 256

NSA_HEADS = 8
NSA_KV_GROUPS = 2
NSA_REP = NSA_HEADS // NSA_KV_GROUPS
NSA_HEAD = 64
NSA_ROT = NSA_HEAD // 4
CMP_LEN = 32
CMP_STRIDE = 16
CMP_HIDDEN = 256
SEL_LEN = 64
SEL_TOP = 8
SEL_Q_BLOCK = 64
WINDOW = 256
N_NSA_BRANCH = 3
FORCE_BONUS = 1e4
KV_W = NSA_KV_GROUPS * NSA_HEAD

N_BRANCH = 2
D_FF_2 = -(-8 * D_MODEL // (3 * 256)) * 256
N_MOD = 6

IN_SIZES = (MLA_Q_LORA, MLA_KV_LORA, MLA_ROPE, NSA_HEADS * NSA_HEAD,
            KV_W, KV_W, KV_W, KV_W, KV_W, KV_W,
            NSA_HEADS * N_NSA_BRANCH, D_MODEL, D_MODEL)
D_IN_2 = sum(IN_SIZES)


def rms_norm_2(x, gain):
    xf = x.astype(jnp.float32)
    y = xf * lax.rsqrt(jnp.mean(xf * xf, axis=-1, keepdims=True) + EPS)
    return (y * gain.astype(jnp.float32)).astype(x.dtype)

def rope_angles(pos, dim):
    inv = ROPE_THETA ** (-jnp.arange(0, dim, 2, dtype=jnp.float32) / dim)
    ang = pos.astype(jnp.float32)[..., None] * inv
    return jnp.cos(ang), jnp.sin(ang)

def apply_rope(x, cos, sin):
    x1, x2 = jnp.split(x, 2, axis=-1)
    cos = cos.astype(x.dtype)
    sin = sin.astype(x.dtype)
    return jnp.concatenate([x1 * cos - x2 * sin, x2 * cos + x1 * sin], axis=-1)

def partial_rope(x, cos, sin):
    return jnp.concatenate([apply_rope(x[..., :NSA_ROT], cos, sin), x[..., NSA_ROT:]], axis=-1)

def causal_block_attention(q, k, v, scale):
    B, S, H, Dk = q.shape
    nb = S // Q_BLOCK
    qb = q.reshape(B, nb, Q_BLOCK, H, Dk).transpose(1, 0, 2, 3, 4)
    kpos = jnp.arange(S)

    def one(args):
        qi, i = args
        s = jnp.einsum('bqhd,bkhd->bhqk', qi, k).astype(jnp.float32) * scale
        qpos = i * Q_BLOCK + jnp.arange(Q_BLOCK)
        s = jnp.where(kpos[None, :] <= qpos[:, None], s, NEG)
        p = jax.nn.softmax(s, axis=-1).astype(v.dtype)
        return jnp.einsum('bhqk,bkhd->bqhd', p, v)

    o = lax.map(one, (qb, jnp.arange(nb)))
    return o.transpose(1, 0, 2, 3, 4).reshape(B, S, H, v.shape[-1])

def mla_attention(c_q, c_kv, k_pe, cos, sin, q_a_gain, w_q_b, kv_a_gain, w_kv_b, q_gain, k_gain):
    B, S, _ = c_q.shape
    q = (rms_norm_2(c_q, q_a_gain) @ w_q_b).reshape(B, S, MLA_HEADS, MLA_QK)
    kv = (rms_norm_2(c_kv, kv_a_gain) @ w_kv_b).reshape(B, S, MLA_HEADS, MLA_NOPE + MLA_V)
    k_nope, v = kv[..., :MLA_NOPE], kv[..., MLA_NOPE:]
    k = jnp.concatenate([k_nope, jnp.broadcast_to(k_pe[:, :, None, :], (B, S, MLA_HEADS, MLA_ROPE))], axis=-1)
    q = rms_norm_2(q, q_gain)
    k = rms_norm_2(k, k_gain)
    cos_h, sin_h = cos[:, :, None], sin[:, :, None]
    q = jnp.concatenate([q[..., :MLA_NOPE], apply_rope(q[..., MLA_NOPE:], cos_h, sin_h)], axis=-1)
    k = jnp.concatenate([k[..., :MLA_NOPE], apply_rope(k[..., MLA_NOPE:], cos_h, sin_h)], axis=-1)
    o = causal_block_attention(q, k, v, MLA_QK ** -0.5)
    return o.reshape(B, S, MLA_HEADS * MLA_V)

def nsa_attention(q, k_c, v_c, k_s, v_s, k_w, v_w, g_logit, cos, sin,
                  q_gain, kc_gain, ks_gain, kw_gain,
                  cmp_pos_k, cmp_w1_k, cmp_w2_k, cmp_pos_v, cmp_w1_v, cmp_w2_v):
    B, S, H, Dh = q.shape
    G, R = NSA_KV_GROUPS, NSA_REP
    f32 = jnp.float32
    scale = Dh ** -0.5
    cos_t, sin_t = cos[:, :, None], sin[:, :, None]
    q = partial_rope(rms_norm_2(q, q_gain), cos_t, sin_t)
    qg = q.reshape(B, S, G, R, Dh)
    t_idx = jnp.arange(S)

    n_cmp = (S - CMP_LEN) // CMP_STRIDE + 1
    starts = jnp.arange(n_cmp) * CMP_STRIDE
    blk_idx = starts[:, None] + jnp.arange(CMP_LEN)[None, :]

    def compress(t, pos_emb, w1, w2):
        blocks = t[:, blk_idx] + pos_emb[None, None, :, None, :]
        flat = blocks.transpose(0, 1, 3, 2, 4).reshape(B, n_cmp, G, CMP_LEN * Dh)
        return jax.nn.silu(flat @ w1) @ w2

    cmp_end = starts + CMP_LEN - 1
    kc = compress(k_c, cmp_pos_k, cmp_w1_k, cmp_w2_k)
    vc = compress(v_c, cmp_pos_v, cmp_w1_v, cmp_w2_v)
    kc = partial_rope(rms_norm_2(kc, kc_gain), cos[:, cmp_end][:, :, None], sin[:, cmp_end][:, :, None])
    s_c = jnp.einsum('bsgrd,bngd->bgrsn', qg, kc).astype(f32) * scale
    valid_c = cmp_end[None, :] <= t_idx[:, None]
    p_c = jax.nn.softmax(jnp.where(valid_c, s_c, NEG), axis=-1) * valid_c
    o_c = jnp.einsum('bgrsn,bngd->bsgrd', p_c.astype(vc.dtype), vc)

    n_sel = S // SEL_LEN
    sel_start = jnp.arange(n_sel) * SEL_LEN
    overlap = ((starts[:, None] < sel_start[None, :] + SEL_LEN) &
               (starts[:, None] + CMP_LEN > sel_start[None, :])).astype(f32)
    imp = jnp.einsum('bgrsn,nj->bgsj', p_c, overlap)
    cur = t_idx // SEL_LEN
    j = jnp.arange(n_sel)
    forced = (j[None, :] == 0) | (j[None, :] == cur[:, None]) | (j[None, :] == cur[:, None] - 1)
    imp = jnp.where(forced, imp + FORCE_BONUS, imp)
    imp = jnp.where(j[None, :] <= cur[:, None], imp, NEG)
    top = min(SEL_TOP, n_sel)
    _, sel_idx = lax.top_k(imp, top)

    ks = partial_rope(rms_norm_2(k_s, ks_gain), cos_t, sin_t)
    k_blocks = ks.reshape(B, n_sel, SEL_LEN, G, Dh).transpose(0, 3, 1, 2, 4)
    v_blocks = v_s.reshape(B, n_sel, SEL_LEN, G, Dh).transpose(0, 3, 1, 2, 4)
    nqb = S // SEL_Q_BLOCK
    q_chunks = qg.reshape(B, nqb, SEL_Q_BLOCK, G, R, Dh).transpose(1, 0, 2, 3, 4, 5)
    idx_chunks = sel_idx.reshape(B, G, nqb, SEL_Q_BLOCK, top).transpose(2, 0, 1, 3, 4)
    gather = jax.vmap(jax.vmap(lambda blk, ix: blk[ix]))

    def sel_chunk(args):
        qi, ix, ci = args
        kg = gather(k_blocks, ix)
        vg = gather(v_blocks, ix)
        s = jnp.einsum('bqgrd,bgqnld->bgrqnl', qi, kg).astype(f32) * scale
        tok = ix[..., None] * SEL_LEN + jnp.arange(SEL_LEN)
        qt = ci * SEL_Q_BLOCK + jnp.arange(SEL_Q_BLOCK)
        mask = tok <= qt[None, None, :, None, None]
        s = jnp.where(mask[:, :, None], s, NEG)
        sh = s.shape
        p = jax.nn.softmax(s.reshape(sh[0], sh[1], sh[2], sh[3], -1), axis=-1).reshape(sh)
        return jnp.einsum('bgrqnl,bgqnld->bqgrd', p.astype(vg.dtype), vg)

    o_s = lax.map(sel_chunk, (q_chunks, idx_chunks, jnp.arange(nqb)))
    o_s = o_s.transpose(1, 0, 2, 3, 4, 5).reshape(B, S, G, R, Dh)

    kw = partial_rope(rms_norm_2(k_w, kw_gain), cos_t, sin_t)
    nqw = S // Q_BLOCK
    span = WINDOW + Q_BLOCK
    kw_pad = jnp.pad(kw, ((0, 0), (WINDOW, 0), (0, 0), (0, 0)))
    vw_pad = jnp.pad(v_w, ((0, 0), (WINDOW, 0), (0, 0), (0, 0)))
    band = jnp.arange(nqw)[:, None] * Q_BLOCK + jnp.arange(span)[None, :]
    kb = kw_pad[:, band]
    vb = vw_pad[:, band]
    qb = qg.reshape(B, nqw, Q_BLOCK, G, R, Dh)
    s_w = jnp.einsum('bcqgrd,bckgd->bcgrqk', qb, kb).astype(f32) * scale
    key_t = band - WINDOW
    q_t = jnp.arange(nqw)[:, None] * Q_BLOCK + jnp.arange(Q_BLOCK)[None, :]
    diff = q_t[:, :, None] - key_t[:, None, :]
    mask_w = (diff >= 0) & (diff < WINDOW) & (key_t[:, None, :] >= 0)
    s_w = jnp.where(mask_w[None, :, None, None], s_w, NEG)
    p_w = jax.nn.softmax(s_w, axis=-1).astype(vb.dtype)
    o_w = jnp.einsum('bcgrqk,bckgd->bcqgrd', p_w, vb).reshape(B, S, G, R, Dh)

    g = jax.nn.sigmoid(g_logit).reshape(B, S, G, R, N_NSA_BRANCH, 1)
    o = g[..., 0, :] * o_c + g[..., 1, :] * o_s + g[..., 2, :] * o_w
    return o.reshape(B, S, H * Dh)

def second_inputs(seed: int = 0) -> dict:
    key = jax.random.key(seed)

    def nrm(i, shape, scale):
        return jax.random.normal(jax.random.fold_in(key, i), shape, jnp.float32) * scale

    def gain(i, n):
        return 1.0 + nrm(i, (DEPTH_2, n), 0.02)

    L = DEPTH_2
    offset = jax.random.randint(jax.random.fold_in(key, 99), (BATCH, 1), 0, 4096)
    positions = (offset + jnp.arange(SEQ)[None, :]).astype(jnp.int32)
    return {
        "x": nrm(0, (BATCH, SEQ, D_MODEL), 1.0),
        "c": nrm(1, (BATCH, D_MODEL), 1.0),
        "positions": positions,
        "ada_w": nrm(2, (L, D_MODEL, N_MOD * D_MODEL), 0.5 * D_MODEL ** -0.5),
        "ada_b": nrm(3, (L, N_MOD * D_MODEL), 0.02),
        "norm1_gain": gain(4, D_MODEL),
        "w_in": nrm(5, (L, D_MODEL, D_IN_2), D_MODEL ** -0.5),
        "mla_q_a_gain": gain(6, MLA_Q_LORA),
        "mla_w_q_b": nrm(7, (L, MLA_Q_LORA, MLA_HEADS * MLA_QK), MLA_Q_LORA ** -0.5),
        "mla_kv_a_gain": gain(8, MLA_KV_LORA),
        "mla_w_kv_b": nrm(9, (L, MLA_KV_LORA, MLA_HEADS * (MLA_NOPE + MLA_V)), MLA_KV_LORA ** -0.5),
        "mla_q_gain": gain(10, MLA_QK),
        "mla_k_gain": gain(11, MLA_QK),
        "nsa_q_gain": gain(12, NSA_HEAD),
        "nsa_kc_gain": gain(13, NSA_HEAD),
        "nsa_ks_gain": gain(14, NSA_HEAD),
        "nsa_kw_gain": gain(15, NSA_HEAD),
        "cmp_pos_k": nrm(16, (L, CMP_LEN, NSA_HEAD), 0.1),
        "cmp_w1_k": nrm(17, (L, CMP_LEN * NSA_HEAD, CMP_HIDDEN), (CMP_LEN * NSA_HEAD) ** -0.5),
        "cmp_w2_k": nrm(18, (L, CMP_HIDDEN, NSA_HEAD), CMP_HIDDEN ** -0.5),
        "cmp_pos_v": nrm(19, (L, CMP_LEN, NSA_HEAD), 0.1),
        "cmp_w1_v": nrm(20, (L, CMP_LEN * NSA_HEAD, CMP_HIDDEN), (CMP_LEN * NSA_HEAD) ** -0.5),
        "cmp_w2_v": nrm(21, (L, CMP_HIDDEN, NSA_HEAD), CMP_HIDDEN ** -0.5),
        "w_o_mla": nrm(22, (L, MLA_HEADS * MLA_V, D_MODEL), (MLA_HEADS * MLA_V) ** -0.5),
        "w_o_nsa": nrm(23, (L, NSA_HEADS * NSA_HEAD, D_MODEL), (NSA_HEADS * NSA_HEAD) ** -0.5),
        "w_out": nrm(24, (L, D_MODEL, D_MODEL), D_MODEL ** -0.5),
        "norm2_gain": gain(25, D_MODEL),
        "ffn_w_gate": nrm(26, (L, D_MODEL, D_FF_2), D_MODEL ** -0.5),
        "ffn_w_up": nrm(27, (L, D_MODEL, D_FF_2), D_MODEL ** -0.5),
        "ffn_w_down": nrm(28, (L, D_FF_2, D_MODEL), D_FF_2 ** -0.5),
    }

def second_block(x, c, positions, ada_w, ada_b, norm1_gain, w_in,
              mla_q_a_gain, mla_w_q_b, mla_kv_a_gain, mla_w_kv_b, mla_q_gain, mla_k_gain,
              nsa_q_gain, nsa_kc_gain, nsa_ks_gain, nsa_kw_gain,
              cmp_pos_k, cmp_w1_k, cmp_w2_k, cmp_pos_v, cmp_w1_v, cmp_w2_v,
              w_o_mla, w_o_nsa, w_out, norm2_gain, ffn_w_gate, ffn_w_up, ffn_w_down):
    B, S, _ = x.shape
    mla_cos, mla_sin = rope_angles(positions, MLA_ROPE)
    nsa_cos, nsa_sin = rope_angles(positions, NSA_ROT)
    split_at = np.cumsum(IN_SIZES)[:-1]
    for l in range(DEPTH_2):
        mod = jax.nn.silu(c) @ ada_w[l] + ada_b[l]
        sh1, sc1, gt1, sh2, sc2, gt2 = [m[:, None, :] for m in jnp.split(mod, N_MOD, axis=-1)]

        h = rms_norm_2(x, norm1_gain[l]) * (1.0 + sc1) + sh1
        z = h @ w_in[l]
        (c_q, c_kv, k_pe, q_n, k_c, v_c, k_s, v_s, k_w, v_w,
         g_nsa, g_mla_merge, g_nsa_merge) = jnp.split(z, split_at, axis=-1)
        y_mla = mla_attention(c_q, c_kv, k_pe, mla_cos, mla_sin,
                              mla_q_a_gain[l], mla_w_q_b[l], mla_kv_a_gain[l], mla_w_kv_b[l],
                              mla_q_gain[l], mla_k_gain[l]) @ w_o_mla[l]
        kvs = lambda t: t.reshape(B, S, NSA_KV_GROUPS, NSA_HEAD)
        y_nsa = nsa_attention(q_n.reshape(B, S, NSA_HEADS, NSA_HEAD),
                              kvs(k_c), kvs(v_c), kvs(k_s), kvs(v_s), kvs(k_w), kvs(v_w),
                              g_nsa.reshape(B, S, NSA_HEADS, N_NSA_BRANCH), nsa_cos, nsa_sin,
                              nsa_q_gain[l], nsa_kc_gain[l], nsa_ks_gain[l], nsa_kw_gain[l],
                              cmp_pos_k[l], cmp_w1_k[l], cmp_w2_k[l],
                              cmp_pos_v[l], cmp_w1_v[l], cmp_w2_v[l]) @ w_o_nsa[l]
        merged = jax.nn.sigmoid(g_mla_merge) * y_mla + jax.nn.sigmoid(g_nsa_merge) * y_nsa
        x = x + gt1 * (merged @ w_out[l])

        h2 = rms_norm_2(x, norm2_gain[l]) * (1.0 + sc2) + sh2
        x = x + gt2 * ((jax.nn.silu(h2 @ ffn_w_gate[l]) * (h2 @ ffn_w_up[l])) @ ffn_w_down[l])
    return x


def setup_inputs(seed=0):
    out = dict(first_inputs(seed))
    for name, value in second_inputs(seed + 1).items():
        if name != "x":
            out[name + "_2"] = value
    return out


def reference(
    x, p, norm_mix_g, w_in, pool_w, pool_scale, conv_w, q_norm_g, k_norm_g, lam_q1, lam_k1,
    lam_q2, lam_k2, sub_norm_g, w_pool_out, w_conv_out, w_attn_out, w_o, norm_mlp_g, w_up,
    w_down, norm_ple_g, w_ple_gate, w_ple_proj, c_2, positions_2, ada_w_2, ada_b_2,
    norm1_gain_2, w_in_2, mla_q_a_gain_2, mla_w_q_b_2, mla_kv_a_gain_2, mla_w_kv_b_2,
    mla_q_gain_2, mla_k_gain_2, nsa_q_gain_2, nsa_kc_gain_2, nsa_ks_gain_2, nsa_kw_gain_2,
    cmp_pos_k_2, cmp_w1_k_2, cmp_w2_k_2, cmp_pos_v_2, cmp_w1_v_2, cmp_w2_v_2, w_o_mla_2,
    w_o_nsa_2, w_out_2, norm2_gain_2, ffn_w_gate_2, ffn_w_up_2, ffn_w_down_2,
):
    x = first_block(
        x, p, norm_mix_g, w_in, pool_w, pool_scale, conv_w, q_norm_g, k_norm_g, lam_q1, lam_k1,
        lam_q2, lam_k2, sub_norm_g, w_pool_out, w_conv_out, w_attn_out, w_o, norm_mlp_g, w_up,
        w_down, norm_ple_g, w_ple_gate, w_ple_proj,
    )
    return second_block(
        x, c_2, positions_2, ada_w_2, ada_b_2, norm1_gain_2, w_in_2, mla_q_a_gain_2,
        mla_w_q_b_2, mla_kv_a_gain_2, mla_w_kv_b_2, mla_q_gain_2, mla_k_gain_2, nsa_q_gain_2,
        nsa_kc_gain_2, nsa_ks_gain_2, nsa_kw_gain_2, cmp_pos_k_2, cmp_w1_k_2, cmp_w2_k_2,
        cmp_pos_v_2, cmp_w1_v_2, cmp_w2_v_2, w_o_mla_2, w_o_nsa_2, w_out_2, norm2_gain_2,
        ffn_w_gate_2, ffn_w_up_2, ffn_w_down_2,
    )


_drawn_inputs = setup_inputs


def setup_inputs(seed=0):
    import zlib

    import numpy as np

    out = dict(_drawn_inputs(seed))
    spreads = {}
    factors = {'lam_q1': 6.374,
     'lam_q2': 4.282,
     'norm_ple_g': 3.674,
     'ada_b_2': 7.103,
     'norm1_gain_2': 8.0,
     'mla_q_a_gain_2': 8.0,
     'mla_w_q_b_2': 7.754,
     'mla_kv_a_gain_2': 22.473,
     'mla_q_gain_2': 8.0,
     'mla_k_gain_2': 8.0,
     'nsa_q_gain_2': 8.0,
     'nsa_kc_gain_2': 8.0,
     'nsa_ks_gain_2': 35.486,
     'nsa_kw_gain_2': 30.709,
     'cmp_pos_k_2': 8.0,
     'cmp_w1_k_2': 8.0,
     'cmp_w2_k_2': 8.0,
     'cmp_pos_v_2': 8.0,
     'cmp_w1_v_2': 4.433,
     'cmp_w2_v_2': 3.607,
     'norm2_gain_2': 8.0}
    for name, (base, spread) in spreads.items():
        noise = np.random.default_rng([zlib.crc32(name.encode()), seed]).standard_normal(out[name].shape)
        drawn = base * np.exp(spread * noise) if base else spread * noise
        out[name] = __import__('jax').numpy.asarray(drawn.astype(out[name].dtype))
    for name, factor in factors.items():
        out[name] = (out[name] * factor).astype(out[name].dtype)
    return out
```

```python
import math
from contextlib import ExitStack

import numpy as np
import concourse.bass as bass
from concourse import mybir

P = 128
S = 512
D = 1024
KT = D // P
DEPTH = 2
QB = S // P
UNIT = 2048
NEG = -1e30
EPS = 1e-6
CMP_N, CMP_W = 31, 32
WINDOWS = (2, 4, 8, 16)
MLA_D = 96
PAD = 16
ROW = PAD + S
CHUNKS_2 = (8, 8, 6)
MAGIC = 12582912.0


def stages():
    out = []
    for l in range(DEPTH):
        out += [(f"qk{l}", 4, 2), (f"v{l}", 2, 4), (f"pool_in{l}", 2, 2), (f"gate_a{l}", 4, 2),
                (f"out_a{l}", 2, 4), (f"conv_in{l}", 6, 2), (f"gate_b{l}", 4, 2), (f"out_b{l}", 2, 4),
                (f"gate_c{l}", 4, 2), (f"out_c{l}", 2, 4), (f"w_o{l}", 4, 2), (f"mlp{l}", 32, 2),
                (f"ple_proj{l}", 1, 8), (f"ple_gate{l}", 4, 2)]
    out += [("lora", 4, 2), ("misc", 1, 1)]
    for half in range(2):
        out += [(f"mla_q{half}", 2, 2), (f"mla_k{half}", 1, 4)] + [("mla_v", 1, 4)] * (half == 0)
    out += [("gate_mla", 4, 2), ("out_mla", 2, 4), ("nsa_in", 4, 2), ("nsa_v", 1, 4), ("cmp", 4, 1),
            ("gate_nsa", 4, 2), ("out_nsa", 2, 4), ("w_out", 4, 2)]
    for c, tiles in enumerate(CHUNKS_2):
        out += [(f"ffn_up{c}", tiles, 2), (f"ffn_down{c}", 4, 2)]
    return out


def stream_table():
    table, n, g = {}, 0, 0
    for name, units, tiles in stages():
        table[name] = (n, g, units, tiles)
        n, g = n + units, g + units * tiles
    return table, n


def columns(widths):
    table, at = {}, 0
    for name, width in widths:
        table[name] = (at, width)
        at += width
    return table, at


def vec_table():
    w = []
    for l in range(DEPTH):
        w += [(f"mix{l}", 8), (f"pool_scale{l}", 4), (f"conv{l}", 12), (f"qg{l}", 1), (f"kg{l}", 1),
              (f"lam{l}", 4), (f"sub{l}", 1), (f"mlp{l}", 8), (f"ple{l}", 8)]
    w += [("n1", 8), ("n2", 8), ("ada_b", 48), ("c", 8), ("q_a", 6), ("kv_a", 2), ("mla_q", 1),
          ("mla_k", 1), ("nsa_q", 1), ("nsa_kc", 1), ("nsa_ks", 1), ("nsa_kw", 1), ("pos_k", 32),
          ("pos_v", 32)]
    return columns(w)


def const_table():
    return columns([("ident", P), ("ones", P), ("blocks", P), ("row96", 31), ("row64", 88),
                    ("causal", P), ("far", P), ("cmp_mask", QB * CMP_W), ("cmp_valid", QB * CMP_W),
                    ("inv_count", 16), ("freq_mla", 1), ("freq_nsa", 1), ("phase_mla", 1),
                    ("rot", P), ("eps", 1)])


def program(nc, weights, ada, vecs_d, consts_d, spread_d, x_t, p_t, pool_w, cmp_w2, positions, out):
    F32, F32R, I32 = mybir.dt.float32, mybir.dt.float32r, mybir.dt.int32
    ALU, ACT, AX = mybir.AluOpType, mybir.ActivationFunctionType, mybir.AxisListType
    ST, NU = stream_table()
    VT, NV = vec_table()
    CT, NCOL = const_table()
    ctx = ExitStack()
    with ctx:
        def sb(name, shape, dt=F32):
            return ctx.enter_context(nc.sbuf_tensor(name, shape, dt))

        raw = [sb(f"raw{i}", [P, UNIT]) for i in range(2)]
        w_hi = [sb(f"w_hi{i}", [P, UNIT], F32R) for i in range(2)]
        w_lo = [sb(f"w_lo{i}", [P, UNIT], F32R) for i in range(2)]
        h = sb("h", [P, KT, S])
        a_hi = sb("a_hi", [P, KT, S], F32R)
        a_lo = sb("a_lo", [P, KT, S], F32R)
        with ExitStack() as place:
            gate = place.enter_context(nc.sbuf_tensor("gate", [P, KT, S], F32))
            merged = place.enter_context(nc.sbuf_tensor("merged", [P, KT, S], F32))
        f_hi = sb("f_hi", [P, KT, S], F32R)
        f_lo = sb("f_lo", [P, KT, S], F32R)
        y_hi = sb("y_hi", [P, 4, S], F32R)
        y_lo = sb("y_lo", [P, 4, S], F32R)
        with ExitStack() as place:
            lora = place.enter_context(nc.sbuf_tensor("lora", [P, KT, S], F32))
        with ExitStack() as place:
            ada_w = [place.enter_context(nc.sbuf_tensor(f"ada_w{i}", [P, UNIT], F32)) for i in range(2)]
        qt = sb("qt", [P, 4, S])
        kt = sb("kt", [P, 4, S])
        vt = sb("vt", [P, 4, S])
        pads = sb("pads", [P, 4, ROW])
        pT = [sb(f"pT{i}", [P, S]) for i in range(2)]
        T = [sb(f"T{i}", [P, S]) for i in range(4)]
        tab = sb("tab", [P, 3, S])
        consts = sb("consts_sb", [P, NCOL])
        vecs = sb("vecs_sb", [P, NV])
        rows = sb("rows", [P, S])
        wsmall = sb("wsmall", [P, S])
        mod = sb("mod", [P, 48])
        scaled = sb("scaled", [P, 24])
        neg_lam = sb("neg_lam", [P, 2])
        small = sb("small", [P, 24])
        gt = sb("gt", [P, QB, 24])

        ps = [ctx.enter_context(nc.psum_tensor(f"ps{i}", [P, S], F32)) for i in range(8)]

        sems = {}

        def sem(name):
            if name not in sems:
                sems[name] = ctx.enter_context(nc.semaphore(name))
            return sems[name]

        def V(name, k=0, r=slice(0, P)):
            at, _ = VT[name]
            return vecs[r, at + k:at + k + 1]

        def V_range(name):
            at, width = VT[name]
            return vecs[:, at:at + width]

        def windows(which):
            return pads[:, 2 * which:2 * which + 2, :].rearrange("p a n -> p (a n)")[:, 0:16 * 64]

        def C(name, r=slice(0, P), lo=0, hi=None):
            at, width = CT[name]
            return consts[r, at + lo:at + (width if hi is None else hi)]

        class Counts:

            def __init__(self):
                self.n, self.open = {}, []

            def next(self, name):
                self.n[name] = self.n.get(name, 0) + 1
                value = self.n[name]
                for i, per, _ in self.open:
                    value = value + i * per[name]
                return sem(name), value

            def enter(self, i, per):
                self.open.append((i, per, dict(self.n)))

            def leave(self, turns):
                _, per, before = self.open.pop()
                for name in set(self.n) | set(per):
                    assert self.n.get(name, 0) - before.get(name, 0) == per.get(name, 0), name
                    self.n[name] = before.get(name, 0) + turns * per.get(name, 0)


        def loaded(n, off2=0):
            return sem(f"loaded{n % 2}"), 16 * (n // 2 + 1) + 16 * off2

        def tile_done(g, off4=0):
            return sem("tile_done"), g + 1 + 4 * off4

        def evacuated(g, off4=0):
            return sem(f"bank_free{g % 4}"), g // 4 + 1 + off4

        def bank(g):
            return ps[g % 4]


        def diff_steps():
            out = []
            for hd in range(4):
                for b in range(QB):
                    w = (b + 1) * P
                    out.append(dict(
                        kind="diff", w=w, rows=P, masks=(),
                        sets=[(qt[64 * c:64 * c + 64, hd, b * P:(b + 1) * P],
                               kt[64 * c:64 * c + 64, hd, 0:w]) for c in range(2)],
                        values=[vt[:, j, hd * P:(hd + 1) * P] for j in range(b + 1)],
                        out=ps[7][:, b * P:(b + 1) * P], first=True, last=True,
                        opens=b == 0, closes=b == QB - 1, tile=hd))
            return out

        def mla_steps(half):
            out = []
            for i in range(4):
                for b in range(QB):
                    w = (b + 1) * P
                    r, hd = 64 * (i % 2), 4 * half + i
                    out.append(dict(
                        kind="plain", w=w, rows=P, masks=((w - P, C("causal")),),
                        sets=[(qt[0:MLA_D, i, b * P:(b + 1) * P], kt[0:MLA_D, i, 0:w])],
                        values=[vt[:, j, hd * 64:(hd + 1) * 64] for j in range(b + 1)],
                        out=ps[7][r:r + 64, b * P:(b + 1) * P], first=True, last=True,
                        opens=b == 0 and i % 2 == 0, closes=b == QB - 1 and i % 2 == 1,
                        tile=2 * half + i // 2))
            return out

        def nsa_steps():
            out = []
            for t in range(4):
                for g in range(2):
                    r, hd = slice(64 * g, 64 * g + 64), t + 4 * g
                    for b in range(QB):
                        q = qt[r, t, b * P:(b + 1) * P]
                        o = ps[7][r, b * P:(b + 1) * P]
                        k0, w = max(0, b - 2), (b + 1) * P
                        n = w - k0 * P
                        base = dict(out=o, tile=t)
                        out.append(dict(
                            kind="cmp", w=CMP_W, rows=CMP_W,
                            masks=((0, C("cmp_mask", lo=b * CMP_W, hi=(b + 1) * CMP_W)),),
                            valid=C("cmp_valid", lo=b * CMP_W, hi=(b + 1) * CMP_W),
                            gate=gt[:, b, 3 * hd:3 * hd + 1],
                            sets=[(q, kt[r, 2, P:P + CMP_W])],
                            values=[kt[0:CMP_W, 2, 256 + 64 * g:256 + 64 * g + 64]],
                            first=True, last=False, opens=b == 0 and g == 0, closes=False, **base))
                        out.append(dict(
                            kind="plain", w=w, rows=P, masks=((w - P, C("causal")),),
                            gate=gt[:, b, 3 * hd + 1:3 * hd + 2],
                            sets=[(q, kt[r, 0, 0:w])],
                            values=[vt[:, j, 64 * g:64 * g + 64] for j in range(b + 1)],
                            first=False, last=False, opens=False, closes=False, **base))
                        out.append(dict(
                            kind="plain", w=n, rows=P,
                            masks=((n - P, C("causal")),) + (((0, C("far")),) if b >= 2 else ()),
                            gate=gt[:, b, 3 * hd + 2:3 * hd + 3],
                            sets=[(q, kt[r, 1, k0 * P:w])],
                            values=[vt[:, j, P + 64 * g:P + 64 * g + 64] for j in range(k0, b + 1)],
                            first=False, last=True, opens=False, closes=b == QB - 1 and g == 1, **base))
            return out

        ATTENTION = [diff_steps()] * DEPTH + [mla_steps(0), mla_steps(1), nsa_steps()]
        STEP0 = [sum(len(a) for a in ATTENTION[:i]) for i in range(len(ATTENTION) + 1)]
        MC = [sum(len(x["sets"]) for a in ATTENTION[:i] for x in a) for i in range(len(ATTENTION) + 1)]

        def probs(m, diff):
            return pads[:, m % (4 if diff else 2), 0:S]

        block = ctx.enter_context(nc.Block())

        @block.sync
        def _(sp):
            sp.dma_start(vecs[:, :], vecs_d).then_inc(sem("vecs_loaded"), 16)
            sp.dma_start(consts[:, :], consts_d).then_inc(sem("consts_loaded"), 16)
            sp.dma_start(h[:, :, :], x_t).then_inc(sem("h_loaded"), 16)
            for n in range(2):
                sp.dma_start(raw[n][:, :], weights[n]).then_inc(sem(f"loaded{n}"), 16)
            sp.dma_start(tab[0:40, 0, :], spread_d).then_inc(sem("spread_loaded"), 16)

            def unit(n, off2=0):
                sp.wait_ge(sem("lo_made"), n - 1 + 2 * off2)
                src = weights[n] if isinstance(off2, int) else weights[n + 2 * off2]
                sp.dma_start(raw[n % 2][:, :], src).then_inc(*inc(loaded(n)))

            def inc(x):
                return x[0], 16

            n0, g0, units, _ = ST["cmp"]

            def loop(a, b):
                if (b - a) % 2:
                    unit(a)
                    a += 1
                with sp.Fori(0, (b - a) // 2) as i:
                    for s in range(2):
                        unit(a + s, i)

            loop(2, n0 + 2)
            for j in range(units):
                sp.wait_ge(*tile_done(g0 + j))
                unit(n0 + 2 + j)
            loop(n0 + 2 + units, NU)
            g_last = ST["ffn_down2"][1]
            for t in range(KT):
                sp.wait_ge(*evacuated(g_last + t))
                sp.dma_start(out[t], h[:, t, :]).then_inc(sem("stored"), 16)
            sp.wait_ge(sem("stored"), 16 * KT)

        @block.gpsimd
        def _(pool):
            c = Counts()

            def seq(ins):
                ins.then_inc(sem("pool_seq"), 1)
                pool.wait_ge(*c.next("pool_seq"))

            pos, turn, ang, t0, t1 = (merged[:, i, :] for i in range(5))
            hi, lo = merged[:, 5, :], merged[:, 6, :]
            posi = merged[:, 7, :].bitcast(I32)
            pool.dma_start(posi, positions.to_broadcast([P, S])).then_inc(sem("pos_loaded"), 16)
            pool.wait_ge(sem("pos_loaded"), 16)
            pool.wait_ge(sem("consts_loaded"), 16)
            seq(pool.tensor_copy(pos, posi))

            def wrap(x, r, y):
                seq(pool.tensor_scalar(r, x, MAGIC, None, ALU.add))
                seq(pool.tensor_scalar(r, r, MAGIC, None, ALU.subtract))
                seq(pool.tensor_tensor(y, x, r, ALU.subtract))

            digits = 15915494309189533576888376337251436203445964574046 * 2 ** 80 // 10 ** 50
            parts = [float(digits >> (66 - 12 * k) & 4095) / 2.0 ** (14 + 12 * k) for k in range(5)]
            for which, freq in ((0, "freq_mla"), (1, "freq_nsa")):
                seq(pool.tensor_scalar(ang, pos, C(freq), None, ALU.mult))
                seq(pool.tensor_scalar(t0, ang, 4097.0, None, ALU.mult))
                seq(pool.tensor_tensor(t1, t0, ang, ALU.subtract))
                seq(pool.tensor_tensor(hi, t0, t1, ALU.subtract))
                seq(pool.tensor_tensor(lo, ang, hi, ALU.subtract))
                first = True
                for half, k in ((hi, 5), (lo, 4)):
                    for part in parts[:k]:
                        seq(pool.tensor_scalar(t0, half, part, None, ALU.mult))
                        wrap(t0, t1, turn if first else t0)
                        if not first:
                            seq(pool.tensor_tensor(turn, turn, t0, ALU.add))
                        first = False
                for table in ((0,) if which == 0 else (1, 2)):
                    shift = C("phase_mla") if table == 0 else (0.25 if table == 1 else 0.0)
                    r = slice(64, P) if table == 0 else slice(0, P)
                    if table == 0:
                        shift = C("phase_mla", r)
                    seq(pool.tensor_scalar(t0[r], turn[r], shift, None, ALU.add))
                    seq(pool.tensor_scalar(t1[r], t0[r], MAGIC, None, ALU.add))
                    seq(pool.tensor_scalar(t1[r], t1[r], MAGIC, None, ALU.subtract))
                    pool.tensor_tensor(tab[r, table, :], t0[r], t1[r], ALU.subtract)\
                        .then_inc(sem("turns_made"), 1)
                    pool.wait_ge(sem("turns_made"), {0: 1, 1: 2, 2: 3}[table])

        @block.scalar
        def _(act):
            c = Counts()

            def split(n, g, off2=0, off4=0):
                if n >= NU:
                    return
                act.wait_ge(*loaded(n, off2))
                if n >= 2:
                    act.wait_ge(*tile_done(g - 1, off4))
                act.activation(w_hi[n % 2][:, :], raw[n % 2][:, :], ACT.Copy).then_inc(sem("hi_made"), 1)

            def x_high(dst, src, **kw):
                act.wait_ge(*c.next("value_made"))
                act.activation(dst, src, kw.pop("func", ACT.Copy), **kw).then_inc(sem("xhi_made"), 1)

            def run(name, tile, per=None, loop=False, first=0, last=None):
                n0, g0, units, tpu = ST[name]
                last = units if last is None else last

                def body(u, off2, off4):
                    n, g = n0 + u, g0 + u * tpu
                    split(n + 1, g, off2, off4)
                    for j in range(tpu):
                        tile(u * tpu + j, g + j, off4, 4 * off4 if not isinstance(off4, int) else 0)

                if not loop:
                    for u in range(first, last):
                        body(u, 0, 0)
                    return
                with act.Fori(0, units // 2) as i:
                    c.enter(i, per or {})
                    for u in range(2):
                        body(u, i, i * (tpu // 2))
                    c.leave(units // 2)

            norms = 0

            def norm(ready, shift=None):
                nonlocal norms
                ready()
                for k in range(KT):
                    if k >= 2:
                        act.wait_ge(sem("sq_added"), 7 * norms + max(1, k - 2))
                    act.activation(T[k % 2][:, :], h[:, k, :], ACT.Square).then_inc(sem("sq_made"), 1)
                norms += 1
                act.wait_ge(*c.next("norm_summed"))
                act.activation(T[0][:, :], ps[7][:, :], ACT.Sqrt, scale=1.0 / D, bias=C("eps"))\
                    .then_inc(sem("std_made"), 1)
                for k in range(KT):
                    if shift is None:
                        x_high(a_hi[:, k, :], T[2 + k % 2][:, :])
                    else:
                        x_high(a_hi[:, k, :], T[2 + k % 2][:, :], func=ACT.Identity,
                               bias=mod[:, shift + k:shift + k + 1])

            def head_squares(t, g, r=slice(0, P)):
                act.wait_ge(*tile_done(g))
                if t >= 2:
                    act.wait_ge(*c.next("hsq_summed"))
                act.activation(T[t % 2][r], bank(g)[r], ACT.Square).then_inc(sem("hsq_made"), 1)

            def head_std(n_rows, width, pending=2):
                for _ in range(pending):
                    at = c.next("hsq_summed")
                act.wait_ge(*at)
                act.activation(rows[0:n_rows, :], ps[5][0:n_rows, :], ACT.Sqrt, scale=1.0 / width,
                               bias=C("eps", slice(0, n_rows))).then_inc(sem("hstd_made"), 1)

            def attention(which):
                steps, s0, m = ATTENTION[which], STEP0[which], MC[which]
                diff = steps[0]["kind"] == "diff"
                for s in range(len(steps) + 1):
                    if s < len(steps):
                        x = steps[s]
                        for j in range(len(x["sets"])):
                            act.wait_ge(*c.next("max_made"))
                            k = 2 * (s % 2) + j
                            act.activation(probs(m, diff)[:, 0:x["w"]], ps[4 + m % 2][:, 0:x["w"]], ACT.Exp,
                                           bias=small[:, k:k + 1], scale=1.0,
                                           accum_out=small[:, 4 + k:5 + k]).then_inc(sem("exp_done"), 1)
                            m += 1
                    if s >= 1:
                        x = steps[s - 1]
                        act.wait_ge(*c.next("pT_in_psum"))
                        if s0 + s - 1 >= 2:
                            act.wait_ge(sem("pv_done"), s0 + s - 2)
                        w = P if x["kind"] == "cmp" else x["w"]
                        act.activation(pT[(s - 1) % 2][0:x["rows"], 0:w], ps[6][0:x["rows"], 0:w], ACT.Copy)\
                            .then_inc(sem("pT_made"), 1)
                        if x["closes"] and not diff:
                            act.wait_ge(sem("pv_done"), s0 + s)
                            act.activation(y_hi[:, x["tile"], :], ps[7][:, :], ACT.Copy)\
                                .then_inc(sem("xhi_made"), 1)

            def to_gate(t, g, off4, to):
                act.wait_ge(*tile_done(g, off4))
                dst = gate[:, t, :] if isinstance(to, int) else gate[:, bass.ds(t + to, 1), :]
                src = bank(g)[:, :] if isinstance(to, int) else bank(g)[:, :].unsqueeze(1)
                act.activation(dst, src, ACT.Tanh, scale=0.5).then_inc(sem(f"bank_free{g % 4}"), 1)

            def nothing(t, g, off4, to):
                pass

            def merged_high(t, g, off4, to):
                x_high(a_hi[:, t, :], T[2 + t % 2][:, :], scale=0.5)

            split(0, 0)
            act.wait_ge(sem("vecs_loaded"), 16)
            act.wait_ge(*c.next("lam_summed"))
            act.activation(small[:, 8:12], ps[6][:, 0:4], ACT.Exp).then_inc(sem("lam_exp"), 1)
            act.activation(small[:, 16:24], V_range("c"), ACT.Tanh, scale=0.5).then_inc(sem("c_tanh"), 1)

            for l in range(DEPTH):
                if l == 0:
                    norm(lambda: act.wait_ge(sem("h_loaded"), 16))
                else:
                    norm(lambda: act.wait_ge(sem("ple_added"), 8 * l))
                act.dma_start(wsmall[:, :], pool_w[l]).then_inc(sem("small_loaded"), 16)

                run(f"qk{l}", lambda t, g, off4, to: head_squares(t, g))
                head_std(40, 64)

                def value(t, g, off4, to):
                    u, tok = t // 4, t % 4
                    act.wait_ge(*tile_done(g))
                    act.activation(vt[:, tok, 256 * u:256 * u + 256], bank(g)[:, 0:256], ACT.Copy)\
                        .then_inc(sem(f"bank_free{g % 4}"), 1)
                run(f"v{l}", value)
                attention(l)
                run(f"pool_in{l}", nothing)
                for t in range(4):
                    act.wait_ge(*c.next("mixed"))
                    act.activation(y_hi[:, t, :], ps[6 + t % 2][:, :], ACT.Copy, scale=V(f"pool_scale{l}", t))\
                        .then_inc(sem("xhi_made"), 1)
                run(f"gate_a{l}", to_gate, loop=True)
                run(f"out_a{l}", nothing)

                def conv(t, g, off4, to):
                    kind, j = t % 3, t // 3
                    act.wait_ge(*tile_done(g))
                    if kind < 2:
                        act.activation(T[kind][:, :], bank(g)[:, :], ACT.Copy)\
                            .then_inc(sem(f"bank_free{g % 4}"), 1)
                    else:
                        x_high(y_hi[:, j, :], T[2 + j % 2][:, :])
                run(f"conv_in{l}", conv)
                run(f"gate_b{l}", to_gate, loop=True)
                run(f"out_b{l}", nothing)
                run(f"gate_c{l}", to_gate, loop=True)
                for hd in range(4):
                    if hd >= 2:
                        act.wait_ge(*c.next("hsq_summed"))
                    act.activation(T[hd % 2][:, :], qt[:, hd, :], ACT.Square).then_inc(sem("hsq_made"), 1)
                head_std(4, P)
                for hd in range(4):
                    x_high(y_hi[:, hd, :], T[2 + hd % 2][:, :])
                run(f"out_c{l}", merged_high)
                run(f"w_o{l}", nothing, loop=True)
                g_wo = ST[f"w_o{l}"][1]
                norm(lambda: act.wait_ge(*evacuated(g_wo + 7)))
                act.dma_start(pads[:, 2:4, 0:S], p_t[l]).then_inc(sem("p_loaded"), 16)
                act.wait_ge(sem("p_loaded"), 16 * (l + 1))
                for t in range(2):
                    act.activation(y_hi[:, t, :], pads[:, 2 + t, 0:S], ACT.Copy).then_inc(sem("xhi_made"), 1)

                n0, g0, _, _ = ST[f"mlp{l}"]
                with act.Fori(0, 4) as ch:
                    c.enter(ch, {"value_made": 8})
                    with act.Fori(0, 2) as i:
                        c.enter(i, {"value_made": 4})
                        for u in range(2):
                            split(n0 + u + 1, g0 + 2 * u, 4 * ch + i, 4 * ch + i)
                            for j in range(2):
                                t = 2 * u + j
                                act.wait_ge(*tile_done(g0 + t, 4 * ch + i))
                                act.activation(T[t % 2][:, :], bank(g0 + t)[:, :], ACT.Relu)\
                                    .then_inc(sem("relu_made"), 1)
                                x_high(f_hi[:, bass.ds(t + 4 * i, 1), :], T[2 + t % 2][:, :].unsqueeze(1))
                        c.leave(2)
                    with act.Fori(0, 2) as i:
                        for u in range(2):
                            split(n0 + 4 + u + 1, g0 + 8 + 2 * u, 4 * ch + i, 4 * ch + i)
                    c.leave(4)

                def projected(t, g, off4, to):
                    act.wait_ge(*tile_done(g))
                    act.activation(gate[:, t, :], bank(g)[:, :], ACT.Copy).then_inc(sem(f"bank_free{g % 4}"), 1)
                run(f"ple_proj{l}", projected)
                norm(lambda: act.wait_ge(*evacuated(g0 + 63)))

                def ple(t, g, off4, to):
                    act.wait_ge(*tile_done(g))
                    if t >= 2:
                        act.wait_ge(sem("ple_added"), 8 * l + t - 1)
                    act.activation(T[t % 2][:, :], bank(g)[:, :], ACT.Tanh, scale=0.5)\
                        .then_inc(sem(f"bank_free{g % 4}"), 1)
                run(f"ple_gate{l}", ple)

            for table in range(3):
                r = slice(64, P) if table == 0 else slice(0, P)
                act.wait_ge(sem("turns_made"), table + 1)
                act.activation(tab[r, table, :], tab[r, table, :], ACT.Sin, scale=6.283185)\
                    .then_inc(sem("tables_made"), 1)
            act.wait_ge(sem("ple_added"), 8 * DEPTH)
            act.dma_start(wsmall[:, 0:256], cmp_w2).then_inc(sem("small_loaded"), 16)
            for a in range(2):
                act.dma_start(ada_w[a][:, :], ada[a]).then_inc(sem(f"ada_loaded{a}"), 16)
            with act.Fori(0, 11) as i:
                for a in range(2):
                    act.wait_ge(sem("ada_acc"), 2 * i + a + 1)
                    act.dma_start(ada_w[a][:, :], ada[2 * i + (a + 2)]).then_inc(sem(f"ada_loaded{a}"), 16)
            norm(lambda: act.wait_ge(sem("mod_made"), 1), shift=0)

            def lora_in(t, g, off4, to):
                head_squares(t, g)
            run("lora", lora_in)
            run("misc", lambda t, g, off4, to: None)
            g = ST["misc"][1]
            act.wait_ge(*c.next("hsq_summed"))
            act.wait_ge(*c.next("hsq_summed"))
            act.activation(pads[:, 0, 0:S], ps[4][:, :], ACT.Sqrt, scale=1.0 / 768, bias=C("eps"))\
                .then_inc(sem("hstd_made"), 1)
            act.activation(pads[:, 1, 0:S], ps[5][:, :], ACT.Sqrt, scale=1.0 / 256, bias=C("eps"))\
                .then_inc(sem("hstd_made"), 1)
            for t in range(KT):
                x_high(f_hi[:, t, :], T[2 + t % 2][:, :])
            act.wait_ge(*c.next("misc_made"))
            act.activation(T[0][0:24, :], pads[0:24, 2, 0:S], ACT.Tanh, scale=0.5).then_inc(sem("g_tanh"), 1)

            for half in range(2):
                def mla_q(t, g, off4, to):
                    head_squares(t, g, slice(0, MLA_D))
                run(f"mla_q{half}", mla_q)

                def mla_k(t, g, off4, to):
                    act.wait_ge(*tile_done(g))
                    act.wait_ge(*c.next("hsq_summed"))
                    act.activation(T[t % 2][64:96, :], pads[64:96, 2, 0:S], ACT.Square)
                    act.activation(T[t % 2][0:64, :], bank(g)[0:64, :], ACT.Square).then_inc(sem("hsq_made"), 1)
                run(f"mla_k{half}", mla_k)
                head_std(8, MLA_D)
                if half == 0:
                    def mla_v(t, g, off4, to):
                        act.wait_ge(*tile_done(g))
                        act.activation(vt[:, t, :], bank(g)[:, :], ACT.Copy).then_inc(sem(f"bank_free{g % 4}"), 1)
                    run("mla_v", mla_v)
                attention(DEPTH + half)
            run("gate_mla", to_gate, loop=True)
            run("out_mla", nothing)

            def nsa_in(t, g, off4, to):
                if t < 6:
                    head_squares(t, g)
            run("nsa_in", nsa_in)
            head_std(40, 64)

            def nsa_v(t, g, off4, to):
                act.wait_ge(*tile_done(g))
                act.activation(vt[:, t, 0:256], bank(g)[:, 0:256], ACT.Copy).then_inc(sem(f"bank_free{g % 4}"), 1)
            run("nsa_v", nsa_v)

            def cmp(t, g, off4, to):
                if t % 2 == 0:
                    act.wait_ge(*tile_done(g))
                    if t == 2:
                        act.wait_ge(*c.next("hid_made"))
                    act.activation(T[0][0:64, 0:256], bank(g)[0:64, 0:256], ACT.Copy)\
                        .then_inc(sem(f"bank_free{g % 4}"), 1)
                    return
                act.wait_ge(*evacuated(g))
                act.activation(T[2][0:64, 0:256], T[1][0:64, 0:256], ACT.Tanh, scale=0.5)\
                    .then_inc(sem("hid_tanh"), 1)
                if t == 1:
                    act.wait_ge(*c.next("kc_in_psum"))
                    act.activation(rows[:, 64:64 + CMP_N], ps[7][:, 0:CMP_N], ACT.Square).then_inc(sem("kc_sq"), 1)
                    act.wait_ge(*c.next("kc_summed"))
                    act.activation(rows[:, 128:128 + CMP_N], ps[5][:, 0:CMP_N], ACT.Sqrt, scale=1.0 / 64,
                                   bias=C("eps")).then_inc(sem("kc_std"), 1)
                else:
                    act.wait_ge(*c.next("vc_in_psum"))
                    act.activation(kt[0:CMP_W, 2, 256:384], ps[7][0:CMP_W, 0:128], ACT.Copy).then_inc(sem("vc_made"), 1)
            run("cmp", cmp)
            attention(DEPTH + 2)
            run("gate_nsa", to_gate, loop=True)
            run("out_nsa", merged_high)
            run("w_out", nothing, loop=True)
            g_wo = ST["w_out"][1]
            norm(lambda: act.wait_ge(*evacuated(g_wo + 7)), shift=24)
            for ch, tiles in enumerate(CHUNKS_2):
                def up(t, g, off4, to):
                    if t % 2 == 0:
                        act.wait_ge(*tile_done(g, off4))
                        act.activation(T[0][:, :], bank(g)[:, :], ACT.Tanh, scale=0.5)\
                            .then_inc(sem("ff_tanh"), 1)
                    else:
                        u = t // 2
                        x_high(f_hi[:, u, :] if isinstance(to, int) else f_hi[:, bass.ds(u + 2 * off4, 1), :],
                               T[2][:, :] if isinstance(to, int) else T[2][:, :].unsqueeze(1))
                run(f"ffn_up{ch}", up, loop=True, per={"value_made": 2})
                run(f"ffn_down{ch}", nothing, loop=ch < 2)

        @block.vector
        def _(dve):
            c = Counts()

            def seq(ins):
                ins.then_inc(sem("dve_seq"), 1)
                dve.wait_ge(*c.next("dve_seq"))

            def split(n, off2=0):
                if n >= NU:
                    return
                dve.wait_ge(sem("hi_made"), n + 1 + 2 * off2)
                dve.tensor_tensor(w_lo[n % 2][:, :], raw[n % 2][:, :], w_hi[n % 2][:, :].bitcast(F32),
                                  ALU.subtract).then_inc(sem("lo_made"), 1)

            def x_low(dst, src, hi, tile=None):
                dve.wait_ge(*c.next("xhi_made"))
                ins = dve.tensor_tensor(dst, src, hi.bitcast(F32), ALU.subtract)
                if tile is None:
                    x_done(ins)
                else:
                    ins.then_inc(sem(f"bank_free{tile[0] % 4}"), 1)
                    dve.wait_ge(*evacuated(*tile))

            def x_done(ins):
                ins.then_inc(sem("x_made"), 1)
                dve.wait_ge(*c.next("x_made"))

            def run(name, tile, per=None, loop=False):
                n0, g0, units, tpu = ST[name]

                def body(u, off2, off4):
                    n, g = n0 + u, g0 + u * tpu
                    split(n + 1, off2)
                    for j in range(tpu):
                        tile(u * tpu + j, g + j, off4, 4 * off4 if not isinstance(off4, int) else 0)

                if not loop:
                    for u in range(units):
                        body(u, 0, 0)
                    return
                with dve.Fori(0, units // 2) as i:
                    c.enter(i, per or {})
                    for u in range(2):
                        body(u, i, i * (tpu // 2))
                    c.leave(units // 2)

            def at(tensor, t, to):
                return tensor[:, t, :] if isinstance(to, int) else tensor[:, bass.ds(t + to, 1), :]

            def like(x, to):
                return x if isinstance(to, int) else x.unsqueeze(1)

            def norm(gains, shift=None):
                total, r = pads[:, 0, 0:S], pads[:, 1, 0:S]
                dve.wait_ge(*c.next("sq_made"))
                dve.wait_ge(*c.next("sq_made"))
                dve.tensor_tensor(total, T[0][:, :], T[1][:, :], ALU.add).then_inc(sem("sq_added"), 1)
                for k in range(2, KT):
                    dve.wait_ge(*c.next("sq_added"))
                    dve.wait_ge(*c.next("sq_made"))
                    dve.tensor_tensor(total, total, T[k % 2][:, :], ALU.add).then_inc(sem("sq_added"), 1)
                c.next("sq_added")
                dve.wait_ge(*c.next("std_made"))
                seq(dve.reciprocal(r, T[0][:, :]))

                def value(k):
                    dve.scalar_tensor_tensor(T[2 + k % 2][:, :], h[:, k, :], gains(k), r, ALU.mult, ALU.mult)\
                        .then_inc(sem("value_made"), 1)

                def low(k):
                    if shift is None:
                        x_low(a_lo[:, k, :], T[2 + k % 2][:, :], a_hi[:, k, :])
                    else:
                        dve.wait_ge(*c.next("xhi_made"))
                        x_done(dve.scalar_tensor_tensor(a_lo[:, k, :], T[2 + k % 2][:, :],
                                                        mod[:, shift + k:shift + k + 1],
                                                        a_hi[:, k, :].bitcast(F32), ALU.add, ALU.subtract))
                value(0)
                for k in range(KT):
                    if k + 1 < KT:
                        value(k + 1)
                    low(k)

            def head_rows(n_rows):
                dve.wait_ge(*c.next("hstd_made"))
                dve.reciprocal(rows[0:n_rows, :], rows[0:n_rows, :]).then_inc(sem("hrows_made"), 1)

            def attention(which):
                steps, m0 = ATTENTION[which], MC[which]
                layer = which
                diff = steps[0]["kind"] == "diff"

                def maxes(s, m):
                    x = steps[s]
                    w = x["w"]
                    for j in range(len(x["sets"])):
                        dve.wait_ge(*c.next("scores_made"))
                        bk = ps[4 + (m + j) % 2]
                        if diff:
                            seq(dve.memset(bk[0:64, w - 64:w], NEG))
                        for lo, mask in x["masks"]:
                            n = mask.shape[-1]
                            seq(dve.tensor_tensor(bk[:, lo:lo + n], bk[:, lo:lo + n], mask, ALU.add))
                        k = 2 * (s % 2) + j
                        dve.tensor_reduce(small[:, k:k + 1], bk[:, 0:w], AX.X, ALU.max, negate=True)\
                            .then_inc(sem("max_made"), 1)

                def weigh(s, m):
                    x = steps[s]
                    w, k = x["w"], 2 * (s % 2)
                    for j in range(len(x["sets"])):
                        dve.wait_ge(*c.next("exp_done"))
                    p = probs(m, diff)[:, 0:w]
                    if s > 0:
                        dve.wait_ge(*c.next("att_made"))
                    if s == len(steps) - 1:
                        c.next("att_made")
                    if diff:
                        seq(dve.reciprocal(small[:, 12:14], small[:, 4 + k:6 + k]))
                        seq(dve.tensor_scalar(small[:, 14:15], small[:, 13:14],
                                              neg_lam[:, layer:layer + 1], None, ALU.mult))
                        seq(dve.tensor_scalar(p, p, small[:, 12:13], None, ALU.mult))
                        dve.scalar_tensor_tensor(p, probs(m + 1, diff)[:, 0:w], small[:, 14:15], p,
                                                 ALU.mult, ALU.add).then_inc(sem("att_made"), 1)
                        return
                    seq(dve.reciprocal(small[:, 12:13], small[:, 4 + k:5 + k]))
                    scale = small[:, 12:13]
                    if "gate" in x:
                        seq(dve.tensor_scalar(small[:, 13:14], scale, x["gate"], None, ALU.mult))
                        scale = small[:, 13:14]
                    if x["kind"] == "cmp":
                        dve.scalar_tensor_tensor(p, p, scale, x["valid"], ALU.mult, ALU.mult)\
                            .then_inc(sem("att_made"), 1)
                    else:
                        dve.tensor_scalar(p, p, scale, None, ALU.mult).then_inc(sem("att_made"), 1)

                ns = len(steps[0]["sets"])
                s0 = STEP0[which]
                maxes(0, m0)
                for s in range(len(steps) + 1):
                    if s + 1 < len(steps):
                        maxes(s + 1, m0 + ns * (s + 1))
                    if s < len(steps):
                        weigh(s, m0 + ns * s)
                    if s >= 1 and steps[s - 1]["closes"]:
                        t = steps[s - 1]["tile"]
                        dve.wait_ge(sem("pv_done"), s0 + s)
                        if diff:
                            dve.tensor_copy(qt[:, t, :], ps[7][:, :]).then_inc(sem("o_made"), 1)
                        else:
                            x_low(y_lo[:, t, :], ps[7][:, :], y_hi[:, t, :])

            def nothing(t, g, off4, to):
                pass

            def add_merged(first, last):
                def tile(t, g, off4, to):
                    dve.wait_ge(*tile_done(g))
                    if t == 0:
                        gates_ready()
                    dst = merged[:, t, :] if first else T[t % 2][:, :]
                    dve.scalar_tensor_tensor(dst, gate[:, t, :], 1.0, bank(g)[:, :], ALU.add, ALU.mult)\
                        .then_inc(sem(f"bank_free{g % 4}"), 1)
                    if first:
                        return
                    dve.wait_ge(*evacuated(g))
                    if not last:
                        seq(dve.tensor_tensor(merged[:, t, :], merged[:, t, :], dst, ALU.add))
                        return
                    u = T[2 + t % 2][:, :]
                    dve.tensor_tensor(u, merged[:, t, :], dst, ALU.add).then_inc(sem("value_made"), 1)
                    dve.wait_ge(*c.next("xhi_made"))
                    x_done(dve.scalar_tensor_tensor(a_lo[:, t, :], u, 0.5, a_hi[:, t, :].bitcast(F32),
                                                    ALU.mult, ALU.subtract))
                return tile

            def merge(gate_stage, out_stage, first, last):
                nonlocal gates_ready
                g_gate = ST[gate_stage][1]
                gates_ready = lambda: dve.wait_ge(*evacuated(g_gate + 7))
                run(gate_stage, nothing, loop=True)
                run(out_stage, add_merged(first, last))

            gates_ready = None

            def add_h(t, g, off4, to):
                dve.wait_ge(*tile_done(g, off4))
                dve.tensor_tensor(at(h, t, to), at(h, t, to), like(bank(g)[:, :], to), ALU.add)\
                    .then_inc(sem(f"bank_free{g % 4}"), 1)

            def add_h_times(col):
                def tile(t, g, off4, to):
                    dve.wait_ge(*tile_done(g, off4))
                    s = mod[:, col + t:col + t + 1] if isinstance(to, int) else mod[:, bass.ds(col + t + to, 1)]
                    dve.scalar_tensor_tensor(at(h, t, to), like(bank(g)[:, :], to), s, at(h, t, to),
                                             ALU.mult, ALU.add).then_inc(sem(f"bank_free{g % 4}"), 1)
                return tile

            split(0)
            dve.wait_ge(sem("vecs_loaded"), 16)
            for l in range(DEPTH):
                for j in range(2):
                    last = dve.tensor_tensor(small[:, 2 * l + j:2 * l + j + 1], V(f"lam{l}", 2 * j),
                                             V(f"lam{l}", 2 * j + 1), ALU.mult)
            last.then_inc(sem("lam_terms"), 1)
            dve.wait_ge(*c.next("lam_exp"))
            for l in range(DEPTH):
                init = 0.8 - 0.6 * math.exp(-0.3 * l)
                seq(dve.scalar_tensor_tensor(neg_lam[:, l:l + 1], small[:, 9 + 2 * l:10 + 2 * l], -init,
                                             small[:, 8 + 2 * l:9 + 2 * l], ALU.add, ALU.subtract))
                seq(dve.tensor_scalar(scaled[:, l:l + 1], V(f"sub{l}"), 1.0 - init, None, ALU.mult))
                seq(dve.tensor_scalar(scaled[:, 2 + l:3 + l], V(f"qg{l}"), 64.0 ** -0.5, None, ALU.mult))
            seq(dve.tensor_scalar(scaled[:, 4:5], V("mla_q"), float(MLA_D) ** -0.5, None, ALU.mult))
            seq(dve.tensor_scalar(scaled[:, 5:6], V("nsa_q"), 64.0 ** -0.5, None, ALU.mult))
            dve.wait_ge(*c.next("c_tanh"))
            seq(dve.scalar_tensor_tensor(scaled[:, 16:24], small[:, 16:24], 1.0, V_range("c"), ALU.add, ALU.mult))
            seq(dve.tensor_scalar(scaled[:, 8:16], scaled[:, 16:24], 0.5, None, ALU.mult))

            for l in range(DEPTH):
                norm(lambda k: V(f"mix{l}", k))

                def qk(t, g, off4, to):
                    dve.wait_ge(*c.next("hsq_made"))
                    dst = qt[:, t, :] if t < 4 else kt[:, t - 4, :]
                    gain = scaled[:, 2 + l:3 + l] if t < 4 else V(f"kg{l}")
                    dve.tensor_scalar(dst, bank(g)[:, :], gain, None, ALU.mult)\
                        .then_inc(sem(f"bank_free{g % 4}"), 1)
                run(f"qk{l}", qk)
                head_rows(40)
                run(f"v{l}", nothing)
                for t in range(8):
                    dve.wait_ge(*c.next("spread"))
                    x = qt[:, t, :] if t < 4 else kt[:, t - 4, :]
                    dve.tensor_tensor(x, x, ps[6 + t % 2][:, :], ALU.mult).then_inc(sem("qk_made"), 1)
                attention(l)

                for j in range(3):
                    seq(dve.memset(pads[:, j, 0:PAD], 0.0))

                def pool_in(t, g, off4, to):
                    dve.wait_ge(*tile_done(g))
                    dve.tensor_copy(pads[:, 0, PAD:ROW], bank(g)[:, :]).then_inc(sem(f"bank_free{g % 4}"), 1)
                    dve.wait_ge(*evacuated(g))
                    src, w = 0, 1
                    for step in range(t + 1):
                        dst = 1 + step % 2
                        seq(dve.tensor_tensor(pads[:, dst, PAD:ROW], pads[:, src, PAD:ROW],
                                              pads[:, src, PAD - w:ROW - w], ALU.add))
                        src, w = dst, 2 * w
                    pooled = T[t % 2]
                    seq(dve.scalar_tensor_tensor(pooled[:, :], pads[:, src, PAD:ROW], 1.0 / w,
                                                 pads[:, 0, PAD:ROW], ALU.mult, ALU.subtract))
                    seq(dve.tensor_tensor(T[2][:, 0:w - 1], pads[:, src, PAD:PAD + w - 1],
                                          C("inv_count", hi=w - 1), ALU.mult))
                    dve.tensor_tensor(pooled[:, 0:w - 1], T[2][:, 0:w - 1], pads[:, 0, PAD:PAD + w - 1],
                                      ALU.subtract).then_inc(sem("pooled"), 1)
                    dve.wait_ge(*c.next("pooled"))
                    if t >= 1:
                        pool_low(t - 1)
                    if t == 3:
                        pool_low(3)

                def pool_low(t):
                    dve.wait_ge(*c.next("xhi_made"))
                    x_done(dve.scalar_tensor_tensor(y_lo[:, t, :], ps[6 + t % 2][:, :], V(f"pool_scale{l}", t),
                                                    y_hi[:, t, :].bitcast(F32), ALU.mult, ALU.subtract))
                run(f"pool_in{l}", pool_in)
                dve.wait_ge(sem("turns_made"), 3)
                merge(f"gate_a{l}", f"out_a{l}", True, False)

                seq(dve.memset(pads[:, 0, 0:PAD], 0.0))

                def conv(t, g, off4, to):
                    kind, j = t % 3, t // 3
                    if kind < 2:
                        return
                    dve.wait_ge(*tile_done(g))
                    dve.wait_ge(*evacuated(g - 1))
                    dve.tensor_tensor(pads[:, 0, PAD:ROW], T[1][:, :], bank(g)[:, :], ALU.mult)\
                        .then_inc(sem(f"bank_free{g % 4}"), 1)
                    dve.wait_ge(*evacuated(g))
                    u = T[2 + j % 2][:, :]
                    seq(dve.tensor_scalar(u, pads[:, 0, PAD:ROW], V(f"conv{l}", 8 + j), None, ALU.mult))
                    for tap in (1, 0):
                        back = 2 - tap
                        seq(dve.scalar_tensor_tensor(u, pads[:, 0, PAD - back:ROW - back],
                                                     V(f"conv{l}", 4 * tap + j), u, ALU.mult, ALU.add))
                    dve.tensor_tensor(u, u, T[0][:, :], ALU.mult).then_inc(sem("value_made"), 1)
                    x_low(y_lo[:, j, :], u, y_hi[:, j, :])
                run(f"conv_in{l}", conv)
                merge(f"gate_b{l}", f"out_b{l}", False, False)

                g_gate = ST[f"gate_c{l}"][1]
                gates_ready = lambda: dve.wait_ge(*evacuated(g_gate + 7))
                run(f"gate_c{l}", nothing, loop=True)
                for hd in range(4):
                    c.next("hsq_made")
                head_rows(4)
                for hd in range(4):
                    dve.wait_ge(*c.next("spread"))
                    u = T[2 + hd % 2][:, :]
                    dve.scalar_tensor_tensor(u, qt[:, hd, :], scaled[:, l:l + 1], ps[6 + hd % 2][:, :],
                                             ALU.mult, ALU.mult).then_inc(sem("value_made"), 1)
                    x_low(y_lo[:, hd, :], u, y_hi[:, hd, :])
                run(f"out_c{l}", add_merged(False, True))
                run(f"w_o{l}", add_h, loop=True)
                norm(lambda k: V(f"mlp{l}", k))
                for t in range(2):
                    x_low(y_lo[:, t, :], pads[:, 2 + t, 0:S], y_hi[:, t, :])

                n0, g0, _, _ = ST[f"mlp{l}"]
                with dve.Fori(0, 4) as ch:
                    c.enter(ch, {"relu_made": 8, "xhi_made": 8})
                    with dve.Fori(0, 2) as i:
                        c.enter(i, {"relu_made": 4, "xhi_made": 4})
                        for u in range(2):
                            split(n0 + u + 1, 4 * ch + i)
                            for j in range(2):
                                t = 2 * u + j
                                dve.wait_ge(*c.next("relu_made"))
                                v = T[2 + t % 2][:, :]
                                dve.tensor_tensor(v, T[t % 2][:, :], bank(g0 + t)[:, :], ALU.mult)\
                                    .then_inc(sem("value_made"), 1)
                                dst = bass.ds(t + 4 * i, 1)
                                x_low(f_lo[:, dst, :], v.unsqueeze(1), f_hi[:, dst, :],
                                      tile=(g0 + t, 4 * ch + i))
                        c.leave(2)
                    with dve.Fori(0, 2) as i:
                        for u in range(2):
                            split(n0 + 4 + u + 1, 4 * ch + i)
                            for j in range(2):
                                t = 2 * u + j
                                dve.wait_ge(*tile_done(g0 + 8 + t, 4 * ch + i))
                                dst = h[:, bass.ds(t + 4 * i, 1), :]
                                dve.tensor_tensor(dst, dst, bank(g0 + 8 + t)[:, :].unsqueeze(1), ALU.add)\
                                    .then_inc(sem(f"bank_free{(g0 + 8 + t) % 4}"), 1)
                    c.leave(4)
                run(f"ple_proj{l}", nothing)
                norm(lambda k: V(f"ple{l}", k))

                def ple(t, g, off4, to):
                    dve.wait_ge(*evacuated(g))
                    v = T[2 + t % 2][:, :]
                    seq(dve.scalar_tensor_tensor(v, T[t % 2][:, :], 1.0, gate[:, t, :], ALU.add, ALU.mult))
                    dve.scalar_tensor_tensor(h[:, t, :], v, 0.5, h[:, t, :], ALU.mult, ALU.add)\
                        .then_inc(sem("ple_added"), 1)
                run(f"ple_gate{l}", ple)

            with dve.Fori(0, 12) as i:
                c.enter(i, {"dve_seq": 14})
                for a in range(2):
                    dve.wait_ge(sem(f"ada_loaded{a}"), 16 * i + 16)
                    acc = T[a][:, 0:256]
                    for k in range(KT):
                        w = ada_w[a][:, 256 * k:256 * k + 256]
                        s = scaled[:, 8 + k:9 + k]
                        if k == 0:
                            ins = dve.tensor_scalar(acc, w, s, None, ALU.mult)
                        else:
                            ins = dve.scalar_tensor_tensor(acc, w, s, acc, ALU.mult, ALU.add)
                        if k < KT - 1:
                            seq(ins)
                    ins.then_inc(sem("ada_acc"), 1)
                    dve.wait_ge(sem("ada_summed"), 2 * i + a + 1)
                c.leave(12)
            seq(dve.tensor_tensor(mod[:, :], ps[6][:, 0:48], V_range("ada_b"), ALU.add))
            for name, at_scale, to in (("n1", 8, 8), ("n2", 32, 16)):
                last = dve.scalar_tensor_tensor(scaled[:, to:to + 8], mod[:, at_scale:at_scale + 8], 1.0,
                                                V_range(name), ALU.add, ALU.mult)
            last.then_inc(sem("mod_made"), 1)
            dve.wait_ge(sem("mod_made"), 1)
            norm(lambda k: scaled[:, 8 + k:9 + k], shift=0)

            def lora_in(t, g, off4, to):
                dve.wait_ge(*c.next("hsq_made"))
                gain = V("q_a", t) if t < 6 else V("kv_a", t - 6)
                dve.tensor_scalar(lora[:, t, :], bank(g)[:, :], gain, None, ALU.mult)\
                    .then_inc(sem(f"bank_free{g % 4}"), 1)
            run("lora", lora_in)
            dve.wait_ge(*c.next("hstd_made"))
            seq(dve.reciprocal(pads[:, 0, 0:S], pads[:, 0, 0:S]))
            dve.wait_ge(*c.next("hstd_made"))
            seq(dve.reciprocal(pads[:, 1, 0:S], pads[:, 1, 0:S]))
            for t in range(KT):
                u = T[2 + t % 2][:, :]
                dve.tensor_tensor(u, lora[:, t, :], pads[:, 0 if t < 6 else 1, 0:S], ALU.mult)\
                    .then_inc(sem("value_made"), 1)
                x_low(f_lo[:, t, :], u, f_hi[:, t, :])

            def misc(t, g, off4, to):
                dve.wait_ge(*tile_done(g))
                dve.wait_ge(sem("tables_made"), 3)
                misc_t, kpe = pads[:, 2, 0:S], pads[:, 3, 0:S]
                dve.tensor_copy(misc_t, bank(g)[:, :]).then_inc(sem("misc_made"), 1)
                seq(dve.scalar_tensor_tensor(T[2][64:96, :], bank(g)[96:128, :], V("mla_k", 0, slice(96, 128)),
                                             tab[96:128, 0, :], ALU.mult, ALU.mult))
                seq(dve.scalar_tensor_tensor(kpe[64:96], bank(g)[64:96, :], V("mla_k", 0, slice(64, 96)),
                                             tab[64:96, 0, :], ALU.mult, ALU.mult))
                dve.tensor_tensor(kpe[64:96], kpe[64:96], T[2][64:96, :], ALU.add)\
                    .then_inc(sem(f"bank_free{g % 4}"), 1)
                dve.wait_ge(*evacuated(g))
            run("misc", misc)
            dve.wait_ge(*c.next("gt_in_psum"))
            seq(dve.tensor_scalar(gt[:, :, :], ps[6][:, 0:QB * P].rearrange("p (b n) -> p b n", b=QB)[:, :, 0:24],
                                  1.0, 0.5, ALU.add, ALU.mult))

            for half in range(2):
                def mla_q(t, g, off4, to):
                    dve.wait_ge(*c.next("hsq_made"))
                    q, b = qt[:, t, :], bank(g)
                    seq(dve.tensor_scalar(q[0:64], b[0:64, :], scaled[0:64, 4:5], None, ALU.mult))
                    seq(dve.scalar_tensor_tensor(T[2][64:96, :], b[96:128, :], scaled[96:128, 4:5],
                                                 tab[96:128, 0, :], ALU.mult, ALU.mult))
                    seq(dve.scalar_tensor_tensor(q[64:96], b[64:96, :], scaled[64:96, 4:5],
                                                 tab[64:96, 0, :], ALU.mult, ALU.mult))
                    dve.tensor_tensor(q[64:96], q[64:96], T[2][64:96, :], ALU.add)\
                        .then_inc(sem(f"bank_free{g % 4}"), 1)
                run(f"mla_q{half}", mla_q)

                def mla_k(t, g, off4, to):
                    dve.wait_ge(*c.next("hsq_made"))
                    seq(dve.tensor_copy(kt[64:96, t, :], pads[64:96, 3, 0:S]))
                    dve.tensor_scalar(kt[0:64, t, :], bank(g)[0:64, :], V("mla_k", 0, slice(0, 64)), None,
                                      ALU.mult).then_inc(sem(f"bank_free{g % 4}"), 1)
                run(f"mla_k{half}", mla_k)
                head_rows(8)
                if half == 0:
                    run("mla_v", nothing)
                for t in range(8):
                    dve.wait_ge(*c.next("spread"))
                    x = qt[0:MLA_D, t, :] if t < 4 else kt[0:MLA_D, t - 4, :]
                    dve.tensor_tensor(x, x, ps[6 + t % 2][0:MLA_D, :], ALU.mult).then_inc(sem("qk_made"), 1)
                attention(DEPTH + half)
            merge("gate_mla", "out_mla", True, False)

            def nsa_tile(t):
                return qt[:, t, :] if t < 4 else kt[:, t - 4, :]

            def nsa_in(t, g, off4, to):
                if t < 6:
                    dve.wait_ge(*c.next("hsq_made"))
                    gain = scaled[:, 5:6] if t < 4 else V("nsa_ks" if t == 4 else "nsa_kw")
                    dve.tensor_scalar(nsa_tile(t), bank(g)[:, :], gain, None, ALU.mult)\
                        .then_inc(sem(f"bank_free{g % 4}"), 1)
                    return
                dve.wait_ge(*tile_done(g))
                flat = windows(t - 6)
                name = "pos_k" if t == 6 else "pos_v"
                for grp in range(2):
                    r = slice(64 * grp, 64 * grp + 64)
                    for par in range(2):
                        dst = flat[64 * par:64 * par + 64].rearrange("p (l g n) -> p l g n", l=16, g=2)[:, :, grp, 0:CMP_N]
                        for lh in range(2):
                            tok = bank(g)[r, :].rearrange("p (n l two) -> p l n two", l=8, two=2)
                            src = tok[:, :, lh:lh + CMP_N, par]
                            at0 = VT[name][0]
                            pos = vecs[r, at0 + 16 * lh + par:at0 + 16 * lh + 16:2].unsqueeze(2)\
                                .to_broadcast([64, 8, CMP_N])
                            last = dve.tensor_tensor(dst[:, 8 * lh:8 * lh + 8, :], src, pos, ALU.add)
                last.then_inc(sem(f"bank_free{g % 4}"), 1)

            seq(dve.memset(pads[:, :, :], 0.0))
            run("nsa_in", nsa_in)
            head_rows(40)
            run("nsa_v", nothing)
            for t in range(6):
                x = nsa_tile(t)
                dve.wait_ge(*c.next("rotated"))
                seq(dve.tensor_tensor(T[2][:, :], ps[4 + t % 2][:, :], tab[:, 2, :], ALU.mult))
                seq(dve.tensor_tensor(x, x, tab[:, 1, :], ALU.mult))
                seq(dve.tensor_tensor(x, x, T[2][:, :], ALU.add))
                dve.wait_ge(*c.next("spread"))
                dve.tensor_tensor(x, x, ps[6 + t % 2][:, :], ALU.mult).then_inc(sem("qk_made"), 1)

            hid = T[3][0:64, 0:256]
            kc = kt[:, 2, P:P + CMP_N]

            def cmp(t, g, off4, to):
                if t % 2 == 0:
                    return
                dve.wait_ge(*tile_done(g))
                dve.wait_ge(*evacuated(g - 1))
                dve.tensor_tensor(T[1][0:64, 0:256], bank(g)[0:64, 0:256], T[0][0:64, 0:256], ALU.add)\
                    .then_inc(sem(f"bank_free{g % 4}"), 1)
                dve.wait_ge(*c.next("hid_tanh"))
                dve.scalar_tensor_tensor(hid, T[2][0:64, 0:256], 1.0, T[1][0:64, 0:256], ALU.add, ALU.mult)\
                    .then_inc(sem("hid_made"), 1)
                dve.wait_ge(*c.next("hid_turned"))
                dve.tensor_scalar(kt[:, 2, 0:P], ps[6][:, 0:P], 0.5, None, ALU.mult).then_inc(sem("hT_made"), 1)
                if t == 1:
                    dve.wait_ge(*c.next("kc_sq"))
                    dve.tensor_scalar(kt[:, 2, P:P + CMP_W], ps[7][:, 0:CMP_W], V("nsa_kc"), None, ALU.mult)\
                        .then_inc(sem("kc_gained"), 1)
                    dve.wait_ge(*c.next("kc_std"))
                    ends = slice(31, S, 16)
                    seq(dve.reciprocal(rows[:, 192:192 + CMP_N], rows[:, 128:128 + CMP_N]))
                    seq(dve.tensor_tensor(rows[:, 256:256 + CMP_N], ps[4][:, 0:CMP_N], tab[:, 2, ends], ALU.mult))
                    seq(dve.tensor_tensor(kc, kc, tab[:, 1, ends], ALU.mult))
                    seq(dve.tensor_tensor(kc, kc, rows[:, 256:256 + CMP_N], ALU.add))
                    dve.tensor_tensor(kc, kc, rows[:, 192:192 + CMP_N], ALU.mult).then_inc(sem("kc_made"), 1)
            run("cmp", cmp)
            attention(DEPTH + 2)
            g_gate = ST["gate_nsa"][1]
            gates_ready = lambda: dve.wait_ge(*evacuated(g_gate + 7))
            run("gate_nsa", nothing, loop=True)
            run("out_nsa", add_merged(False, True))
            run("w_out", add_h_times(16), loop=True)
            norm(lambda k: scaled[:, 16 + k:17 + k], shift=24)
            for ch, tiles in enumerate(CHUNKS_2):
                def up(t, g, off4, to):
                    if t % 2 == 0:
                        dve.wait_ge(*c.next("ff_tanh"))
                        dve.scalar_tensor_tensor(T[1][:, :], T[0][:, :], 1.0, bank(g)[:, :], ALU.add, ALU.mult)\
                            .then_inc(sem(f"bank_free{g % 4}"), 1)
                        dve.wait_ge(*evacuated(g, off4))
                    else:
                        u = t // 2
                        dve.wait_ge(*tile_done(g, off4))
                        dve.scalar_tensor_tensor(T[2][:, :], T[1][:, :], 0.5, bank(g)[:, :], ALU.mult, ALU.mult)\
                            .then_inc(sem("value_made"), 1)
                        if isinstance(to, int):
                            x_low(f_lo[:, u, :], T[2][:, :], f_hi[:, u, :], tile=(g, off4))
                        else:
                            dst = bass.ds(u + 2 * off4, 1)
                            x_low(f_lo[:, dst, :], T[2][:, :].unsqueeze(1), f_hi[:, dst, :],
                                  tile=(g, off4))
                run(f"ffn_up{ch}", up, loop=True, per={"ff_tanh": 2, "xhi_made": 2})
                run(f"ffn_down{ch}", add_h_times(40), loop=ch < 2)

        @block.tensor
        def _(pe):
            c = Counts()

            def products(dst, n, g, off4, pairs, last_signal=True):
                if g >= 4 or not isinstance(off4, int):
                    pe.wait_ge(sem(f"bank_free{g % 4}"), g // 4 + off4)
                total = 3 * len(pairs)
                done = 0
                for a, b in pairs:
                    for i, j in ((0, 0), (0, 1), (1, 0)):
                        ins = pe.matmul(dst, a[i], b[j], start=done == 0, stop=done == total - 1)
                        done += 1
                ins.then_inc(sem("tile_done"), 1)

            def weight(n, lo, hi):
                return w_hi[n % 2][:, lo:hi], w_lo[n % 2][:, lo:hi]

            def ready(n, off2=0):
                pe.wait_ge(sem("lo_made"), n + 1 + 2 * off2)

            def unit(n, g, x, kts, cols, off2=0, off4=0, m=P, tiles=None, k0=0):
                ready(n, off2)
                for j in range(cols // P if tiles is None else tiles):
                    pairs = [(weight(n, k * cols + j * P, k * cols + j * P + m),
                              (x[0][:, k0 + k, :], x[1][:, k0 + k, :])) for k in range(kts)]
                    products(bank(g + j)[0:m, :], n, g + j, off4, pairs)

            def unit_tokens(n, g, x, kts, cols, k0=0):
                ready(n)
                for t in range(QB):
                    pairs = [((x[0][:, k0 + k, t * P:(t + 1) * P], x[1][:, k0 + k, t * P:(t + 1) * P]),
                              weight(n, k * cols, (k + 1) * cols)) for k in range(kts)]
                    products(bank(g + t)[:, 0:cols], n, g + t, 0, pairs)

            A, Fx, Y = (a_hi, a_lo), (f_hi, f_lo), (y_hi, y_lo)

            def run(name, x, kts, cols, loop=False, after=None, tiles=None):
                n0, g0, units, tpu = ST[name]
                if not loop:
                    for u in range(units):
                        unit(n0 + u, g0 + u * tpu, x, kts, cols, tiles=tiles)
                        if after:
                            after(u)
                    return
                with pe.Fori(0, units // 2) as i:
                    for u in range(2):
                        unit(n0 + u, g0 + u * tpu, x, kts, cols, i, i * (tpu // 2))

            def inputs_ready(k):
                for _ in range(k):
                    at = c.next("x_made")
                pe.wait_ge(*at)

            def norm():
                for _ in range(KT - 1):
                    at = c.next("sq_added")
                pe.wait_ge(*at)
                pe.matmul(ps[7][:, :], C("ones"), pads[:, 0, 0:S], start=True, stop=True)\
                    .then_inc(sem("norm_summed"), 1)

            def sum_squares(dst, lhsT, rhs, start, stop):
                pe.wait_ge(*c.next("hsq_made"))
                pe.matmul(dst, lhsT, rhs, start=start, stop=stop).then_inc(sem("hsq_summed"), 1)

            def row64(r):
                return C("row64", lo=47 - r, hi=87 - r)

            def attention(which):
                steps, s0, m0 = ATTENTION[which], STEP0[which], MC[which]
                ns = len(steps[0]["sets"])
                diff = steps[0]["kind"] == "diff"
                local = Counts()

                def scores(s):
                    x = steps[s]
                    for j, (q, k) in enumerate(x["sets"]):
                        m = ns * s + j
                        if m >= 2:
                            pe.wait_ge(sem("exp_done"), m0 + m - 1)
                        pe.matmul(ps[4 + (m0 + m) % 2][:, 0:x["w"]], q, k, start=True, stop=True)\
                            .then_inc(sem("scores_made"), 1)

                def turn(s):
                    x = steps[s]
                    if s >= 1:
                        pe.wait_ge(*c.next("pT_made"))
                    pe.wait_ge(*c.next("att_made"))
                    p = probs(m0 + ns * s, diff)
                    if x["kind"] == "cmp":
                        ins = pe.transpose(ps[6][0:CMP_W, 0:P], p[:, 0:CMP_W], C("ident"))
                    else:
                        for j in range(x["w"] // P):
                            ins = pe.transpose(ps[6][:, j * P:(j + 1) * P], p[:, j * P:(j + 1) * P], C("ident"))
                    ins.then_inc(sem("pT_in_psum"), 1)

                def apply(s):
                    x = steps[s]
                    if s == len(steps) - 1:
                        pe.wait_ge(*c.next("pT_made"))
                    if x["opens"] and s > 0:
                        pe.wait_ge(*c.next("o_made" if diff else "x_made"))
                    n = len(x["values"])
                    for j, v in enumerate(x["values"]):
                        ins = pe.matmul(x["out"], v, pT[s % 2][0:x["rows"], j * P:(j + 1) * P],
                                        start=x["first"] and j == 0, stop=x["last"] and j == n - 1)
                    ins.then_inc(sem("pv_done"), 1)

                scores(0)
                for s in range(len(steps)):
                    if s + 1 < len(steps):
                        scores(s + 1)
                    turn(s)
                    if s >= 1:
                        apply(s - 1)
                apply(len(steps) - 1)

            pe.wait_ge(sem("lam_terms"), 1)
            pe.wait_ge(sem("consts_loaded"), 16)
            pe.matmul(ps[6][:, 0:4], C("ones"), small[:, 0:4], start=True, stop=True)\
                .then_inc(sem("lam_summed"), 1)

            for l in range(DEPTH):
                norm()
                inputs_ready(8)

                def sums(u):
                    if u >= 1:
                        for t in (2 * u - 2, 2 * u - 1):
                            sum_squares(ps[5][0:40, :], row64(2 * t if t < 4 else 32 + 2 * (t - 4)),
                                        T[t % 2][:, :], t == 0, t == 7)
                run(f"qk{l}", A, 8, 256, after=sums)
                sums(4)
                n, g, _, _ = ST[f"v{l}"]
                for u in range(2):
                    unit_tokens(n + u, g + 4 * u, A, 8, 256)
                pe.wait_ge(*c.next("hrows_made"))
                if l == 0:
                    pe.wait_ge(sem("spread_loaded"), 16)

                def spread_heads(tiles, rows_of):
                    for t in range(tiles):
                        if t >= 2:
                            pe.wait_ge(*c.next("qk_made"))
                        lhsT, rhs, dst = rows_of(t)
                        pe.matmul(dst, lhsT, rhs, start=True, stop=True).then_inc(sem("spread"), 1)

                def two_heads(t):
                    r0 = 0 if t < 4 else 32
                    j = t % 4
                    return tab[r0:r0 + 8, 0, j * P:(j + 1) * P], rows[r0:r0 + 8, :], ps[6 + t % 2][:, :]
                spread_heads(8, two_heads)
                c.next("qk_made")
                pe.wait_ge(*c.next("qk_made"))
                pe.wait_ge(*evacuated(g + 7))
                attention(l)
                run(f"pool_in{l}", A, 8, 256)
                pe.wait_ge(sem("small_loaded"), 16 * (l + 1))
                pe.wait_ge(*c.next("o_made"))
                for t in range(4):
                    pe.wait_ge(*c.next("pooled"))
                    if t >= 2:
                        pe.wait_ge(*c.next("x_made"))
                    pe.matmul(ps[6 + t % 2][:, :], wsmall[:, t * P:(t + 1) * P], T[t % 2][:, :],
                              start=True, stop=True).then_inc(sem("mixed"), 1)
                run(f"gate_a{l}", A, 8, 256, loop=True)
                inputs_ready(2)
                run(f"out_a{l}", Y, 4, 512)
                run(f"conv_in{l}", A, 8, 256)
                run(f"gate_b{l}", A, 8, 256, loop=True)
                inputs_ready(4)
                run(f"out_b{l}", Y, 4, 512)
                run(f"gate_c{l}", A, 8, 256, loop=True)
                for hd in range(4):
                    sum_squares(ps[5][0:4, :], C("row96", lo=15 - hd, hi=19 - hd), T[hd % 2][:, :], hd == 0, hd == 3)
                pe.wait_ge(*c.next("hrows_made"))
                for hd in range(4):
                    if hd >= 2:
                        pe.wait_ge(*c.next("x_made"))
                    pe.matmul(ps[6 + hd % 2][:, :], C("ident", slice(0, 4), hd, hd + 1).to_broadcast([4, P]),
                              rows[0:4, :], start=True, stop=True).then_inc(sem("spread"), 1)
                inputs_ready(2)
                run(f"out_c{l}", Y, 4, 512)
                inputs_ready(8)
                run(f"w_o{l}", A, 8, 256, loop=True)
                norm()
                inputs_ready(8)
                n0, g0, _, _ = ST[f"mlp{l}"]
                with pe.Fori(0, 4) as ch:
                    with pe.Fori(0, 2) as i:
                        for u in range(2):
                            unit(n0 + u, g0 + 2 * u, A, 8, 256, 4 * ch + i, 4 * ch + i)
                    with pe.Fori(0, 2) as i:
                        for u in range(2):
                            if u == 0:
                                pe.wait_ge(*evacuated(g0 + 7, 4 * ch))
                            unit(n0 + 4 + u, g0 + 8 + 2 * u, Fx, 8, 256, 4 * ch + i, 4 * ch + i)
                inputs_ready(2)
                run(f"ple_proj{l}", Y, 2, 1024)
                norm()
                inputs_ready(8)
                run(f"ple_gate{l}", A, 8, 256)

            with pe.Fori(0, 12) as i:
                for a in range(2):
                    pe.wait_ge(sem("ada_acc"), 2 * i + a + 1)
                    for m in range(2):
                        ins = pe.matmul(ps[6][:, bass.ds(4 * i + (2 * a + m), 1)], T[a][:, m * P:(m + 1) * P],
                                        C("ones", hi=1), start=True, stop=True)
                    ins.then_inc(sem("ada_summed"), 1)
            norm()
            inputs_ready(8)

            def lora_sums(u):
                if u >= 1:
                    for t in (2 * u - 2, 2 * u - 1):
                        sum_squares(ps[4 if t < 6 else 5][:, :], C("ones"), T[t % 2][:, :], t in (0, 6), t in (5, 7))
            run("lora", A, 8, 256, after=lora_sums)
            lora_sums(4)
            run("misc", A, 8, 128)
            pe.wait_ge(sem("g_tanh"), 1)
            for b in range(QB):
                ins = pe.transpose(ps[6][:, b * P:b * P + 24], T[0][0:24, b * P:(b + 1) * P],
                                   C("ident", slice(0, 24), 0, 24))
            ins.then_inc(sem("gt_in_psum"), 1)
            inputs_ready(8)

            def row96(j):
                return C("row96", slice(0, MLA_D), 15 - j, 23 - j)

            for half in range(2):
                n, g, _, _ = ST[f"mla_q{half}"]
                for u in range(2):
                    unit(n + u, g + 2 * u, Fx, 6, 256)
                    for t in (2 * u, 2 * u + 1):
                        sum_squares(ps[5][0:8, :], row96(t), T[t % 2][0:MLA_D, :], t == 0, False)
                n, g, _, _ = ST[f"mla_k{half}"]
                unit(n, g, Fx, 2, 512, k0=6)
                for t in range(4):
                    sum_squares(ps[5][0:8, :], row96(4 + t), T[t % 2][0:MLA_D, :], False, t == 3)
                if half == 0:
                    n, gv, _, _ = ST["mla_v"]
                    unit_tokens(n, gv, Fx, 2, 512, k0=6)
                pe.wait_ge(*c.next("hrows_made"))
                for t in range(8):
                    if t >= 2:
                        pe.wait_ge(*c.next("qk_made"))
                    pe.matmul(ps[6 + t % 2][0:MLA_D, :], C("ident", slice(0, 8), t, t + 1).to_broadcast([8, MLA_D]),
                              rows[0:8, :], start=True, stop=True).then_inc(sem("spread"), 1)
                c.next("qk_made")
                pe.wait_ge(*c.next("qk_made"))
                if half == 0:
                    pe.wait_ge(*evacuated(gv + 3))
                attention(DEPTH + half)
                if half == 0:
                    pe.wait_ge(*c.next("x_made"))
            run("gate_mla", A, 8, 256, loop=True)
            inputs_ready(1)
            run("out_mla", Y, 4, 512)

            def nsa_sums(u):
                if 1 <= u <= 3:
                    for t in (2 * u - 2, 2 * u - 1):
                        sum_squares(ps[5][0:40, :], row64(2 * t if t < 4 else 32 + 2 * (t - 4)),
                                    T[t % 2][:, :], t == 0, t == 5)
            run("nsa_in", A, 8, 256, after=nsa_sums)
            n, g, _, _ = ST["nsa_v"]
            unit_tokens(n, g, A, 8, 256)
            pe.wait_ge(*c.next("hrows_made"))
            for t in range(6):
                if t >= 2:
                    pe.wait_ge(*c.next("qk_made"))
                x = qt[:, t, :] if t < 4 else kt[:, t - 4, :]
                pe.matmul(ps[4 + t % 2][:, :], C("rot"), x, start=True, stop=True).then_inc(sem("rotated"), 1)
                lhsT, rhs, dst = two_heads(t)
                pe.matmul(dst, lhsT, rhs, start=True, stop=True).then_inc(sem("spread"), 1)
            c.next("qk_made")
            pe.wait_ge(*c.next("qk_made"))

            n0, g0, _, _ = ST["cmp"]
            for which in range(2):
                flat = windows(which)
                for part in range(2):
                    n, g = n0 + 2 * which + part, g0 + 2 * which + part
                    ready(n)
                    pe.wait_ge(sem(f"bank_free{g % 4}"), g // 4)
                    if which == 0 and part == 0:
                        pe.wait_ge(*evacuated(ST["nsa_in"][1] + 7))
                    for j in range(8):
                        lp = 8 * part + j
                        ins = pe.matmul(bank(g)[0:64, 0:256], flat[:, 64 * lp:64 * lp + 64],
                                        raw[n % 2][:, 256 * j:256 * j + 256], start=j == 0, stop=j == 7)
                    ins.then_inc(sem("tile_done"), 1)
                pe.wait_ge(*c.next("hid_made"))
                for k in range(2):
                    ins = pe.transpose(ps[6][:, 64 * k:64 * k + 64], T[3][0:64, k * P:(k + 1) * P],
                                       C("ident", slice(0, 64), 0, 64))
                ins.then_inc(sem("hid_turned"), 1)
                pe.wait_ge(*c.next("hT_made"))
                if which == 0:
                    for grp in range(2):
                        for k in range(2):
                            ins = pe.matmul(ps[7][64 * grp:64 * grp + 64, 0:CMP_W],
                                            wsmall[:, 64 * k:64 * k + 64],
                                            kt[:, 2, 64 * k + 32 * grp:64 * k + 32 * grp + CMP_W],
                                            start=k == 0, stop=k == 1)
                    ins.then_inc(sem("kc_in_psum"), 1)
                    pe.wait_ge(*c.next("kc_gained"))
                    pe.matmul(ps[4][:, 0:CMP_N], C("rot"), kt[:, 2, P:P + CMP_N], start=True, stop=True)
                    pe.matmul(ps[5][:, 0:CMP_N], C("blocks"), rows[:, 64:64 + CMP_N], start=True, stop=True)\
                        .then_inc(sem("kc_summed"), 1)
                    pe.wait_ge(*c.next("kc_made"))
                else:
                    for grp in range(2):
                        for k in range(2):
                            ins = pe.matmul(ps[7][0:CMP_W, 64 * grp:64 * grp + 64],
                                            kt[:, 2, 64 * k + 32 * grp:64 * k + 32 * grp + CMP_W],
                                            wsmall[:, P + 64 * k:P + 64 * k + 64], start=k == 0, stop=k == 1)
                    ins.then_inc(sem("vc_in_psum"), 1)
                    pe.wait_ge(sem("vc_made"), 1)
            attention(DEPTH + 2)
            run("gate_nsa", A, 8, 256, loop=True)
            inputs_ready(1)
            run("out_nsa", Y, 4, 512)
            inputs_ready(8)
            run("w_out", A, 8, 256, loop=True)
            norm()
            inputs_ready(8)
            for ch, tiles in enumerate(CHUNKS_2):
                run(f"ffn_up{ch}", A, 8, 256, loop=True)
                pe.wait_ge(*evacuated(ST[f"ffn_up{ch}"][1] + 2 * tiles - 1))
                run(f"ffn_down{ch}", Fx, tiles, 256, loop=ch < 2)


def feature_units(w, kts, cols):
    K, N = w.shape
    assert K == kts * P and N % cols == 0
    u = w.reshape(kts, P, N // cols, cols).transpose(2, 1, 0, 3).reshape(N // cols, P, kts * cols)
    return pad_units(u)


def pad_units(u):
    if u.shape[2] == UNIT:
        return u
    out = np.zeros((u.shape[0], P, UNIT), np.float32)
    out[:, :, :u.shape[2]] = u
    return out


def lay_out(a):
    f = lambda name: np.asarray(a[name])
    zero = lambda *s: np.zeros(s, np.float32)
    units = []
    for l in range(DEPTH):
        w = f("w_in")[l]
        part = lambda i: w[:, 512 * i:512 * (i + 1)]
        gates = w[:, 3584:]
        conv = np.concatenate([part(i)[:, P * j:P * (j + 1)] for j in range(4) for i in (2, 1, 3)], 1)
        out_units = lambda m: pad_units(m.reshape(4, P, 2, 512).transpose(2, 1, 0, 3).reshape(2, P, UNIT))
        units += [feature_units(np.concatenate([part(4), part(5)], 1), 8, 256), feature_units(part(6), 8, 256),
                  feature_units(part(0), 8, 256), feature_units(gates[:, :1024], 8, 256),
                  out_units(f("w_pool_out")[l]), feature_units(conv, 8, 256),
                  feature_units(gates[:, 1024:2048], 8, 256), out_units(f("w_conv_out")[l]),
                  feature_units(gates[:, 2048:], 8, 256), out_units(f("w_attn_out")[l]),
                  feature_units(f("w_o")[l], 8, 256)]
        for ch in range(4):
            units += [feature_units(f("w_up")[l][:, 1024 * ch:1024 * (ch + 1)], 8, 256),
                      feature_units(f("w_down")[l][1024 * ch:1024 * (ch + 1)], 8, 256)]
        units += [feature_units(f("w_ple_proj")[l], 2, 1024), feature_units(f("w_ple_gate")[l], 8, 256)]
    w = f("w_in_2")[0]
    sizes = (768, 256, 32, 512, 128, 128, 128, 128, 128, 128, 24, 1024, 1024)
    cut = np.split(w, np.cumsum(sizes)[:-1], axis=1)
    c_q, c_kv, k_pe, q_n, k_c, v_c, k_s, v_s, k_w, v_w, g_n, g_mla, g_nsa = cut
    swap = lambda m: np.concatenate([m[..., 16:32], m[..., 0:16]], -1)
    misc = np.concatenate([g_n, zero(D, 40), k_pe, swap(k_pe)], 1)
    q_pairs = q_n.reshape(D, 2, 4, 64).transpose(0, 2, 1, 3).reshape(D, 512)
    q_b = f("mla_w_q_b_2")[0].reshape(768, 8, MLA_D)
    q_b = np.concatenate([q_b, swap(q_b[..., 64:])], -1).reshape(768, 8 * P)
    kv_b = f("mla_w_kv_b_2")[0].reshape(256, 8, P)
    k_b = np.concatenate([kv_b[..., :64], zero(256, 8, 64)], -1).reshape(256, 8 * P)
    v_b = kv_b[..., 64:].reshape(256, 512)
    units += [feature_units(np.concatenate([c_q, c_kv], 1), 8, 256), feature_units(misc, 8, P)]
    for half in range(2):
        units += [feature_units(q_b[:, 512 * half:512 * (half + 1)], 6, 256),
                  feature_units(k_b[:, 512 * half:512 * (half + 1)], 2, 512)]
        if half == 0:
            units += [feature_units(v_b, 2, 512)]
    out_units = lambda m: pad_units(m.reshape(4, P, 2, 512).transpose(2, 1, 0, 3).reshape(2, P, UNIT))
    o_nsa = f("w_o_nsa_2")[0].reshape(2, 4, 64, D).transpose(1, 0, 2, 3).reshape(512, D)
    cmp1 = [f(n)[0].reshape(2, 8, P, 256).transpose(0, 2, 1, 3).reshape(2, P, UNIT)
            for n in ("cmp_w1_k_2", "cmp_w1_v_2")]
    units += [feature_units(g_mla, 8, 256), out_units(f("w_o_mla_2")[0]),
              feature_units(np.concatenate([q_pairs, k_s, k_w, k_c, v_c], 1), 8, 256),
              feature_units(np.concatenate([v_s, v_w], 1), 8, 256)] + cmp1
    units += [feature_units(g_nsa, 8, 256), out_units(o_nsa), feature_units(f("w_out_2")[0], 8, 256)]
    at = 0
    for tiles in CHUNKS_2:
        n = P * tiles
        pair = np.stack([f(m)[0][:, at:at + n].reshape(D, tiles, P) for m in ("ffn_w_gate_2", "ffn_w_up_2")], 2)
        units += [feature_units(pair.reshape(D, 2 * n), 8, 256),
                  feature_units(f("ffn_w_down_2")[0][at:at + n], tiles, 256)]
        at += n
    weights = np.concatenate(units, 0)
    ada = feature_units(f("ada_w_2")[0], 8, 256)

    cols = {}
    tall = lambda v: v.reshape(-1, P).T
    twice = lambda v: np.concatenate([v, v])[:, None]
    for l in range(DEPTH):
        cols[f"mix{l}"] = tall(f("norm_mix_g")[l])
        cols[f"pool_scale{l}"] = tall(f("pool_scale")[l])
        cols[f"conv{l}"] = tall(f("conv_w")[l].reshape(-1))
        cols[f"qg{l}"], cols[f"kg{l}"] = twice(f("q_norm_g")[l]), twice(f("k_norm_g")[l])
        lam = np.stack([f(n)[l] for n in ("lam_q1", "lam_k1", "lam_q2", "lam_k2")], 1)
        cols[f"lam{l}"] = np.concatenate([lam, zero(64, 4)], 0)
        cols[f"sub{l}"] = f("sub_norm_g")[l][:, None]
        cols[f"mlp{l}"], cols[f"ple{l}"] = tall(f("norm_mlp_g")[l]), tall(f("norm_ple_g")[l])
    cols["n1"], cols["n2"] = tall(f("norm1_gain_2")[0]), tall(f("norm2_gain_2")[0])
    cols["ada_b"], cols["c"] = tall(f("ada_b_2")[0]), tall(f("c_2")[0])
    cols["q_a"], cols["kv_a"] = tall(f("mla_q_a_gain_2")[0]), tall(f("mla_kv_a_gain_2")[0])
    for name, key in (("mla_q", "mla_q_gain_2"), ("mla_k", "mla_k_gain_2")):
        g = f(key)[0]
        cols[name] = np.concatenate([g, swap(g[64:])])[:, None]
    for name in ("q", "kc", "ks", "kw"):
        cols["nsa_" + name] = twice(f(f"nsa_{name}_gain_2")[0])
    for name in ("k", "v"):
        t = f(f"cmp_pos_{name}_2")[0].T
        cols["pos_" + name] = np.concatenate([t, t], 0)
    table, width = vec_table()
    vecs = zero(P, width)
    for name, (at, n) in table.items():
        vecs[:, at:at + n] = cols[name]
    w2 = np.concatenate([f(n)[0].reshape(2, P, 64).transpose(1, 0, 2).reshape(P, P)
                         for n in ("cmp_w2_k_2", "cmp_w2_v_2")], 1)
    return dict(
        weights=weights, ada=ada, vecs=vecs, cmp_w2=w2,
        x_t=f("x")[0].T.reshape(KT, P, S).transpose(1, 0, 2),
        p_t=f("p")[:, 0].transpose(0, 2, 1).reshape(DEPTH, 2, P, S).transpose(0, 2, 1, 3),
        pool_w=f("pool_w").transpose(0, 2, 1, 3).reshape(DEPTH, P, 4 * P),
        positions=f("positions_2").astype(np.int32))


def constants():
    table, width = const_table()
    c = {name: np.zeros((P, n), np.float64) for name, (_, n) in table.items()}
    i, j = np.arange(P)[:, None], np.arange(P)[None]
    c["ident"] = i == j
    c["ones"][:] = 1
    c["blocks"] = i // 64 == j // 64
    c["row96"][:, 15] = 1
    c["row64"][:64, 47] = 1
    c["row64"][64:, 48] = 1
    c["causal"] = np.where(j > i, NEG, 0)
    c["far"] = np.where(j <= i, NEG, 0)
    for b in range(QB):
        n = np.arange(CMP_W)[None]
        ok = (16 * n + 31 <= b * P + i) & (n < CMP_N)
        c["cmp_mask"][:, b * CMP_W:(b + 1) * CMP_W] = np.where(ok, 0, NEG)
        c["cmp_valid"][:, b * CMP_W:(b + 1) * CMP_W] = ok
    c["inv_count"][:] = 1.0 / np.arange(1, 17)
    inv = lambda dim: 500000.0 ** (-np.arange(0, dim, 2) / dim)
    c["freq_mla"][64:, 0] = np.tile(inv(32), 4)
    for half in (0, 64):
        c["freq_nsa"][half:half + 16, 0] = np.tile(inv(16), 2)
        for d in range(8):
            c["rot"][half + d + 8, half + d] = -1
            c["rot"][half + d, half + d + 8] = 1
    c["phase_mla"][64:96, 0] = 0.25
    c["phase_mla"][96:112, 0] = 0.5
    c["eps"][:] = EPS
    out = np.zeros((P, width), np.float32)
    for name, (at, n) in table.items():
        out[:, at:at + n] = c[name]
    spread = np.zeros((40, 4, 2, 64), np.float32)
    for t in range(4):
        for k in range(2):
            spread[2 * t + k, t, k] = spread[32 + 2 * t + k, t, k] = 1
    return out, spread.reshape(40, S)


def kernel(**inputs):
    import concourse.bacc as bacc
    from concourse.bass_utils import run_bass_kernel_spmd

    arrays = lay_out(inputs)
    arrays["consts"], arrays["spread"] = constants()
    arrays = {k: np.ascontiguousarray(v) for k, v in arrays.items()}
    nc = bacc.Bacc("TRN2", target_bir_lowering=False, num_devices=1)
    d = {k: nc.dram_tensor(k, v.shape, mybir.dt.from_np(v.dtype), kind="ExternalInput").ap()
         for k, v in arrays.items()}
    out = nc.dram_tensor("out", (KT, P, S), mybir.dt.float32, kind="ExternalOutput").ap()
    program(nc, d["weights"], d["ada"], d["vecs"], d["consts"], d["spread"], d["x_t"], d["p_t"],
            d["pool_w"], d["cmp_w2"], d["positions"], out)
    r = run_bass_kernel_spmd(nc, [arrays], core_ids=[0])
    return np.ascontiguousarray(r.results[0]["out"].reshape(D, S).T)[None]
```

```python
import math
from contextlib import ExitStack

import numpy as np
import concourse.bass as bass
from concourse import mybir

P = 128
S = 512
D = 1024
KT = D // P
DEPTH = 2
QB = S // P
UNIT = 2048
NEG = -1e30
EPS = 1e-6
CMP_N, CMP_W = 31, 32
WINDOWS = (2, 4, 8, 16)
MLA_D = 96
PAD = 16
ROW = PAD + S
CHUNKS_2 = (8, 8, 6)
MAGIC = 12582912.0


def stages():
    out = []
    for l in range(DEPTH):
        out += [(f"qk{l}", 4, 2), (f"v{l}", 2, 4), (f"conv_in{l}", 6, 2), (f"gate_b{l}", 4, 2),
                (f"out_b{l}", 2, 4), (f"pool_in{l}", 2, 2), (f"gate_a{l}", 4, 2), (f"out_a{l}", 2, 4),
                (f"gate_c{l}", 4, 2), (f"out_c{l}", 2, 4), (f"w_o{l}", 4, 2), (f"mlp{l}", 32, 2),
                (f"ple_proj{l}", 1, 8), (f"ple_gate{l}", 4, 2)]
    out += [("lora", 4, 2), ("misc", 1, 1)]
    for half in range(2):
        out += [(f"mla_q{half}", 2, 2), (f"mla_k{half}", 1, 4)] + [("mla_v", 1, 4)] * (half == 0)
    out += [("gate_mla", 4, 2), ("out_mla", 2, 4), ("nsa_in", 4, 2), ("nsa_v", 1, 4), ("cmp0", 2, 1),
            ("gate_nsa0", 1, 2), ("cmp1", 2, 1), ("gate_nsa1", 1, 2), ("gate_nsa2", 2, 2),
            ("out_nsa", 2, 4), ("w_out", 4, 2)]
    for c, tiles in enumerate(CHUNKS_2):
        out += [(f"ffn_up{c}", tiles, 2), (f"ffn_down{c}", 4, 2)]
    return out


def stream_table():
    table, n, g = {}, 0, 0
    for name, units, tiles in stages():
        table[name] = (n, g, units, tiles)
        n, g = n + units, g + units * tiles
    return table, n


def columns(widths):
    table, at = {}, 0
    for name, width in widths:
        table[name] = (at, width)
        at += width
    return table, at


def vec_table():
    w = []
    for l in range(DEPTH):
        w += [(f"mix{l}", 8), (f"pool_scale{l}", 4), (f"conv{l}", 12), (f"qg{l}", 1), (f"kg{l}", 1),
              (f"lam{l}", 4), (f"sub{l}", 1), (f"mlp{l}", 8), (f"ple{l}", 8)]
    w += [("n1", 8), ("n2", 8), ("ada_b", 48), ("c", 8), ("q_a", 6), ("kv_a", 2), ("mla_q", 1),
          ("mla_k", 1), ("nsa_q", 1), ("nsa_kc", 1), ("nsa_ks", 1), ("nsa_kw", 1), ("pos_k", 32),
          ("pos_v", 32)]
    return columns(w)


def const_table():
    return columns([("ident", P), ("ones", P), ("blocks", P), ("row96", 31), ("row64", 88),
                    ("causal", P), ("far", P), ("cmp_mask", QB * CMP_W), ("cmp_valid", QB * CMP_W),
                    ("inv_count", 16), ("freq_mla", 1), ("freq_nsa", 1), ("phase_mla", 1),
                    ("rot", P), ("eps", 1)])


def program(nc, weights, ada, vecs_d, consts_d, spread_d, x_t, p_t, pool_w, cmp_w2, positions, out):
    F32, F32R, I32 = mybir.dt.float32, mybir.dt.float32r, mybir.dt.int32
    ALU, ACT, AX = mybir.AluOpType, mybir.ActivationFunctionType, mybir.AxisListType
    ST, NU = stream_table()
    VT, NV = vec_table()
    CT, NCOL = const_table()
    ctx = ExitStack()
    with ctx:
        def sb(name, shape, dt=F32):
            return ctx.enter_context(nc.sbuf_tensor(name, shape, dt))

        raw = [sb(f"raw{i}", [P, UNIT]) for i in range(2)]
        w_hi = [sb(f"w_hi{i}", [P, UNIT], F32R) for i in range(2)]
        w_lo = [sb(f"w_lo{i}", [P, UNIT], F32R) for i in range(2)]
        h = sb("h", [P, KT, S])
        a_hi = sb("a_hi", [P, KT, S], F32R)
        a_lo = sb("a_lo", [P, KT, S], F32R)
        with ExitStack() as place:
            gate = place.enter_context(nc.sbuf_tensor("gate", [P, KT, S], F32))
            merged = place.enter_context(nc.sbuf_tensor("merged", [P, KT, S], F32))
        f_hi = sb("f_hi", [P, KT, S], F32R)
        f_lo = sb("f_lo", [P, KT, S], F32R)
        y_hi = sb("y_hi", [P, 4, S], F32R)
        y_lo = sb("y_lo", [P, 4, S], F32R)
        with ExitStack() as place:
            lora = place.enter_context(nc.sbuf_tensor("lora", [P, KT, S], F32))
        with ExitStack() as place:
            ada_w = place.enter_context(nc.sbuf_tensor("ada_w", [P, UNIT], F32))
        qt = sb("qt", [P, 4, S])
        kt = sb("kt", [P, 4, S])
        vt = sb("vt", [P, 4, S])
        pads = sb("pads", [P, 4, ROW])
        pT = [sb(f"pT{i}", [P, S]) for i in range(2)]
        T = [sb(f"T{i}", [P, S]) for i in range(4)]
        tab = sb("tab", [P, 3, S])
        consts = sb("consts_sb", [P, NCOL])
        vecs = sb("vecs_sb", [P, NV])
        rows = sb("rows", [P, S])
        wsmall = sb("wsmall", [P, S])
        mod = sb("mod", [P, 48])
        scaled = sb("scaled", [P, 24])
        neg_lam = sb("neg_lam", [P, 2])
        small = sb("small", [P, 28])
        gt = sb("gt", [P, QB, 24])

        ps = [ctx.enter_context(nc.psum_tensor(f"ps{i}", [P, S], F32)) for i in range(8)]

        sems = {}

        def sem(name):
            if name not in sems:
                sems[name] = ctx.enter_context(nc.semaphore(name))
            return sems[name]

        def V(name, k=0, r=slice(0, P)):
            at, _ = VT[name]
            return vecs[r, at + k:at + k + 1]

        def V_range(name):
            at, width = VT[name]
            return vecs[:, at:at + width]

        def windows(which):
            return pads[:, 2 * which:2 * which + 2, :].rearrange("p a n -> p (a n)")[:, 0:16 * 64]

        def C(name, r=slice(0, P), lo=0, hi=None):
            at, width = CT[name]
            return consts[r, at + lo:at + (width if hi is None else hi)]

        class Counts:

            def __init__(self):
                self.n, self.open = {}, []

            def next(self, name):
                self.n[name] = self.n.get(name, 0) + 1
                value = self.n[name]
                for i, per, _ in self.open:
                    value = value + i * per[name]
                return sem(name), value

            def enter(self, i, per):
                self.open.append((i, per, dict(self.n)))

            def leave(self, turns):
                _, per, before = self.open.pop()
                for name in set(self.n) | set(per):
                    assert self.n.get(name, 0) - before.get(name, 0) == per.get(name, 0), name
                    self.n[name] = before.get(name, 0) + turns * per.get(name, 0)


        def loaded(n, off2=0):
            return sem(f"loaded{n % 2}"), 16 * (n // 2 + 1) + 16 * off2

        def tile_done(g, off4=0):
            return sem("tile_done"), g + 1 + 4 * off4

        def evacuated(g, off4=0):
            return sem(f"bank_free{g % 4}"), g // 4 + 1 + off4

        def bank(g):
            return ps[g % 4]

        def ada_index(l, down, ch, i):
            if l == 0:
                return 4 * ch + i + (2 if down else 0)
            return None if down else 2 * ch + i + 16


        def diff_steps():
            out = []
            for hd in range(4):
                for b in range(QB):
                    w = (b + 1) * P
                    out.append(dict(
                        kind="diff", w=w, rows=P, masks=(),
                        sets=[(qt[64 * c:64 * c + 64, hd, b * P:(b + 1) * P],
                               kt[64 * c:64 * c + 64, hd, 0:w]) for c in range(2)],
                        values=[vt[:, j, hd * P:(hd + 1) * P] for j in range(b + 1)],
                        out=ps[7][:, b * P:(b + 1) * P], first=True, last=True,
                        opens=b == 0, closes=b == QB - 1, tile=hd))
            return out

        def mla_steps(half):
            out = []
            for i in range(4):
                for b in range(QB):
                    w = (b + 1) * P
                    r, hd = 64 * (i % 2), 4 * half + i
                    out.append(dict(
                        kind="plain", w=w, rows=P, masks=((w - P, C("causal")),),
                        sets=[(qt[0:MLA_D, i, b * P:(b + 1) * P], kt[0:MLA_D, i, 0:w])],
                        values=[vt[:, j, hd * 64:(hd + 1) * 64] for j in range(b + 1)],
                        out=ps[7][r:r + 64, b * P:(b + 1) * P], first=True, last=True,
                        opens=b == 0 and i % 2 == 0, closes=b == QB - 1 and i % 2 == 1,
                        tile=2 * half + i // 2))
            return out

        def nsa_steps():
            out = []
            for t in range(4):
                for g in range(2):
                    r, hd = slice(64 * g, 64 * g + 64), t + 4 * g
                    for b in range(QB):
                        q = qt[r, t, b * P:(b + 1) * P]
                        o = ps[7][r, b * P:(b + 1) * P]
                        k0, w = max(0, b - 2), (b + 1) * P
                        n = w - k0 * P
                        base = dict(out=o, tile=t)
                        out.append(dict(
                            kind="cmp", w=CMP_W, rows=CMP_W,
                            masks=((0, C("cmp_mask", lo=b * CMP_W, hi=(b + 1) * CMP_W)),),
                            gate=gt[:, b, 3 * hd:3 * hd + 1],
                            sets=[(q, kt[r, 2, P:P + CMP_W])],
                            values=[kt[0:CMP_W, 2, 256 + 64 * g:256 + 64 * g + 64]],
                            first=True, last=False, opens=b == 0 and g == 0, closes=False, **base))
                        out.append(dict(
                            kind="plain", w=w, rows=P, masks=((w - P, C("causal")),),
                            gate=gt[:, b, 3 * hd + 1:3 * hd + 2],
                            sets=[(q, kt[r, 0, 0:w])],
                            values=[vt[:, j, 64 * g:64 * g + 64] for j in range(b + 1)],
                            first=False, last=False, opens=False, closes=False, **base))
                        out.append(dict(
                            kind="plain", w=n, rows=P,
                            masks=((n - P, C("causal")),) + (((0, C("far")),) if b >= 2 else ()),
                            gate=gt[:, b, 3 * hd + 2:3 * hd + 3],
                            sets=[(q, kt[r, 1, k0 * P:w])],
                            values=[vt[:, j, P + 64 * g:P + 64 * g + 64] for j in range(k0, b + 1)],
                            first=False, last=True, opens=False, closes=b == QB - 1 and g == 1, **base))
            return out

        ATTENTION = [diff_steps()] * DEPTH + [mla_steps(0), mla_steps(1), nsa_steps()]
        STEP0 = [sum(len(a) for a in ATTENTION[:i]) for i in range(len(ATTENTION) + 1)]
        MC = [sum(len(x["sets"]) for a in ATTENTION[:i] for x in a) for i in range(len(ATTENTION) + 1)]

        ALONG = {DEPTH + 1: ("gate_mla", 0), DEPTH + 2: ("gate_nsa2", 4)}

        def pieces(which):
            n = len(ATTENTION[which])
            if which not in ALONG:
                return [[] for _ in range(n)]
            _, _, units, tiles = ST[ALONG[which][0]]
            every = [(u, j, k) for u in range(units) for j in range(tiles) for k in range(KT)]
            at = [len(every) * i // (n - 1) for i in range(n)]
            return [every[at[i]:at[i + 1]] for i in range(n - 1)] + [[]]

        def probs(m, diff):
            return pads[:, m % (4 if diff else 2), 0:S]

        def score_bank(m, diff):
            return ps[(4, 5, 2, 3)[m % 4]] if diff else ps[4 + m % 2]

        block = ctx.enter_context(nc.Block())

        @block.sync
        def _(sp):
            for k in range(0, KT, 2):
                sp.dma_start(h[:, k:k + 2, :], x_t[:, k:k + 2, :]).then_inc(sem(f"h_loaded{k}"), 16)
            sp.dma_start(vecs[:, :], vecs_d).then_inc(sem("vecs_loaded"), 16)
            sp.dma_start(raw[0][:, :], weights[0]).then_inc(sem("loaded0"), 16)
            sp.dma_start(consts[:, :], consts_d).then_inc(sem("consts_loaded"), 16)
            sp.dma_start(raw[1][:, :], weights[1]).then_inc(sem("loaded1"), 16)
            sp.dma_start(tab[0:40, 0, :], spread_d).then_inc(sem("spread_loaded"), 16)

            def unit(n, off2=0):
                sp.wait_ge(sem("lo_made"), n - 1 + 2 * off2)
                src = weights[n] if isinstance(off2, int) else weights[n + 2 * off2]
                sp.dma_start(raw[n % 2][:, :], src).then_inc(*inc(loaded(n)))

            def inc(x):
                return x[0], 16

            def loop(a, b):
                if (b - a) % 2:
                    unit(a)
                    a += 1
                if a == b:
                    return
                with sp.Fori(0, (b - a) // 2) as i:
                    for s in range(2):
                        unit(a + s, i)

            at = 2
            for stage in ("cmp0", "cmp1"):
                n0, g0, units, _ = ST[stage]
                if at < n0 + 2:
                    loop(at, n0 + 2)
                for j in range(units):
                    sp.wait_ge(*tile_done(g0 + j))
                    unit(n0 + 2 + j)
                at = n0 + 2 + units
            loop(at, NU)
            g_last = ST["ffn_down2"][1]
            for t in range(KT):
                sp.wait_ge(*evacuated(g_last + t))
                sp.dma_start(out[t], h[:, t, :]).then_inc(sem("stored"), 16)
            sp.wait_ge(sem("stored"), 16 * KT)

        @block.gpsimd
        def _(pool):
            c = Counts()

            def seq(ins):
                ins.then_inc(sem("pool_seq"), 1)
                pool.wait_ge(*c.next("pool_seq"))

            pos, turn, ang, t0, t1 = (merged[:, i, :] for i in range(5))
            hi, lo = merged[:, 5, :], merged[:, 6, :]
            posi = merged[:, 7, :].bitcast(I32)
            pool.dma_start(posi, positions.to_broadcast([P, S])).then_inc(sem("pos_loaded"), 16)
            pool.wait_ge(sem("pos_loaded"), 16)
            pool.wait_ge(sem("consts_loaded"), 16)
            seq(pool.tensor_copy(pos, posi))

            def wrap(x, r, y):
                seq(pool.tensor_scalar(r, x, MAGIC, None, ALU.add))
                seq(pool.tensor_scalar(r, r, MAGIC, None, ALU.subtract))
                seq(pool.tensor_tensor(y, x, r, ALU.subtract))

            digits = 15915494309189533576888376337251436203445964574046 * 2 ** 80 // 10 ** 50
            parts = [float(digits >> (66 - 12 * k) & 4095) / 2.0 ** (14 + 12 * k) for k in range(5)]
            for which, freq in ((0, "freq_mla"), (1, "freq_nsa")):
                seq(pool.tensor_scalar(ang, pos, C(freq), None, ALU.mult))
                seq(pool.tensor_scalar(t0, ang, 4097.0, None, ALU.mult))
                seq(pool.tensor_tensor(t1, t0, ang, ALU.subtract))
                seq(pool.tensor_tensor(hi, t0, t1, ALU.subtract))
                seq(pool.tensor_tensor(lo, ang, hi, ALU.subtract))
                first = True
                for half, k in ((hi, 5), (lo, 4)):
                    for part in parts[:k]:
                        seq(pool.tensor_scalar(t0, half, part, None, ALU.mult))
                        wrap(t0, t1, turn if first else t0)
                        if not first:
                            seq(pool.tensor_tensor(turn, turn, t0, ALU.add))
                        first = False
                for table in ((0,) if which == 0 else (1, 2)):
                    shift = C("phase_mla") if table == 0 else (0.25 if table == 1 else 0.0)
                    r = slice(64, P) if table == 0 else slice(0, P)
                    if table == 0:
                        shift = C("phase_mla", r)
                    seq(pool.tensor_scalar(t0[r], turn[r], shift, None, ALU.add))
                    seq(pool.tensor_scalar(t1[r], t0[r], MAGIC, None, ALU.add))
                    seq(pool.tensor_scalar(t1[r], t1[r], MAGIC, None, ALU.subtract))
                    pool.tensor_tensor(tab[r, table, :], t0[r], t1[r], ALU.subtract)\
                        .then_inc(sem("turns_made"), 1)
                    pool.wait_ge(sem("turns_made"), {0: 1, 1: 2, 2: 3}[table])

        @block.scalar
        def _(act):
            c = Counts()

            def split(n, g, off2=0, off4=0):
                if n >= NU:
                    return
                act.wait_ge(*loaded(n, off2))
                if n >= 2:
                    act.wait_ge(*tile_done(g - 1, off4))
                act.activation(w_hi[n % 2][:, :], raw[n % 2][:, :], ACT.Copy).then_inc(sem("hi_made"), 1)

            def x_high(dst, src, **kw):
                act.wait_ge(*c.next("value_made"))
                act.activation(dst, src, kw.pop("func", ACT.Copy), **kw).then_inc(sem("xhi_made"), 1)

            def run(name, tile, per=None, loop=False, first=0, last=None):
                n0, g0, units, tpu = ST[name]
                last = units if last is None else last

                def body(u, off2, off4):
                    n, g = n0 + u, g0 + u * tpu
                    split(n + 1, g, off2, off4)
                    for j in range(tpu):
                        tile(u * tpu + j, g + j, off4, 4 * off4 if not isinstance(off4, int) else 0)

                if not loop:
                    for u in range(first, last):
                        body(u, 0, 0)
                    return
                with act.Fori(0, units // 2) as i:
                    c.enter(i, per or {})
                    for u in range(2):
                        body(u, i, i * (tpu // 2))
                    c.leave(units // 2)

            norms = 0

            def square(k, *ready):
                act.wait_ge(*ready)
                if k >= 2:
                    act.wait_ge(sem("sq_added"), 7 * norms + max(1, k - 2))
                act.activation(pT[k % 2][:, :], h[:, k, :], ACT.Square).then_inc(sem("sq_made"), 1)

            def norm_std():
                nonlocal norms
                norms += 1
                act.wait_ge(*c.next("norm_summed"))
                act.activation(small[:, 16:20], ps[7][:, 0:QB], ACT.Sqrt, scale=1.0 / D, bias=C("eps"))\
                    .then_inc(sem("std_made"), 1)

            def norm_high(shift=None):
                for k in range(KT):
                    if shift is None:
                        x_high(a_hi[:, k, :], T[2 + k % 2][:, :])
                    else:
                        x_high(a_hi[:, k, :], T[2 + k % 2][:, :], func=ACT.Identity,
                               bias=mod[:, shift + k:shift + k + 1])

            def head_squares(t, g, r=slice(0, P)):
                act.wait_ge(*tile_done(g))
                if t >= 2:
                    act.wait_ge(*c.next("hsq_summed"))
                act.activation(T[t % 2][r], bank(g)[r], ACT.Square).then_inc(sem("hsq_made"), 1)

            def head_std(n_rows, width, pending=2):
                for _ in range(pending):
                    at = c.next("hsq_summed")
                act.wait_ge(*at)
                act.activation(rows[0:n_rows, :], ps[5][0:n_rows, :], ACT.Sqrt, scale=1.0 / width,
                               bias=C("eps", slice(0, n_rows))).then_inc(sem("hstd_made"), 1)

            def attention(which):
                steps, s0, m = ATTENTION[which], STEP0[which], MC[which]
                diff = steps[0]["kind"] == "diff"
                along, plan = ALONG.get(which), pieces(which)
                n0, g0, _, tpu = ST[along[0]] if along else (0, 0, 0, 0)
                for s in range(len(steps) + 2):
                    if s < len(steps):
                        x = steps[s]
                        for j in range(len(x["sets"])):
                            act.wait_ge(*c.next("max_made"))
                            k = 2 * (s % 2) + j
                            act.activation(probs(m, diff)[:, 0:x["w"]], score_bank(m, diff)[:, 0:x["w"]], ACT.Exp,
                                           bias=small[:, k:k + 1], scale=1.0,
                                           accum_out=small[:, 4 + k:5 + k]).then_inc(sem("exp_done"), 1)
                            m += 1
                    if s >= 2 and steps[s - 2]["closes"] and not diff:
                        act.wait_ge(sem("pv_done"), s0 + s - 1)
                        act.activation(y_hi[:, steps[s - 2]["tile"], :], ps[7][:, :], ACT.Copy)\
                            .then_inc(sem("xhi_made"), 1)
                    if 1 <= s <= len(steps):
                        x = steps[s - 1]
                        act.wait_ge(*c.next("pT_in_psum"))
                        if s0 + s - 1 >= 2:
                            act.wait_ge(sem("pv_done"), s0 + s - 2)
                        w = P if x["kind"] == "cmp" else x["w"]
                        act.activation(pT[(s - 1) % 2][0:x["rows"], 0:w], ps[6][0:x["rows"], 0:w], ACT.Copy)\
                            .then_inc(sem("pT_made"), 1)
                        for u, j, k in plan[s - 1]:
                            if k == KT - 1:
                                to_gate(along[1] + tpu * u + j, g0 + tpu * u + j, 0, 0)
                    for u, j, k in plan[s] if s < len(steps) else ():
                        if j == k == 0:
                            split(n0 + u + 1, g0 + u * tpu)

            def to_gate(t, g, off4, to):
                act.wait_ge(*tile_done(g, off4))
                dst = gate[:, t, :] if isinstance(to, int) else gate[:, bass.ds(t + to, 1), :]
                src = bank(g)[:, :] if isinstance(to, int) else bank(g)[:, :].unsqueeze(1)
                act.activation(dst, src, ACT.Tanh, scale=0.5).then_inc(sem(f"bank_free{g % 4}"), 1)

            def nothing(t, g, off4, to):
                pass

            def merged_high(t, g, off4, to):
                x_high(a_hi[:, t, :], T[2 + t % 2][:, :], scale=0.5)

            def load_ada(k):
                if k is not None:
                    act.wait_ge(sem("ada_acc"), k + 1)
                    act.dma_start(ada_w[:, :], ada[k]).then_inc(sem("ada_loaded"), 16)

            for k in range(KT):
                square(k, sem(f"h_loaded{k - k % 2}"), 16)
            split(0, 0)
            act.wait_ge(sem("vecs_loaded"), 16)
            act.wait_ge(*c.next("lam_summed"))
            act.activation(small[:, 8:12], ps[6][:, 0:4], ACT.Exp).then_inc(sem("lam_exp"), 1)
            act.activation(rows[:, 0:8], V_range("c"), ACT.Tanh, scale=0.5).then_inc(sem("c_tanh"), 1)

            for l in range(DEPTH):
                norm_std()
                norm_high()
                act.dma_start(wsmall[:, :], pool_w[l]).then_inc(sem("small_loaded"), 16)

                run(f"qk{l}", lambda t, g, off4, to: head_squares(t, g))
                head_std(40, 64)

                def value(t, g, off4, to):
                    u, tok = t // 4, t % 4
                    act.wait_ge(*tile_done(g))
                    act.activation(vt[:, tok, 256 * u:256 * u + 256], bank(g)[:, 0:256], ACT.Copy)\
                        .then_inc(sem(f"bank_free{g % 4}"), 1)
                run(f"v{l}", value)
                attention(l)
                def conv(t, g, off4, to):
                    kind, j = t % 3, t // 3
                    act.wait_ge(*tile_done(g))
                    if kind < 2:
                        act.activation(T[kind][:, :], bank(g)[:, :], ACT.Copy)\
                            .then_inc(sem(f"bank_free{g % 4}"), 1)
                    else:
                        x_high(y_hi[:, j, :], T[2 + j % 2][:, :])
                run(f"conv_in{l}", conv)
                run(f"gate_b{l}", to_gate)
                run(f"out_b{l}", nothing)
                run(f"pool_in{l}", nothing)

                def gate_and_mixed(t, g, off4, to):
                    to_gate(t, g, off4, to)
                    for m in (t - 4, t - 3) if t in (4, 6) else ():
                        act.wait_ge(*c.next("mixed"))
                        act.activation(y_hi[:, m, :], ps[6 + m % 2][:, :], ACT.Copy, scale=V(f"pool_scale{l}", m))\
                            .then_inc(sem("xhi_made"), 1)
                run(f"gate_a{l}", gate_and_mixed)
                run(f"out_a{l}", nothing)

                run(f"gate_c{l}", to_gate)
                for hd in range(4):
                    if hd >= 2:
                        act.wait_ge(*c.next("hsq_summed"))
                    act.activation(T[hd % 2][:, :], qt[:, hd, :], ACT.Square).then_inc(sem("hsq_made"), 1)
                head_std(4, P)
                for hd in range(4):
                    x_high(y_hi[:, hd, :], T[2 + hd % 2][:, :])
                run(f"out_c{l}", merged_high)
                run(f"w_o{l}", lambda t, g, off4, to: square(t, *evacuated(g)))
                norm_std()
                norm_high()
                act.dma_start(pads[:, 2:4, 0:S], p_t[l]).then_inc(sem("p_loaded"), 16)
                act.wait_ge(sem("p_loaded"), 16 * (l + 1))
                for t in range(2):
                    act.activation(y_hi[:, t, :], pads[:, 2 + t, 0:S], ACT.Copy).then_inc(sem("xhi_made"), 1)

                n0, g0, _, _ = ST[f"mlp{l}"]

                def up(ch):
                    for i in range(2):
                        load_ada(ada_index(l, False, ch, i))
                        for u in range(2):
                            split(n0 + u + 1, g0 + 2 * u, 4 * ch + i, 4 * ch + i)
                            for j in range(2):
                                t = 2 * u + j
                                act.wait_ge(*tile_done(g0 + t, 4 * ch + i))
                                act.activation(T[t % 2][:, :], bank(g0 + t)[:, :], ACT.Relu)\
                                    .then_inc(sem("relu_made"), 1)
                                x_high(f_hi[:, bass.ds(t + 4 * i, 1), :], T[2 + t % 2][:, :].unsqueeze(1))

                def down(ch, i, squares=False):
                    load_ada(ada_index(l, True, ch, i))
                    for u in range(2):
                        split(n0 + 4 + u + 1, g0 + 8 + 2 * u, 4 * ch + i, 4 * ch + i)
                        for t in (2 * u, 2 * u + 1) if squares else ():
                            square(t + 4 * i, *evacuated(g0 + 8 + t, 4 * ch + i))

                with act.Fori(0, 3) as ch:
                    c.enter(ch, {"value_made": 8})
                    up(ch)
                    for i in range(2):
                        down(ch, i)
                    c.leave(3)
                up(3)
                for i in range(2):
                    down(3, i, squares=True)

                def projected(t, g, off4, to):
                    if t == 4:
                        norm_std()
                    act.wait_ge(*tile_done(g))
                    act.activation(gate[:, t, :], bank(g)[:, :], ACT.Copy).then_inc(sem(f"bank_free{g % 4}"), 1)
                run(f"ple_proj{l}", projected)
                norm_high()

                def ple(t, g, off4, to):
                    act.wait_ge(*tile_done(g))
                    if t >= 2:
                        act.wait_ge(sem("ple_added"), 8 * l + t - 1)
                    act.activation(T[t % 2][:, :], bank(g)[:, :], ACT.Tanh, scale=0.5)\
                        .then_inc(sem(f"bank_free{g % 4}"), 1)
                    if t >= 1:
                        square(t - 1, sem("ple_added"), 8 * l + t)
                    if t == 7:
                        square(7, sem("ple_added"), 8 * l + 8)
                run(f"ple_gate{l}", ple)

            for table in range(3):
                r = slice(64, P) if table == 0 else slice(0, P)
                act.wait_ge(sem("turns_made"), table + 1)
                act.activation(tab[r, table, :], tab[r, table, :], ACT.Sin, scale=6.283185)\
                    .then_inc(sem("tables_made"), 1)
            act.wait_ge(sem("ple_added"), 8 * DEPTH)
            act.dma_start(wsmall[:, 0:256], cmp_w2).then_inc(sem("small_loaded"), 16)
            norm_std()
            norm_high(shift=0)

            def lora_in(t, g, off4, to):
                head_squares(t, g)
            run("lora", lora_in)
            g = ST["misc"][1]
            act.wait_ge(*c.next("hsq_summed"))
            act.wait_ge(*c.next("hsq_summed"))
            act.activation(small[:, 16:20], ps[4][:, 0:QB], ACT.Sqrt, scale=1.0 / 768, bias=C("eps"))
            act.activation(small[:, 12:16], ps[5][:, 0:QB], ACT.Sqrt, scale=1.0 / 256, bias=C("eps"))\
                .then_inc(sem("std_made"), 1)
            split(ST["misc"][0] + 1, g)
            for t in range(KT):
                x_high(f_hi[:, t, :], T[2 + t % 2][:, :])
            act.wait_ge(*c.next("misc_made"))
            act.activation(rows[0:24, :], pads[0:24, 2, 0:S], ACT.Tanh, scale=0.5).then_inc(sem("g_tanh"), 1)

            for half in range(2):
                def mla_q(t, g, off4, to):
                    head_squares(t, g, slice(0, MLA_D))
                run(f"mla_q{half}", mla_q)

                def mla_k(t, g, off4, to):
                    act.wait_ge(*tile_done(g))
                    act.wait_ge(*c.next("hsq_summed"))
                    act.activation(T[t % 2][64:96, :], pads[64:96, 2, 0:S], ACT.Square)
                    act.activation(T[t % 2][0:64, :], bank(g)[0:64, :], ACT.Square).then_inc(sem("hsq_made"), 1)
                run(f"mla_k{half}", mla_k)
                head_std(8, MLA_D)
                if half == 0:
                    def mla_v(t, g, off4, to):
                        act.wait_ge(*tile_done(g))
                        act.activation(vt[:, t, :], bank(g)[:, :], ACT.Copy).then_inc(sem(f"bank_free{g % 4}"), 1)
                    run("mla_v", mla_v)
                attention(DEPTH + half)
            run("out_mla", nothing)

            def nsa_in(t, g, off4, to):
                if t < 6:
                    head_squares(t, g)
            run("nsa_in", nsa_in)
            head_std(40, 64)

            def nsa_v(t, g, off4, to):
                act.wait_ge(*tile_done(g))
                act.activation(vt[:, t, 0:256], bank(g)[:, 0:256], ACT.Copy).then_inc(sem(f"bank_free{g % 4}"), 1)
            run("nsa_v", nsa_v)

            def cmp(t, g, off4, to):
                if t % 2 == 0:
                    act.wait_ge(*tile_done(g))
                    if t == 2:
                        act.wait_ge(*c.next("hid_made"))
                    act.activation(T[0][0:64, 0:256], bank(g)[0:64, 0:256], ACT.Copy)\
                        .then_inc(sem(f"bank_free{g % 4}"), 1)
                    return
                act.wait_ge(*evacuated(g))
                act.activation(T[2][0:64, 0:256], T[1][0:64, 0:256], ACT.Tanh, scale=0.5)\
                    .then_inc(sem("hid_tanh"), 1)
                if t == 1:
                    act.wait_ge(*c.next("kc_in_psum"))
                    act.activation(rows[:, 64:64 + CMP_N], ps[7][:, 0:CMP_N], ACT.Square).then_inc(sem("kc_sq"), 1)
                    act.wait_ge(*c.next("kc_summed"))
                    act.activation(rows[:, 128:128 + CMP_N], ps[5][:, 0:CMP_N], ACT.Sqrt, scale=1.0 / 64,
                                   bias=C("eps")).then_inc(sem("kc_std"), 1)
                else:
                    act.wait_ge(*c.next("vc_in_psum"))
                    act.activation(kt[0:CMP_W, 2, 256:384], ps[7][0:CMP_W, 0:128], ACT.Copy).then_inc(sem("vc_made"), 1)
            for w in range(2):
                run(f"cmp{w}", lambda t, g, off4, to: cmp(2 * w + t, g, off4, to))
                run(f"gate_nsa{w}", lambda t, g, off4, to: to_gate(2 * w + t, g, off4, to))
            attention(DEPTH + 2)
            run("out_nsa", merged_high)
            run("w_out", lambda t, g, off4, to: square(t, *evacuated(g)))
            norm_std()
            norm_high(shift=24)
            for ch, tiles in enumerate(CHUNKS_2):
                def up(t, g, off4, to):
                    if t % 2 == 0:
                        act.wait_ge(*tile_done(g, off4))
                        act.activation(T[0][:, :], bank(g)[:, :], ACT.Tanh, scale=0.5)\
                            .then_inc(sem("ff_tanh"), 1)
                    else:
                        u = t // 2
                        x_high(f_hi[:, u, :] if isinstance(to, int) else f_hi[:, bass.ds(u + 2 * off4, 1), :],
                               T[2][:, :] if isinstance(to, int) else T[2][:, :].unsqueeze(1))
                run(f"ffn_up{ch}", up, loop=True, per={"value_made": 2})
                run(f"ffn_down{ch}", nothing)

        @block.vector
        def _(dve):
            c = Counts()

            def seq(ins):
                ins.then_inc(sem("dve_seq"), 1)
                dve.wait_ge(*c.next("dve_seq"))

            def split(n, off2=0):
                if n >= NU:
                    return
                dve.wait_ge(sem("hi_made"), n + 1 + 2 * off2)
                dve.tensor_tensor(w_lo[n % 2][:, :], raw[n % 2][:, :], w_hi[n % 2][:, :].bitcast(F32),
                                  ALU.subtract).then_inc(sem("lo_made"), 1)

            def x_low(dst, src, hi, tile=None):
                dve.wait_ge(*c.next("xhi_made"))
                ins = dve.tensor_tensor(dst, src, hi.bitcast(F32), ALU.subtract)
                if tile is None:
                    x_done(ins)
                else:
                    ins.then_inc(sem(f"bank_free{tile[0] % 4}"), 1)
                    dve.wait_ge(*evacuated(*tile))

            def x_done(ins):
                ins.then_inc(sem("x_made"), 1)
                dve.wait_ge(*c.next("x_made"))

            def run(name, tile, per=None, loop=False):
                n0, g0, units, tpu = ST[name]

                def body(u, off2, off4):
                    n, g = n0 + u, g0 + u * tpu
                    split(n + 1, off2)
                    for j in range(tpu):
                        tile(u * tpu + j, g + j, off4, 4 * off4 if not isinstance(off4, int) else 0)

                if not loop:
                    for u in range(units):
                        body(u, 0, 0)
                    return
                with dve.Fori(0, units // 2) as i:
                    c.enter(i, per or {})
                    for u in range(2):
                        body(u, i, i * (tpu // 2))
                    c.leave(units // 2)

            def at(tensor, t, to):
                return tensor[:, t, :] if isinstance(to, int) else tensor[:, bass.ds(t + to, 1), :]

            def like(x, to):
                return x if isinstance(to, int) else x.unsqueeze(1)

            def add_square(k):
                dve.wait_ge(*c.next("sq_made"))
                if k == 0:
                    return
                total = pads[:, 0, 0:S]
                first = total
                if k == 1:
                    first = pT[0][:, :]
                else:
                    dve.wait_ge(*c.next("sq_added"))
                dve.tensor_tensor(total, first, pT[k % 2][:, :], ALU.add).then_inc(sem("sq_added"), 1)
                if k == KT - 1:
                    c.next("sq_added")

            def with_squares(tile):
                def both(t, g, off4, to):
                    tile(t, g, off4, to)
                    if t >= 1:
                        add_square(t - 1)
                    if t == KT - 1:
                        add_square(t)
                return both

            def norm(gains, shift=None):
                dve.wait_ge(*c.next("std_made"))
                dve.reciprocal(small[:, 20:24], small[:, 16:20]).then_inc(sem("norm_r"), 1)
                r = ps[7][:, :]
                dve.wait_ge(*c.next("norm_spread"))

                def value(k):
                    dve.scalar_tensor_tensor(T[2 + k % 2][:, :], h[:, k, :], gains(k), r, ALU.mult, ALU.mult)\
                        .then_inc(sem("value_made"), 1)

                def low(k):
                    if shift is None:
                        x_low(a_lo[:, k, :], T[2 + k % 2][:, :], a_hi[:, k, :])
                    else:
                        dve.wait_ge(*c.next("xhi_made"))
                        x_done(dve.scalar_tensor_tensor(a_lo[:, k, :], T[2 + k % 2][:, :],
                                                        mod[:, shift + k:shift + k + 1],
                                                        a_hi[:, k, :].bitcast(F32), ALU.add, ALU.subtract))
                value(0)
                for k in range(KT):
                    if k + 1 < KT:
                        value(k + 1)
                    low(k)

            def head_rows(n_rows):
                dve.wait_ge(*c.next("hstd_made"))
                dve.reciprocal(rows[0:n_rows, :], rows[0:n_rows, :]).then_inc(sem("hrows_made"), 1)

            def attention(which):
                steps, m0 = ATTENTION[which], MC[which]
                layer = which
                diff = steps[0]["kind"] == "diff"

                def maxes(s, m):
                    x = steps[s]
                    w = x["w"]
                    for j in range(len(x["sets"])):
                        dve.wait_ge(*c.next("scores_made"))
                        bk = score_bank(m + j, diff)
                        if diff:
                            seq(dve.memset(bk[0:64, w - 64:w], NEG))
                        for lo, mask in x["masks"]:
                            n = mask.shape[-1]
                            seq(dve.tensor_tensor(bk[:, lo:lo + n], bk[:, lo:lo + n], mask, ALU.add))
                        k = 2 * (s % 2) + j
                        dve.tensor_reduce(small[:, k:k + 1], bk[:, 0:w], AX.X, ALU.max, negate=True)\
                            .then_inc(sem("max_made"), 1)

                def weigh(s, m):
                    x = steps[s]
                    w, k = x["w"], 2 * (s % 2)
                    for j in range(len(x["sets"])):
                        dve.wait_ge(*c.next("exp_done"))
                    p = probs(m, diff)[:, 0:w]
                    if s > 0:
                        dve.wait_ge(*c.next("att_made"))
                    if s == len(steps) - 1:
                        c.next("att_made")
                    if diff:
                        seq(dve.reciprocal(small[:, 12:14], small[:, 4 + k:6 + k]))
                        seq(dve.tensor_scalar(small[:, 14:15], small[:, 13:14],
                                              neg_lam[:, layer:layer + 1], None, ALU.mult))
                        seq(dve.tensor_scalar(p, p, small[:, 12:13], None, ALU.mult))
                        dve.scalar_tensor_tensor(p, probs(m + 1, diff)[:, 0:w], small[:, 14:15], p,
                                                 ALU.mult, ALU.add).then_inc(sem("att_made"), 1)
                        return
                    seq(dve.reciprocal(small[:, 12:13], small[:, 4 + k:5 + k]))
                    if "gate" in x:
                        ins = dve.tensor_scalar(p, p, small[:, 12:13], x["gate"], ALU.mult, ALU.mult)
                    else:
                        ins = dve.tensor_scalar(p, p, small[:, 12:13], None, ALU.mult)
                    ins.then_inc(sem("att_made"), 1)

                ns = len(steps[0]["sets"])
                s0 = STEP0[which]
                plan = pieces(which)
                n0 = ST[ALONG[which][0]][0] if which in ALONG else 0
                maxes(0, m0)
                for s in range(len(steps) + 2):
                    if s + 1 < len(steps):
                        maxes(s + 1, m0 + ns * (s + 1))
                    if s >= 2 and steps[s - 2]["closes"]:
                        t = steps[s - 2]["tile"]
                        dve.wait_ge(sem("pv_done"), s0 + s - 1)
                        if diff:
                            dve.tensor_copy(qt[:, t, :], ps[7][:, :]).then_inc(sem("o_made"), 1)
                        else:
                            x_low(y_lo[:, t, :], ps[7][:, :], y_hi[:, t, :])
                    if s < len(steps):
                        weigh(s, m0 + ns * s)
                    for u, j, k in plan[s] if s < len(steps) else ():
                        if j == k == 0:
                            split(n0 + u + 1)

            def nothing(t, g, off4, to):
                pass

            def add_merged(first, last):
                def tile(t, g, off4, to):
                    dve.wait_ge(*tile_done(g))
                    if t == 0:
                        gates_ready()
                    dst = merged[:, t, :] if first else T[t % 2][:, :]
                    dve.scalar_tensor_tensor(dst, gate[:, t, :], 1.0, bank(g)[:, :], ALU.add, ALU.mult)\
                        .then_inc(sem(f"bank_free{g % 4}"), 1)
                    if first:
                        return
                    dve.wait_ge(*evacuated(g))
                    if not last:
                        seq(dve.tensor_tensor(merged[:, t, :], merged[:, t, :], dst, ALU.add))
                        return
                    u = T[2 + t % 2][:, :]
                    dve.tensor_tensor(u, merged[:, t, :], dst, ALU.add).then_inc(sem("value_made"), 1)
                    dve.wait_ge(*c.next("xhi_made"))
                    x_done(dve.scalar_tensor_tensor(a_lo[:, t, :], u, 0.5, a_hi[:, t, :].bitcast(F32),
                                                    ALU.mult, ALU.subtract))
                return tile

            def merge(gate_stage, out_stage, first, last, between=nothing):
                nonlocal gates_ready
                g_gate = ST[gate_stage][1]
                gates_ready = lambda: dve.wait_ge(*evacuated(g_gate + 7))
                run(gate_stage, between)
                run(out_stage, add_merged(first, last))

            gates_ready = None

            def ada_unit(k):
                if k is None:
                    return
                dve.wait_ge(sem("ada_loaded"), 16 * k + 16)
                acc = vt[:, 0, 0:256]
                for j in range(KT):
                    w, x = ada_w[:, 256 * j:256 * j + 256], scaled[:, 8 + j:9 + j]
                    if j == 0:
                        ins = dve.tensor_scalar(acc, w, x, None, ALU.mult)
                    else:
                        ins = dve.scalar_tensor_tensor(acc, w, x, acc, ALU.mult, ALU.add)
                    if j < KT - 1:
                        seq(ins)
                ins.then_inc(sem("ada_acc"), 1)

            def ada_read(k):
                if k is not None:
                    dve.wait_ge(sem("ada_summed"), k + 1)

            def modulation(l):
                lo, hi = (0, 32) if l == 0 else (32, 48)
                dve.wait_ge(sem("ada_summed"), hi // 2)
                at0 = VT["ada_b"][0]
                seq(dve.tensor_tensor(mod[:, lo:hi], ps[6][:, lo:hi], vecs[:, at0 + lo:at0 + hi], ALU.add))
                if l == 0:
                    return
                for name, at_scale, to in (("n1", 8, 8), ("n2", 32, 16)):
                    last = dve.scalar_tensor_tensor(scaled[:, to:to + 8], mod[:, at_scale:at_scale + 8], 1.0,
                                                    V_range(name), ALU.add, ALU.mult)
                last.then_inc(sem("mod_made"), 1)
                dve.wait_ge(sem("mod_made"), 1)

            def add_h(t, g, off4, to):
                dve.wait_ge(*tile_done(g, off4))
                dve.tensor_tensor(at(h, t, to), at(h, t, to), like(bank(g)[:, :], to), ALU.add)\
                    .then_inc(sem(f"bank_free{g % 4}"), 1)

            def add_h_times(col):
                def tile(t, g, off4, to):
                    dve.wait_ge(*tile_done(g, off4))
                    s = mod[:, col + t:col + t + 1] if isinstance(to, int) else mod[:, bass.ds(col + t + to, 1)]
                    dve.scalar_tensor_tensor(at(h, t, to), like(bank(g)[:, :], to), s, at(h, t, to),
                                             ALU.mult, ALU.add).then_inc(sem(f"bank_free{g % 4}"), 1)
                return tile

            for k in range(KT):
                add_square(k)
            split(0)
            dve.wait_ge(sem("vecs_loaded"), 16)
            for l in range(DEPTH):
                for j in range(2):
                    last = dve.tensor_tensor(small[:, 2 * l + j:2 * l + j + 1], V(f"lam{l}", 2 * j),
                                             V(f"lam{l}", 2 * j + 1), ALU.mult)
            last.then_inc(sem("lam_terms"), 1)
            dve.wait_ge(*c.next("lam_exp"))
            for l in range(DEPTH):
                init = 0.8 - 0.6 * math.exp(-0.3 * l)
                seq(dve.scalar_tensor_tensor(neg_lam[:, l:l + 1], small[:, 9 + 2 * l:10 + 2 * l], -init,
                                             small[:, 8 + 2 * l:9 + 2 * l], ALU.add, ALU.subtract))
                seq(dve.tensor_scalar(scaled[:, l:l + 1], V(f"sub{l}"), 1.0 - init, None, ALU.mult))
                seq(dve.tensor_scalar(scaled[:, 2 + l:3 + l], V(f"qg{l}"), 64.0 ** -0.5, None, ALU.mult))
            seq(dve.tensor_scalar(scaled[:, 4:5], V("mla_q"), float(MLA_D) ** -0.5, None, ALU.mult))
            seq(dve.tensor_scalar(scaled[:, 5:6], V("nsa_q"), 64.0 ** -0.5, None, ALU.mult))
            dve.wait_ge(*c.next("c_tanh"))
            seq(dve.scalar_tensor_tensor(scaled[:, 16:24], rows[:, 0:8], 1.0, V_range("c"), ALU.add, ALU.mult))
            dve.tensor_scalar(scaled[:, 8:16], scaled[:, 16:24], 0.5, None, ALU.mult)\
                .then_inc(sem("ada_acc"), 1)
            dve.wait_ge(sem("ada_acc"), 1)

            for l in range(DEPTH):
                norm(lambda k: V(f"mix{l}", k))

                def qk(t, g, off4, to):
                    dve.wait_ge(*c.next("hsq_made"))
                    dst = qt[:, t, :] if t < 4 else kt[:, t - 4, :]
                    gain = scaled[:, 2 + l:3 + l] if t < 4 else V(f"kg{l}")
                    dve.tensor_scalar(dst, bank(g)[:, :], gain, None, ALU.mult)\
                        .then_inc(sem(f"bank_free{g % 4}"), 1)
                run(f"qk{l}", qk)
                head_rows(40)
                run(f"v{l}", nothing)
                for t in range(8):
                    dve.wait_ge(*c.next("spread"))
                    x = qt[:, t, :] if t < 4 else kt[:, t - 4, :]
                    dve.tensor_tensor(x, x, ps[6 + t % 2][:, :], ALU.mult).then_inc(sem("qk_made"), 1)
                attention(l)

                seq(dve.memset(pads[:, 0, 0:PAD], 0.0))

                def conv(t, g, off4, to):
                    kind, j = t % 3, t // 3
                    if kind < 2:
                        return
                    dve.wait_ge(*tile_done(g))
                    dve.wait_ge(*evacuated(g - 1))
                    dve.tensor_tensor(pads[:, 0, PAD:ROW], T[1][:, :], bank(g)[:, :], ALU.mult)\
                        .then_inc(sem(f"bank_free{g % 4}"), 1)
                    dve.wait_ge(*evacuated(g))
                    u = T[2 + j % 2][:, :]
                    seq(dve.tensor_scalar(u, pads[:, 0, PAD:ROW], V(f"conv{l}", 8 + j), None, ALU.mult))
                    for tap in (1, 0):
                        back = 2 - tap
                        seq(dve.scalar_tensor_tensor(u, pads[:, 0, PAD - back:ROW - back],
                                                     V(f"conv{l}", 4 * tap + j), u, ALU.mult, ALU.add))
                    dve.tensor_tensor(u, u, T[0][:, :], ALU.mult).then_inc(sem("value_made"), 1)
                    x_low(y_lo[:, j, :], u, y_hi[:, j, :])
                run(f"conv_in{l}", conv)
                dve.wait_ge(sem("turns_made"), 3)
                merge(f"gate_b{l}", f"out_b{l}", True, False)

                for j in range(3):
                    seq(dve.memset(pads[:, j, 0:PAD], 0.0))

                def pool_in(t, g, off4, to):
                    dve.wait_ge(*tile_done(g))
                    dve.tensor_copy(pads[:, 0, PAD:ROW], bank(g)[:, :]).then_inc(sem(f"bank_free{g % 4}"), 1)
                    dve.wait_ge(*evacuated(g))
                    src, w = 0, 1
                    for step in range(t + 1):
                        dst = 1 + step % 2
                        seq(dve.tensor_tensor(pads[:, dst, PAD:ROW], pads[:, src, PAD:ROW],
                                              pads[:, src, PAD - w:ROW - w], ALU.add))
                        src, w = dst, 2 * w
                    pooled = T[t]
                    seq(dve.scalar_tensor_tensor(pooled[:, :], pads[:, src, PAD:ROW], 1.0 / w,
                                                 pads[:, 0, PAD:ROW], ALU.mult, ALU.subtract))
                    seq(dve.tensor_tensor(pT[0][:, 0:w - 1], pads[:, src, PAD:PAD + w - 1],
                                          C("inv_count", hi=w - 1), ALU.mult))
                    dve.tensor_tensor(pooled[:, 0:w - 1], pT[0][:, 0:w - 1], pads[:, 0, PAD:PAD + w - 1],
                                      ALU.subtract).then_inc(sem("pooled"), 1)
                    dve.wait_ge(*c.next("pooled"))

                def pool_low(t):
                    dve.wait_ge(*c.next("xhi_made"))
                    x_done(dve.scalar_tensor_tensor(y_lo[:, t, :], ps[6 + t % 2][:, :], V(f"pool_scale{l}", t),
                                                    y_hi[:, t, :].bitcast(F32), ALU.mult, ALU.subtract))
                run(f"pool_in{l}", pool_in)
                def mixed_low(t, g, off4, to):
                    if t in (4, 6):
                        pool_low(t - 4)
                        pool_low(t - 3)
                merge(f"gate_a{l}", f"out_a{l}", False, False, mixed_low)

                g_gate = ST[f"gate_c{l}"][1]
                gates_ready = lambda: dve.wait_ge(*evacuated(g_gate + 7))
                run(f"gate_c{l}", nothing)
                for hd in range(4):
                    c.next("hsq_made")
                head_rows(4)
                for hd in range(4):
                    dve.wait_ge(*c.next("spread"))
                    u = T[2 + hd % 2][:, :]
                    dve.scalar_tensor_tensor(u, qt[:, hd, :], scaled[:, l:l + 1], ps[6 + hd % 2][:, :],
                                             ALU.mult, ALU.mult).then_inc(sem("value_made"), 1)
                    x_low(y_lo[:, hd, :], u, y_hi[:, hd, :])
                run(f"out_c{l}", add_merged(False, True))
                run(f"w_o{l}", with_squares(add_h))
                norm(lambda k: V(f"mlp{l}", k))
                for t in range(2):
                    x_low(y_lo[:, t, :], pads[:, 2 + t, 0:S], y_hi[:, t, :])

                n0, g0, _, _ = ST[f"mlp{l}"]

                def up(ch):
                    for i in range(2):
                        for u in range(2):
                            split(n0 + u + 1, 4 * ch + i)
                            if u == 1:
                                ada_unit(ada_index(l, False, ch, i))
                            for j in range(2):
                                t = 2 * u + j
                                dve.wait_ge(*c.next("relu_made"))
                                v = T[2 + t % 2][:, :]
                                dve.tensor_tensor(v, T[t % 2][:, :], bank(g0 + t)[:, :], ALU.mult)\
                                    .then_inc(sem("value_made"), 1)
                                dst = bass.ds(t + 4 * i, 1)
                                x_low(f_lo[:, dst, :], v.unsqueeze(1), f_hi[:, dst, :],
                                      tile=(g0 + t, 4 * ch + i))
                        ada_read(ada_index(l, False, ch, i))

                def down(ch, i, squares=False):
                    for u in range(2):
                        split(n0 + 4 + u + 1, 4 * ch + i)
                        if u == 1:
                            ada_unit(ada_index(l, True, ch, i))
                        for j in range(2):
                            t = 2 * u + j
                            dve.wait_ge(*tile_done(g0 + 8 + t, 4 * ch + i))
                            dst = h[:, bass.ds(t + 4 * i, 1), :]
                            dve.tensor_tensor(dst, dst, bank(g0 + 8 + t)[:, :].unsqueeze(1), ALU.add)\
                                .then_inc(sem(f"bank_free{(g0 + 8 + t) % 4}"), 1)
                            if squares and t + 4 * i >= 1:
                                add_square(t + 4 * i - 1)
                    ada_read(ada_index(l, True, ch, i))
                    if squares and i == 1:
                        add_square(KT - 1)

                with dve.Fori(0, 3) as ch:
                    c.enter(ch, {"relu_made": 8, "xhi_made": 8, "dve_seq": 28 if l == 0 else 14})
                    up(ch)
                    for i in range(2):
                        down(ch, i)
                    c.leave(3)
                up(3)
                for i in range(2):
                    down(3, i, squares=True)
                modulation(l)
                run(f"ple_proj{l}", nothing)
                norm(lambda k: V(f"ple{l}", k))

                def ple(t, g, off4, to):
                    dve.wait_ge(*evacuated(g))
                    v = T[2 + t % 2][:, :]
                    seq(dve.scalar_tensor_tensor(v, T[t % 2][:, :], 1.0, gate[:, t, :], ALU.add, ALU.mult))
                    dve.scalar_tensor_tensor(h[:, t, :], v, 0.5, h[:, t, :], ALU.mult, ALU.add)\
                        .then_inc(sem("ple_added"), 1)
                run(f"ple_gate{l}", with_squares(ple))

            norm(lambda k: scaled[:, 8 + k:9 + k], shift=0)

            def lora_in(t, g, off4, to):
                dve.wait_ge(*c.next("hsq_made"))
                gain = V("q_a", t) if t < 6 else V("kv_a", t - 6)
                dve.tensor_scalar(lora[:, t, :], bank(g)[:, :], gain, None, ALU.mult)\
                    .then_inc(sem(f"bank_free{g % 4}"), 1)
            run("lora", lora_in)
            dve.wait_ge(*c.next("std_made"))
            dve.reciprocal(small[:, 20:24], small[:, 16:20])
            dve.reciprocal(small[:, 24:28], small[:, 12:16]).then_inc(sem("norm_r"), 1)

            def lora_values():
                dve.wait_ge(*c.next("norm_spread"))

                def value(t):
                    dve.tensor_tensor(T[2 + t % 2][:, :], lora[:, t, :], ps[4 if t < 6 else 5][:, :], ALU.mult)\
                        .then_inc(sem("value_made"), 1)
                value(0)
                for t in range(KT):
                    if t + 1 < KT:
                        value(t + 1)
                    x_low(f_lo[:, t, :], T[2 + t % 2][:, :], f_hi[:, t, :])

            def misc(t, g, off4, to):
                lora_values()
                dve.wait_ge(*tile_done(g))
                dve.wait_ge(sem("tables_made"), 3)
                misc_t, kpe = pads[:, 2, 0:S], pads[:, 3, 0:S]
                dve.tensor_copy(misc_t, bank(g)[:, :]).then_inc(sem("misc_made"), 1)
                seq(dve.scalar_tensor_tensor(T[2][64:96, :], bank(g)[96:128, :], V("mla_k", 0, slice(96, 128)),
                                             tab[96:128, 0, :], ALU.mult, ALU.mult))
                seq(dve.scalar_tensor_tensor(kpe[64:96], bank(g)[64:96, :], V("mla_k", 0, slice(64, 96)),
                                             tab[64:96, 0, :], ALU.mult, ALU.mult))
                dve.tensor_tensor(kpe[64:96], kpe[64:96], T[2][64:96, :], ALU.add)\
                    .then_inc(sem(f"bank_free{g % 4}"), 1)
                dve.wait_ge(*evacuated(g))
            run("misc", misc)
            dve.wait_ge(*c.next("gt_in_psum"))
            seq(dve.tensor_scalar(gt[:, :, :], ps[6][:, 0:QB * P].rearrange("p (b n) -> p b n", b=QB)[:, :, 0:24],
                                  1.0, 0.5, ALU.add, ALU.mult))
            sees_one = C("cmp_valid")[:, 0:QB * CMP_W:CMP_W].unsqueeze(2).to_broadcast([P, QB, 8])
            seq(dve.tensor_tensor(gt[:, :, 0:24:3], gt[:, :, 0:24:3], sees_one, ALU.mult))

            for half in range(2):
                def mla_q(t, g, off4, to):
                    dve.wait_ge(*c.next("hsq_made"))
                    q, b = qt[:, t, :], bank(g)
                    seq(dve.tensor_scalar(q[0:64], b[0:64, :], scaled[0:64, 4:5], None, ALU.mult))
                    seq(dve.scalar_tensor_tensor(T[2][64:96, :], b[96:128, :], scaled[96:128, 4:5],
                                                 tab[96:128, 0, :], ALU.mult, ALU.mult))
                    seq(dve.scalar_tensor_tensor(q[64:96], b[64:96, :], scaled[64:96, 4:5],
                                                 tab[64:96, 0, :], ALU.mult, ALU.mult))
                    dve.tensor_tensor(q[64:96], q[64:96], T[2][64:96, :], ALU.add)\
                        .then_inc(sem(f"bank_free{g % 4}"), 1)
                run(f"mla_q{half}", mla_q)

                def mla_k(t, g, off4, to):
                    dve.wait_ge(*c.next("hsq_made"))
                    seq(dve.tensor_copy(kt[64:96, t, :], pads[64:96, 3, 0:S]))
                    dve.tensor_scalar(kt[0:64, t, :], bank(g)[0:64, :], V("mla_k", 0, slice(0, 64)), None,
                                      ALU.mult).then_inc(sem(f"bank_free{g % 4}"), 1)
                run(f"mla_k{half}", mla_k)
                head_rows(8)
                if half == 0:
                    run("mla_v", nothing)
                for t in range(8):
                    dve.wait_ge(*c.next("spread"))
                    x = qt[0:MLA_D, t, :] if t < 4 else kt[0:MLA_D, t - 4, :]
                    dve.tensor_tensor(x, x, ps[6 + t % 2][0:MLA_D, :], ALU.mult).then_inc(sem("qk_made"), 1)
                attention(DEPTH + half)
            g_mla = ST["gate_mla"][1]
            gates_ready = lambda: dve.wait_ge(*evacuated(g_mla + 7))
            run("out_mla", add_merged(True, False))

            def nsa_tile(t):
                return qt[:, t, :] if t < 4 else kt[:, t - 4, :]

            def nsa_in(t, g, off4, to):
                if t < 6:
                    dve.wait_ge(*c.next("hsq_made"))
                    gain = scaled[:, 5:6] if t < 4 else V("nsa_ks" if t == 4 else "nsa_kw")
                    dve.tensor_scalar(nsa_tile(t), bank(g)[:, :], gain, None, ALU.mult)\
                        .then_inc(sem(f"bank_free{g % 4}"), 1)
                    return
                dve.wait_ge(*tile_done(g))
                flat = windows(t - 6)
                name = "pos_k" if t == 6 else "pos_v"
                for grp in range(2):
                    r = slice(64 * grp, 64 * grp + 64)
                    for par in range(2):
                        dst = flat[64 * par:64 * par + 64].rearrange("p (l g n) -> p l g n", l=16, g=2)[:, :, grp, 0:CMP_N]
                        for lh in range(2):
                            tok = bank(g)[r, :].rearrange("p (n l two) -> p l n two", l=8, two=2)
                            src = tok[:, :, lh:lh + CMP_N, par]
                            at0 = VT[name][0]
                            pos = vecs[r, at0 + 16 * lh + par:at0 + 16 * lh + 16:2].unsqueeze(2)\
                                .to_broadcast([64, 8, CMP_N])
                            last = dve.tensor_tensor(dst[:, 8 * lh:8 * lh + 8, :], src, pos, ALU.add)
                last.then_inc(sem(f"bank_free{g % 4}"), 1)

            seq(dve.memset(pads[:, :, :], 0.0))
            run("nsa_in", nsa_in)
            head_rows(40)
            run("nsa_v", nothing)
            for t in range(6):
                x = nsa_tile(t)
                dve.wait_ge(*c.next("rotated"))
                seq(dve.tensor_tensor(T[2][:, :], ps[4 + t % 2][:, :], tab[:, 2, :], ALU.mult))
                seq(dve.tensor_tensor(x, x, tab[:, 1, :], ALU.mult))
                seq(dve.tensor_tensor(x, x, T[2][:, :], ALU.add))
                dve.wait_ge(*c.next("spread"))
                dve.tensor_tensor(x, x, ps[6 + t % 2][:, :], ALU.mult).then_inc(sem("qk_made"), 1)

            hid = T[3][0:64, 0:256]
            kc = kt[:, 2, P:P + CMP_N]

            def cmp(t, g, off4, to):
                if t % 2 == 0:
                    return
                dve.wait_ge(*tile_done(g))
                dve.wait_ge(*evacuated(g - 1))
                dve.tensor_tensor(T[1][0:64, 0:256], bank(g)[0:64, 0:256], T[0][0:64, 0:256], ALU.add)\
                    .then_inc(sem(f"bank_free{g % 4}"), 1)
                dve.wait_ge(*c.next("hid_tanh"))
                dve.scalar_tensor_tensor(hid, T[2][0:64, 0:256], 1.0, T[1][0:64, 0:256], ALU.add, ALU.mult)\
                    .then_inc(sem("hid_made"), 1)
                dve.wait_ge(*c.next("hid_turned"))
                dve.tensor_scalar(kt[:, 2, 0:P], ps[6][:, 0:P], 0.5, None, ALU.mult).then_inc(sem("hT_made"), 1)
                if t == 1:
                    dve.wait_ge(*c.next("kc_sq"))
                    dve.tensor_scalar(kt[:, 2, P:P + CMP_W], ps[7][:, 0:CMP_W], V("nsa_kc"), None, ALU.mult)\
                        .then_inc(sem("kc_gained"), 1)
                    dve.wait_ge(*c.next("kc_std"))
                    ends = slice(31, S, 16)
                    seq(dve.reciprocal(rows[:, 192:192 + CMP_N], rows[:, 128:128 + CMP_N]))
                    seq(dve.tensor_tensor(rows[:, 256:256 + CMP_N], ps[4][:, 0:CMP_N], tab[:, 2, ends], ALU.mult))
                    seq(dve.tensor_tensor(kc, kc, tab[:, 1, ends], ALU.mult))
                    seq(dve.tensor_tensor(kc, kc, rows[:, 256:256 + CMP_N], ALU.add))
                    dve.tensor_tensor(kc, kc, rows[:, 192:192 + CMP_N], ALU.mult).then_inc(sem("kc_made"), 1)
            for w in range(2):
                run(f"cmp{w}", lambda t, g, off4, to: cmp(2 * w + t, g, off4, to))
                run(f"gate_nsa{w}", nothing)
            attention(DEPTH + 2)
            g_nsa = ST["gate_nsa2"][1]
            gates_ready = lambda: dve.wait_ge(*evacuated(g_nsa + 3))
            run("out_nsa", add_merged(False, True))
            run("w_out", with_squares(add_h_times(16)))
            norm(lambda k: scaled[:, 16 + k:17 + k], shift=24)
            for ch, tiles in enumerate(CHUNKS_2):
                def up(t, g, off4, to):
                    if t % 2 == 0:
                        dve.wait_ge(*c.next("ff_tanh"))
                        dve.scalar_tensor_tensor(T[1][:, :], T[0][:, :], 1.0, bank(g)[:, :], ALU.add, ALU.mult)\
                            .then_inc(sem(f"bank_free{g % 4}"), 1)
                        dve.wait_ge(*evacuated(g, off4))
                    else:
                        u = t // 2
                        dve.wait_ge(*tile_done(g, off4))
                        dve.scalar_tensor_tensor(T[2][:, :], T[1][:, :], 0.5, bank(g)[:, :], ALU.mult, ALU.mult)\
                            .then_inc(sem("value_made"), 1)
                        if isinstance(to, int):
                            x_low(f_lo[:, u, :], T[2][:, :], f_hi[:, u, :], tile=(g, off4))
                        else:
                            dst = bass.ds(u + 2 * off4, 1)
                            x_low(f_lo[:, dst, :], T[2][:, :].unsqueeze(1), f_hi[:, dst, :],
                                  tile=(g, off4))
                run(f"ffn_up{ch}", up, loop=True, per={"ff_tanh": 2, "xhi_made": 2})
                run(f"ffn_down{ch}", add_h_times(40))

        @block.tensor
        def _(pe):
            c = Counts()

            def products(dst, n, g, off4, pairs, inputs=None):
                if g >= 4 or not isinstance(off4, int):
                    pe.wait_ge(sem(f"bank_free{g % 4}"), g // 4 + off4)
                total = 3 * len(pairs)
                done = 0
                for k, (a, b) in enumerate(pairs):
                    if inputs is not None:
                        pe.wait_ge(*inputs[k])
                    for i, j in ((0, 0), (0, 1), (1, 0)):
                        ins = pe.matmul(dst, a[i], b[j], start=done == 0, stop=done == total - 1)
                        done += 1
                ins.then_inc(sem("tile_done"), 1)

            def weight(n, lo, hi):
                return w_hi[n % 2][:, lo:hi], w_lo[n % 2][:, lo:hi]

            def ready(n, off2=0):
                pe.wait_ge(sem("lo_made"), n + 1 + 2 * off2)

            def unit(n, g, x, kts, cols, off2=0, off4=0, m=P, tiles=None, k0=0, inputs=None, before=None):
                ready(n, off2)
                count = cols // P if tiles is None else tiles
                if inputs is not None and count <= 2:
                    if g >= 4 or not isinstance(off4, int):
                        for j in range(count):
                            pe.wait_ge(sem(f"bank_free{(g + j) % 4}"), (g + j) // 4 + off4)
                    for k in range(kts):
                        pe.wait_ge(*inputs[k])
                        for j in range(count):
                            a = weight(n, k * cols + j * P, k * cols + j * P + m)
                            for p, q in ((0, 0), (0, 1), (1, 0)):
                                ins = pe.matmul(bank(g + j)[0:m, :], a[p], x[q][:, k0 + k, :],
                                                start=k == 0 and (p, q) == (0, 0),
                                                stop=k == kts - 1 and (p, q) == (1, 0))
                            if k == kts - 1:
                                ins.then_inc(sem("tile_done"), 1)
                    return
                for j in range(count):
                    if before:
                        before(j)
                    pairs = [(weight(n, k * cols + j * P, k * cols + j * P + m),
                              (x[0][:, k0 + k, :], x[1][:, k0 + k, :])) for k in range(kts)]
                    products(bank(g + j)[0:m, :], n, g + j, off4, pairs, inputs if j == 0 else None)

            def unit_tokens(n, g, x, kts, cols, k0=0):
                ready(n)
                for t in range(QB):
                    pairs = [((x[0][:, k0 + k, t * P:(t + 1) * P], x[1][:, k0 + k, t * P:(t + 1) * P]),
                              weight(n, k * cols, (k + 1) * cols)) for k in range(kts)]
                    products(bank(g + t)[:, 0:cols], n, g + t, 0, pairs)

            A, Fx, Y = (a_hi, a_lo), (f_hi, f_lo), (y_hi, y_lo)

            def run(name, x, kts, cols, loop=False, after=None, tiles=None, inputs=None, before=None):
                n0, g0, units, tpu = ST[name]
                if not loop:
                    for u in range(units):
                        unit(n0 + u, g0 + u * tpu, x, kts, cols, tiles=tiles, before=before,
                             inputs=inputs if u == 0 else None)
                        if after:
                            after(u)
                    return
                with pe.Fori(0, units // 2) as i:
                    for u in range(2):
                        unit(n0 + u, g0 + u * tpu, x, kts, cols, i, i * (tpu // 2),
                             inputs=inputs if u == 0 else None)

            def coming(k):
                return [c.next("x_made") for _ in range(k)]

            def inputs_ready(k):
                for _ in range(k):
                    at = c.next("x_made")
                pe.wait_ge(*at)

            def norm_sums():
                for _ in range(KT - 1):
                    at = c.next("sq_added")
                pe.wait_ge(*at)
                for b in range(QB):
                    ins = pe.matmul(ps[7][:, b:b + 1], pads[:, 0, b * P:(b + 1) * P], C("ones", hi=1),
                                    start=True, stop=True)
                ins.then_inc(sem("norm_summed"), 1)

            def norm_spread():
                pe.wait_ge(*c.next("norm_r"))
                for b in range(QB):
                    ins = pe.matmul(ps[7][:, b * P:(b + 1) * P], small[:, 20 + b:21 + b].to_broadcast([P, P]),
                                    C("ident"), start=True, stop=True)
                ins.then_inc(sem("norm_spread"), 1)

            def norm():
                norm_sums()
                norm_spread()

            def sum_squares(dst, lhsT, rhs, start, stop):
                pe.wait_ge(*c.next("hsq_made"))
                pe.matmul(dst, lhsT, rhs, start=start, stop=stop).then_inc(sem("hsq_summed"), 1)

            def row64(r):
                return C("row64", lo=47 - r, hi=87 - r)

            def attention(which):
                steps, s0, m0 = ATTENTION[which], STEP0[which], MC[which]
                ns = len(steps[0]["sets"])
                diff = steps[0]["kind"] == "diff"

                def scores(s):
                    x = steps[s]
                    for j, (q, k) in enumerate(x["sets"]):
                        m = ns * s + j
                        if m >= 2 * ns:
                            pe.wait_ge(sem("exp_done"), m0 + m - 2 * ns + 1)
                        pe.matmul(score_bank(m0 + m, diff)[:, 0:x["w"]], q, k, start=True, stop=True)\
                            .then_inc(sem("scores_made"), 1)

                def turn(s):
                    x = steps[s]
                    if s >= 1:
                        pe.wait_ge(*c.next("pT_made"))
                    pe.wait_ge(*c.next("att_made"))
                    p = probs(m0 + ns * s, diff)
                    if x["kind"] == "cmp":
                        ins = pe.transpose(ps[6][0:CMP_W, 0:P], p[:, 0:CMP_W], C("ident"))
                    else:
                        for j in range(x["w"] // P):
                            ins = pe.transpose(ps[6][:, j * P:(j + 1) * P], p[:, j * P:(j + 1) * P], C("ident"))
                    ins.then_inc(sem("pT_in_psum"), 1)

                def apply(s):
                    x = steps[s]
                    if s == len(steps) - 1:
                        pe.wait_ge(*c.next("pT_made"))
                    if x["opens"] and s > 0:
                        pe.wait_ge(*c.next("o_made" if diff else "x_made"))
                    n = len(x["values"])
                    for j, v in enumerate(x["values"]):
                        ins = pe.matmul(x["out"], v, pT[s % 2][0:x["rows"], j * P:(j + 1) * P],
                                        start=x["first"] and j == 0, stop=x["last"] and j == n - 1)
                    ins.then_inc(sem("pv_done"), 1)

                plan = pieces(which)
                n0, g0, _, tpu = ST[ALONG[which][0]] if which in ALONG else (0, 0, 0, 0)

                def piece(u, j, k):
                    n, g = n0 + u, g0 + tpu * u + j
                    if j == k == 0:
                        ready(n)
                    if k == 0:
                        pe.wait_ge(sem(f"bank_free{g % 4}"), g // 4)
                    w = weight(n, k * 256 + j * P, k * 256 + (j + 1) * P)
                    for p, q in ((0, 0), (0, 1), (1, 0)):
                        ins = pe.matmul(bank(g)[:, :], w[p], A[q][:, k, :], start=k == 0 and (p, q) == (0, 0),
                                        stop=k == KT - 1 and (p, q) == (1, 0))
                    if k == KT - 1:
                        ins.then_inc(sem("tile_done"), 1)

                scores(0)
                scores(1)
                for s in range(len(steps)):
                    if s + 2 < len(steps):
                        scores(s + 2)
                    for at in plan[s]:
                        piece(*at)
                    turn(s)
                    if s >= 1:
                        apply(s - 1)
                apply(len(steps) - 1)

            def ada_sum(k):
                if k is None:
                    return
                pe.wait_ge(sem("ada_acc"), k + 2)
                for m in range(2):
                    ins = pe.matmul(ps[6][:, bass.ds(2 * k + m, 1)], vt[:, 0, m * P:(m + 1) * P],
                                    C("ones", hi=1), start=True, stop=True)
                ins.then_inc(sem("ada_summed"), 1)

            pe.wait_ge(sem("lam_terms"), 1)
            pe.wait_ge(sem("consts_loaded"), 16)
            pe.matmul(ps[6][:, 0:4], C("ones"), small[:, 0:4], start=True, stop=True)\
                .then_inc(sem("lam_summed"), 1)

            for l in range(DEPTH):
                norm()
                x_tiles = coming(8)

                def sums(u):
                    if u >= 1:
                        for t in (2 * u - 2, 2 * u - 1):
                            sum_squares(ps[5][0:40, :], row64(2 * t if t < 4 else 32 + 2 * (t - 4)),
                                        T[t % 2][:, :], t == 0, t == 7)
                run(f"qk{l}", A, 8, 256, after=sums, inputs=x_tiles)
                sums(4)
                n, g, _, _ = ST[f"v{l}"]
                for u in range(2):
                    unit_tokens(n + u, g + 4 * u, A, 8, 256)
                pe.wait_ge(*c.next("hrows_made"))
                if l == 0:
                    pe.wait_ge(sem("spread_loaded"), 16)

                def spread_heads(tiles, rows_of):
                    for t in range(tiles):
                        if t >= 2:
                            pe.wait_ge(*c.next("qk_made"))
                        lhsT, rhs, dst = rows_of(t)
                        pe.matmul(dst, lhsT, rhs, start=True, stop=True).then_inc(sem("spread"), 1)

                def two_heads(t):
                    r0 = 0 if t < 4 else 32
                    j = t % 4
                    return tab[r0:r0 + 8, 0, j * P:(j + 1) * P], rows[r0:r0 + 8, :], ps[6 + t % 2][:, :]
                spread_heads(8, two_heads)
                c.next("qk_made")
                pe.wait_ge(*c.next("qk_made"))
                pe.wait_ge(*evacuated(g + 7))
                attention(l)
                pe.wait_ge(*c.next("o_made"))
                run(f"conv_in{l}", A, 8, 256)
                run(f"gate_b{l}", A, 8, 256)
                inputs_ready(4)
                run(f"out_b{l}", Y, 4, 512)
                run(f"pool_in{l}", A, 8, 256)
                pe.wait_ge(sem("small_loaded"), 16 * (l + 1))
                y_tiles = coming(4)

                def mix(u):
                    if u not in (1, 2):
                        return
                    for t in (2 * u - 2, 2 * u - 1):
                        pe.wait_ge(*c.next("pooled"))
                        if t >= 2:
                            pe.wait_ge(*y_tiles[t - 2])
                        pe.matmul(ps[6 + t % 2][:, :], wsmall[:, t * P:(t + 1) * P], T[t][:, :],
                                  start=True, stop=True).then_inc(sem("mixed"), 1)
                run(f"gate_a{l}", A, 8, 256, after=mix)
                pe.wait_ge(*y_tiles[3])
                run(f"out_a{l}", Y, 4, 512)
                run(f"gate_c{l}", A, 8, 256)
                for hd in range(4):
                    sum_squares(ps[5][0:4, :], C("row96", lo=15 - hd, hi=19 - hd), T[hd % 2][:, :], hd == 0, hd == 3)
                pe.wait_ge(*c.next("hrows_made"))
                y_tiles = coming(4)
                for hd in range(4):
                    if hd >= 2:
                        pe.wait_ge(*y_tiles[hd - 2])
                    pe.matmul(ps[6 + hd % 2][:, :], C("ident", slice(0, 4), hd, hd + 1).to_broadcast([4, P]),
                              rows[0:4, :], start=True, stop=True).then_inc(sem("spread"), 1)
                run(f"out_c{l}", Y, 4, 512, inputs=y_tiles)
                run(f"w_o{l}", A, 8, 256, inputs=coming(8))
                norm()
                x_tiles = coming(8)
                n0, g0, _, _ = ST[f"mlp{l}"]

                def up(ch):
                    for i in range(2):
                        for u in range(2):
                            unit(n0 + u, g0 + 2 * u, A, 8, 256, 4 * ch + i, 4 * ch + i,
                                 inputs=x_tiles if u == i == 0 else None)
                        ada_sum(ada_index(l, False, ch, i))

                def down(ch, i):
                    hidden = [evacuated(g0 + k, 4 * ch) for k in range(KT)]
                    for u in range(2):
                        unit(n0 + 4 + u, g0 + 8 + 2 * u, Fx, 8, 256, 4 * ch + i, 4 * ch + i,
                             inputs=hidden if u == i == 0 else None)
                    ada_sum(ada_index(l, True, ch, i))

                with pe.Fori(0, 3) as ch:
                    up(ch)
                    for i in range(2):
                        down(ch, i)
                up(3)
                for i in range(2):
                    down(3, i)
                inputs_ready(2)

                def norm_between(j):
                    if j == 4:
                        norm_sums()
                    if j == 6:
                        norm_spread()
                run(f"ple_proj{l}", Y, 2, 1024, before=norm_between)
                run(f"ple_gate{l}", A, 8, 256, inputs=coming(8))

            norm()
            x_tiles = coming(8)

            def lora_sums(u):
                if u >= 1:
                    for t in (2 * u - 2, 2 * u - 1):
                        pe.wait_ge(*c.next("hsq_made"))
                        for b in range(QB):
                            ins = pe.matmul(ps[4 if t < 6 else 5][:, b:b + 1], T[t % 2][:, b * P:(b + 1) * P],
                                            C("ones", hi=1), start=t in (0, 6) and b == 0,
                                            stop=t in (5, 7) and b == QB - 1)
                        ins.then_inc(sem("hsq_summed"), 1)
            run("lora", A, 8, 256, after=lora_sums, inputs=x_tiles)
            lora_sums(4)
            run("misc", A, 8, 128)
            pe.wait_ge(*c.next("norm_r"))
            for i in range(2):
                for b in range(QB):
                    ins = pe.matmul(ps[4 + i][:, b * P:(b + 1) * P],
                                    small[:, 20 + 4 * i + b:21 + 4 * i + b].to_broadcast([P, P]),
                                    C("ident"), start=True, stop=True)
            ins.then_inc(sem("norm_spread"), 1)
            lora_tiles = coming(8)

            def turn_gates():
                pe.wait_ge(sem("g_tanh"), 1)
                for b in range(QB):
                    ins = pe.transpose(ps[6][:, b * P:b * P + 24], rows[0:24, b * P:(b + 1) * P],
                                       C("ident", slice(0, 24), 0, 24))
                ins.then_inc(sem("gt_in_psum"), 1)

            def row96(j):
                return C("row96", slice(0, MLA_D), 15 - j, 23 - j)

            for half in range(2):
                n, g, _, _ = ST[f"mla_q{half}"]
                for u in range(2):
                    unit(n + u, g + 2 * u, Fx, 6, 256, inputs=lora_tiles if half == u == 0 else None)
                    if half == u == 0:
                        turn_gates()
                    for t in (2 * u, 2 * u + 1):
                        sum_squares(ps[5][0:8, :], row96(t), T[t % 2][0:MLA_D, :], t == 0, False)
                n, g, _, _ = ST[f"mla_k{half}"]
                if half == 0:
                    pe.wait_ge(*lora_tiles[7])
                unit(n, g, Fx, 2, 512, k0=6)
                for t in range(4):
                    sum_squares(ps[5][0:8, :], row96(4 + t), T[t % 2][0:MLA_D, :], False, t == 3)
                if half == 0:
                    n, gv, _, _ = ST["mla_v"]
                    unit_tokens(n, gv, Fx, 2, 512, k0=6)
                pe.wait_ge(*c.next("hrows_made"))
                for t in range(8):
                    if t >= 2:
                        pe.wait_ge(*c.next("qk_made"))
                    pe.matmul(ps[6 + t % 2][0:MLA_D, :], C("ident", slice(0, 8), t, t + 1).to_broadcast([8, MLA_D]),
                              rows[0:8, :], start=True, stop=True).then_inc(sem("spread"), 1)
                c.next("qk_made")
                pe.wait_ge(*c.next("qk_made"))
                if half == 0:
                    pe.wait_ge(*evacuated(gv + 3))
                attention(DEPTH + half)
                if half == 0:
                    pe.wait_ge(*c.next("x_made"))
            inputs_ready(1)
            run("out_mla", Y, 4, 512)

            def nsa_sums(u):
                if 1 <= u <= 3:
                    for t in (2 * u - 2, 2 * u - 1):
                        sum_squares(ps[5][0:40, :], row64(2 * t if t < 4 else 32 + 2 * (t - 4)),
                                    T[t % 2][:, :], t == 0, t == 5)
            run("nsa_in", A, 8, 256, after=nsa_sums)
            n, g, _, _ = ST["nsa_v"]
            unit_tokens(n, g, A, 8, 256)
            pe.wait_ge(*c.next("hrows_made"))
            for t in range(6):
                if t >= 2:
                    pe.wait_ge(*c.next("qk_made"))
                x = qt[:, t, :] if t < 4 else kt[:, t - 4, :]
                pe.matmul(ps[4 + t % 2][:, :], C("rot"), x, start=True, stop=True).then_inc(sem("rotated"), 1)
                lhsT, rhs, dst = two_heads(t)
                pe.matmul(dst, lhsT, rhs, start=True, stop=True).then_inc(sem("spread"), 1)
            c.next("qk_made")
            pe.wait_ge(*c.next("qk_made"))

            pe.wait_ge(sem("small_loaded"), 16 * (DEPTH + 1))
            for which in range(2):
                flat = windows(which)
                n0, g0, _, _ = ST[f"cmp{which}"]
                for part in range(2):
                    n, g = n0 + part, g0 + part
                    ready(n)
                    pe.wait_ge(sem(f"bank_free{g % 4}"), g // 4)
                    if which == 0 and part == 0:
                        pe.wait_ge(*evacuated(ST["nsa_in"][1] + 7))
                    for j in range(8):
                        lp = 8 * part + j
                        ins = pe.matmul(bank(g)[0:64, 0:256], flat[:, 64 * lp:64 * lp + 64],
                                        raw[n % 2][:, 256 * j:256 * j + 256], start=j == 0, stop=j == 7)
                    ins.then_inc(sem("tile_done"), 1)
                run(f"gate_nsa{which}", A, 8, 256)
                pe.wait_ge(*c.next("hid_made"))
                for k in range(2):
                    ins = pe.transpose(ps[6][:, 64 * k:64 * k + 64], T[3][0:64, k * P:(k + 1) * P],
                                       C("ident", slice(0, 64), 0, 64))
                ins.then_inc(sem("hid_turned"), 1)
                pe.wait_ge(*c.next("hT_made"))
                if which == 0:
                    for grp in range(2):
                        for k in range(2):
                            ins = pe.matmul(ps[7][64 * grp:64 * grp + 64, 0:CMP_W],
                                            wsmall[:, 64 * k:64 * k + 64],
                                            kt[:, 2, 64 * k + 32 * grp:64 * k + 32 * grp + CMP_W],
                                            start=k == 0, stop=k == 1)
                    ins.then_inc(sem("kc_in_psum"), 1)
                    pe.wait_ge(*c.next("kc_gained"))
                    pe.matmul(ps[4][:, 0:CMP_N], C("rot"), kt[:, 2, P:P + CMP_N], start=True, stop=True)
                    pe.matmul(ps[5][:, 0:CMP_N], C("blocks"), rows[:, 64:64 + CMP_N], start=True, stop=True)\
                        .then_inc(sem("kc_summed"), 1)
                    pe.wait_ge(*c.next("kc_made"))
                else:
                    for grp in range(2):
                        for k in range(2):
                            ins = pe.matmul(ps[7][0:CMP_W, 64 * grp:64 * grp + 64],
                                            kt[:, 2, 64 * k + 32 * grp:64 * k + 32 * grp + CMP_W],
                                            wsmall[:, P + 64 * k:P + 64 * k + 64], start=k == 0, stop=k == 1)
                    ins.then_inc(sem("vc_in_psum"), 1)
                    pe.wait_ge(sem("vc_made"), 1)
            attention(DEPTH + 2)
            inputs_ready(1)
            run("out_nsa", Y, 4, 512)
            x_tiles = coming(8)
            run("w_out", A, 8, 256, inputs=x_tiles)
            norm()
            x_tiles = coming(8)
            for ch, tiles in enumerate(CHUNKS_2):
                run(f"ffn_up{ch}", A, 8, 256, loop=True, inputs=x_tiles if ch == 0 else None)
                hidden = [evacuated(ST[f"ffn_up{ch}"][1] + 2 * k + 1) for k in range(tiles)]
                run(f"ffn_down{ch}", Fx, tiles, 256, inputs=hidden)


def feature_units(w, kts, cols):
    K, N = w.shape
    assert K == kts * P and N % cols == 0
    u = w.reshape(kts, P, N // cols, cols).transpose(2, 1, 0, 3).reshape(N // cols, P, kts * cols)
    return pad_units(u)


def pad_units(u):
    if u.shape[2] == UNIT:
        return u
    out = np.zeros((u.shape[0], P, UNIT), np.float32)
    out[:, :, :u.shape[2]] = u
    return out


def lay_out(a):
    f = lambda name: np.asarray(a[name])
    zero = lambda *s: np.zeros(s, np.float32)
    units = []
    for l in range(DEPTH):
        w = f("w_in")[l]
        part = lambda i: w[:, 512 * i:512 * (i + 1)]
        gates = w[:, 3584:]
        conv = np.concatenate([part(i)[:, P * j:P * (j + 1)] for j in range(4) for i in (2, 1, 3)], 1)
        out_units = lambda m: pad_units(m.reshape(4, P, 2, 512).transpose(2, 1, 0, 3).reshape(2, P, UNIT))
        units += [feature_units(np.concatenate([part(4), part(5)], 1), 8, 256), feature_units(part(6), 8, 256),
                  feature_units(conv, 8, 256), feature_units(gates[:, 1024:2048], 8, 256),
                  out_units(f("w_conv_out")[l]), feature_units(part(0), 8, 256),
                  feature_units(gates[:, :1024], 8, 256), out_units(f("w_pool_out")[l]),
                  feature_units(gates[:, 2048:], 8, 256), out_units(f("w_attn_out")[l]),
                  feature_units(f("w_o")[l], 8, 256)]
        for ch in range(4):
            units += [feature_units(f("w_up")[l][:, 1024 * ch:1024 * (ch + 1)], 8, 256),
                      feature_units(f("w_down")[l][1024 * ch:1024 * (ch + 1)], 8, 256)]
        units += [feature_units(f("w_ple_proj")[l], 2, 1024), feature_units(f("w_ple_gate")[l], 8, 256)]
    w = f("w_in_2")[0]
    sizes = (768, 256, 32, 512, 128, 128, 128, 128, 128, 128, 24, 1024, 1024)
    cut = np.split(w, np.cumsum(sizes)[:-1], axis=1)
    c_q, c_kv, k_pe, q_n, k_c, v_c, k_s, v_s, k_w, v_w, g_n, g_mla, g_nsa = cut
    swap = lambda m: np.concatenate([m[..., 16:32], m[..., 0:16]], -1)
    misc = np.concatenate([g_n, zero(D, 40), k_pe, swap(k_pe)], 1)
    q_pairs = q_n.reshape(D, 2, 4, 64).transpose(0, 2, 1, 3).reshape(D, 512)
    q_b = f("mla_w_q_b_2")[0].reshape(768, 8, MLA_D)
    q_b = np.concatenate([q_b, swap(q_b[..., 64:])], -1).reshape(768, 8 * P)
    kv_b = f("mla_w_kv_b_2")[0].reshape(256, 8, P)
    k_b = np.concatenate([kv_b[..., :64], zero(256, 8, 64)], -1).reshape(256, 8 * P)
    v_b = kv_b[..., 64:].reshape(256, 512)
    units += [feature_units(np.concatenate([c_q, c_kv], 1), 8, 256), feature_units(misc, 8, P)]
    for half in range(2):
        units += [feature_units(q_b[:, 512 * half:512 * (half + 1)], 6, 256),
                  feature_units(k_b[:, 512 * half:512 * (half + 1)], 2, 512)]
        if half == 0:
            units += [feature_units(v_b, 2, 512)]
    out_units = lambda m: pad_units(m.reshape(4, P, 2, 512).transpose(2, 1, 0, 3).reshape(2, P, UNIT))
    o_nsa = f("w_o_nsa_2")[0].reshape(2, 4, 64, D).transpose(1, 0, 2, 3).reshape(512, D)
    cmp1 = [f(n)[0].reshape(2, 8, P, 256).transpose(0, 2, 1, 3).reshape(2, P, UNIT)
            for n in ("cmp_w1_k_2", "cmp_w1_v_2")]
    units += [feature_units(g_mla, 8, 256), out_units(f("w_o_mla_2")[0]),
              feature_units(np.concatenate([q_pairs, k_s, k_w, k_c, v_c], 1), 8, 256),
              feature_units(np.concatenate([v_s, v_w], 1), 8, 256)]
    for i in range(2):
        units += [cmp1[i], feature_units(g_nsa[:, 256 * i:256 * (i + 1)], 8, 256)]
    units += [feature_units(g_nsa[:, 512:], 8, 256), out_units(o_nsa), feature_units(f("w_out_2")[0], 8, 256)]
    at = 0
    for tiles in CHUNKS_2:
        n = P * tiles
        pair = np.stack([f(m)[0][:, at:at + n].reshape(D, tiles, P) for m in ("ffn_w_gate_2", "ffn_w_up_2")], 2)
        units += [feature_units(pair.reshape(D, 2 * n), 8, 256),
                  feature_units(f("ffn_w_down_2")[0][at:at + n], tiles, 256)]
        at += n
    weights = np.concatenate(units, 0)
    ada = feature_units(f("ada_w_2")[0], 8, 256)

    cols = {}
    tall = lambda v: v.reshape(-1, P).T
    twice = lambda v: np.concatenate([v, v])[:, None]
    for l in range(DEPTH):
        cols[f"mix{l}"] = tall(f("norm_mix_g")[l])
        cols[f"pool_scale{l}"] = tall(f("pool_scale")[l])
        cols[f"conv{l}"] = tall(f("conv_w")[l].reshape(-1))
        cols[f"qg{l}"], cols[f"kg{l}"] = twice(f("q_norm_g")[l]), twice(f("k_norm_g")[l])
        lam = np.stack([f(n)[l] for n in ("lam_q1", "lam_k1", "lam_q2", "lam_k2")], 1)
        cols[f"lam{l}"] = np.concatenate([lam, zero(64, 4)], 0)
        cols[f"sub{l}"] = f("sub_norm_g")[l][:, None]
        cols[f"mlp{l}"], cols[f"ple{l}"] = tall(f("norm_mlp_g")[l]), tall(f("norm_ple_g")[l])
    cols["n1"], cols["n2"] = tall(f("norm1_gain_2")[0]), tall(f("norm2_gain_2")[0])
    cols["ada_b"], cols["c"] = tall(f("ada_b_2")[0]), tall(f("c_2")[0])
    cols["q_a"], cols["kv_a"] = tall(f("mla_q_a_gain_2")[0]), tall(f("mla_kv_a_gain_2")[0])
    for name, key in (("mla_q", "mla_q_gain_2"), ("mla_k", "mla_k_gain_2")):
        g = f(key)[0]
        cols[name] = np.concatenate([g, swap(g[64:])])[:, None]
    for name in ("q", "kc", "ks", "kw"):
        cols["nsa_" + name] = twice(f(f"nsa_{name}_gain_2")[0])
    for name in ("k", "v"):
        t = f(f"cmp_pos_{name}_2")[0].T
        cols["pos_" + name] = np.concatenate([t, t], 0)
    table, width = vec_table()
    vecs = zero(P, width)
    for name, (at, n) in table.items():
        vecs[:, at:at + n] = cols[name]
    w2 = np.concatenate([f(n)[0].reshape(2, P, 64).transpose(1, 0, 2).reshape(P, P)
                         for n in ("cmp_w2_k_2", "cmp_w2_v_2")], 1)
    return dict(
        weights=weights, ada=ada, vecs=vecs, cmp_w2=w2,
        x_t=f("x")[0].T.reshape(KT, P, S).transpose(1, 0, 2),
        p_t=f("p")[:, 0].transpose(0, 2, 1).reshape(DEPTH, 2, P, S).transpose(0, 2, 1, 3),
        pool_w=f("pool_w").transpose(0, 2, 1, 3).reshape(DEPTH, P, 4 * P),
        positions=f("positions_2").astype(np.int32))


def constants():
    table, width = const_table()
    c = {name: np.zeros((P, n), np.float64) for name, (_, n) in table.items()}
    i, j = np.arange(P)[:, None], np.arange(P)[None]
    c["ident"] = i == j
    c["ones"][:] = 1
    c["blocks"] = i // 64 == j // 64
    c["row96"][:, 15] = 1
    c["row64"][:64, 47] = 1
    c["row64"][64:, 48] = 1
    c["causal"] = np.where(j > i, NEG, 0)
    c["far"] = np.where(j <= i, NEG, 0)
    for b in range(QB):
        n = np.arange(CMP_W)[None]
        ok = (16 * n + 31 <= b * P + i) & (n < CMP_N)
        c["cmp_mask"][:, b * CMP_W:(b + 1) * CMP_W] = np.where(ok, 0, NEG)
        c["cmp_valid"][:, b * CMP_W:(b + 1) * CMP_W] = ok
    c["inv_count"][:] = 1.0 / np.arange(1, 17)
    inv = lambda dim: 500000.0 ** (-np.arange(0, dim, 2) / dim)
    c["freq_mla"][64:, 0] = np.tile(inv(32), 4)
    for half in (0, 64):
        c["freq_nsa"][half:half + 16, 0] = np.tile(inv(16), 2)
        for d in range(8):
            c["rot"][half + d + 8, half + d] = -1
            c["rot"][half + d, half + d + 8] = 1
    c["phase_mla"][64:96, 0] = 0.25
    c["phase_mla"][96:112, 0] = 0.5
    c["eps"][:] = EPS
    out = np.zeros((P, width), np.float32)
    for name, (at, n) in table.items():
        out[:, at:at + n] = c[name]
    spread = np.zeros((40, 4, 2, 64), np.float32)
    for t in range(4):
        for k in range(2):
            spread[2 * t + k, t, k] = spread[32 + 2 * t + k, t, k] = 1
    return out, spread.reshape(40, S)


def kernel(**inputs):
    import concourse.bacc as bacc
    from concourse.bass_utils import run_bass_kernel_spmd

    arrays = lay_out(inputs)
    arrays["consts"], arrays["spread"] = constants()
    arrays = {k: np.ascontiguousarray(v) for k, v in arrays.items()}
    nc = bacc.Bacc("TRN2", target_bir_lowering=False, num_devices=1)
    d = {k: nc.dram_tensor(k, v.shape, mybir.dt.from_np(v.dtype), kind="ExternalInput").ap()
         for k, v in arrays.items()}
    out = nc.dram_tensor("out", (KT, P, S), mybir.dt.float32, kind="ExternalOutput").ap()
    program(nc, d["weights"], d["ada"], d["vecs"], d["consts"], d["spread"], d["x_t"], d["p_t"],
            d["pool_w"], d["cmp_w2"], d["positions"], out)
    r = run_bass_kernel_spmd(nc, [arrays], core_ids=[0])
    return np.ascontiguousarray(r.results[0]["out"].reshape(D, S).T)[None]
```
